# Optimizing a Trainium2 kernel written in Bass

```python
import math
import jax, jax.numpy as jnp
from jax import lax
import numpy as np

D_MODEL = 1024
BATCH = 1
SEQ = 1024
DEPTH = 1

CHUNK = 64
QBLOCK = 128
EPS = 1e-6

DN_HEADS = 4
DN_DK = 128
DN_DV = 128
CONV_K = 4
SA_HEADS = 4
SA_DQK = 128
SA_DV = 128
KV_RANK = 256
IDX_HEADS = 4
IDX_DIM = 64
IDX_TOPK_MAX = 256
SM_SCALE = SA_DQK ** -0.5
IDX_W_SCALE = (IDX_HEADS * IDX_DIM) ** -0.5
N_EXPERTS = 64
TOP_K = 8
N_GROUPS = 8
TOPK_GROUPS = 4
D_EXPERT = 256
D_SHARED = 256
ROUTED_SCALE = 2.5
MOE_BLOCK = 128

DN_QK = DN_HEADS * DN_DK
DN_V = DN_HEADS * DN_DV
CONV_DIM = 2 * DN_QK + DN_V
SA_Q = SA_HEADS * SA_DQK
IDX_Q = IDX_HEADS * IDX_DIM
IN_SIZES = (DN_QK, DN_QK, DN_V, DN_V, DN_HEADS, DN_HEADS, SA_Q, KV_RANK, IDX_Q, IDX_DIM, IDX_HEADS)
D_IN = 2 * DN_QK + 2 * DN_V + 2 * DN_HEADS + SA_Q + KV_RANK + IDX_Q + IDX_DIM + IDX_HEADS
MIX_WIDTH = DN_V + SA_HEADS * SA_DV

kernel_name = "hybrid_deltanet_dsa_moe_adaln_block"

def rms_norm(x, g):
    x32 = x.astype(jnp.float32)
    y = x32 * lax.rsqrt(jnp.mean(x32 * x32, axis=-1, keepdims=True) + EPS)
    return (y * g.astype(jnp.float32)).astype(x.dtype)

def layer_norm(x, g, b):
    x32 = x.astype(jnp.float32)
    mu = jnp.mean(x32, axis=-1, keepdims=True)
    xc = x32 - mu
    y = xc * lax.rsqrt(jnp.mean(xc * xc, axis=-1, keepdims=True) + EPS)
    return (y * g.astype(jnp.float32) + b.astype(jnp.float32)).astype(x.dtype)

def l2_normalize(x):
    x32 = x.astype(jnp.float32)
    return (x32 * lax.rsqrt(jnp.sum(x32 * x32, axis=-1, keepdims=True) + EPS)).astype(x.dtype)

def split_cols(a, sizes):
    offsets = []
    acc = 0
    for s in sizes[:-1]:
        acc += s
        offsets.append(acc)
    return jnp.split(a, offsets, axis=-1)

def causal_depthwise_conv(x, w):
    ch = x.shape[-1]
    return lax.conv_general_dilated(
        x, w[:, None, :].astype(x.dtype), window_strides=(1,),
        padding=[(w.shape[0] - 1, 0)], dimension_numbers=("NWC", "WIO", "NWC"),
        feature_group_count=ch)

def gated_delta_rule(q, k, v, g, beta):
    B, T, H, DK = q.shape
    DV = v.shape[-1]
    n = T // CHUNK
    f32 = jnp.float32

    def blk(a):
        a = a.astype(f32).reshape(B, n, CHUNK, H, *a.shape[3:])
        return jnp.swapaxes(a, 2, 3)

    q, k, v, g, beta = blk(q), blk(k), blk(v), blk(g), blk(beta)
    g = jnp.cumsum(g, axis=-1)
    pos = jnp.arange(CHUNK)
    causal = pos[:, None] >= pos[None, :]
    strict = pos[:, None] > pos[None, :]
    decay = jnp.exp(jnp.where(causal, g[..., :, None] - g[..., None, :], -jnp.inf))
    kb = k * beta[..., None]
    a_strict = jnp.where(strict, jnp.einsum("bnhid,bnhjd->bnhij", kb, k) * decay, 0.0)
    lhs = a_strict + jnp.eye(CHUNK, dtype=f32)
    rhs = jnp.concatenate([v * beta[..., None], kb * jnp.exp(g)[..., None]], axis=-1)
    sol = lax.linalg.triangular_solve(lhs, rhs, left_side=True, lower=True)
    u, w = sol[..., :DV], sol[..., DV:]
    qk = jnp.einsum("bnhid,bnhjd->bnhij", q, k) * decay
    q_dec = q * jnp.exp(g)[..., None]
    k_dec = k * jnp.exp(g[..., -1:] - g)[..., None]
    g_tot = jnp.exp(g[..., -1])

    def step(S, inp):
        q_c, qk_c, u_c, w_c, k_c, gt = inp
        v_new = u_c - jnp.einsum("bhcd,bhde->bhce", w_c, S)
        o = jnp.einsum("bhcd,bhde->bhce", q_c, S) + jnp.einsum("bhij,bhje->bhie", qk_c, v_new)
        S = S * gt[..., None, None] + jnp.einsum("bhcd,bhce->bhde", k_c, v_new)
        return S, o

    S0 = jnp.zeros((B, H, DK, DV), f32)
    xs = tuple(jnp.moveaxis(a, 1, 0) for a in (q_dec, qk, u, w, k_dec, g_tot))
    _, o = lax.scan(step, S0, xs)
    return jnp.swapaxes(jnp.moveaxis(o, 0, 1), 2, 3).reshape(B, T, H, DV)

def sparse_attention(q_lat, ckv, q_ix, k_ix, w_ix, topk):
    B, T, H, R = q_lat.shape
    nb = T // QBLOCK
    key_pos = jnp.arange(T)

    def to_blocks(a):
        return jnp.moveaxis(a.reshape(B, nb, QBLOCK, *a.shape[2:]), 1, 0)

    def attend_block(args):
        ql, qi, wi, start = args
        t = start + jnp.arange(QBLOCK)
        limit = (t // CHUNK + 1) * CHUNK
        admissible = key_pos[None, :] < limit[:, None]
        rel = jax.nn.relu(jnp.einsum("bqhd,bsd->bqhs", qi, k_ix))
        score = jnp.einsum("bqh,bqhs->bqs", wi, rel).astype(jnp.float32)
        score = jnp.where(admissible[None], score, -jnp.inf)
        _, idx = lax.top_k(score, topk)
        valid = idx < limit[None, :, None]
        kv = jax.vmap(lambda a, i: a[i])(ckv, idx)
        logits = jnp.einsum("bqhr,bqkr->bqhk", ql, kv).astype(jnp.float32) * SM_SCALE
        logits = jnp.where(valid[:, :, None, :], logits, -jnp.inf)
        p = jax.nn.softmax(logits, axis=-1).astype(kv.dtype)
        return jnp.einsum("bqhk,bqkr->bqhr", p, kv)

    starts = jnp.arange(nb) * QBLOCK
    out = lax.map(attend_block, (to_blocks(q_lat), to_blocks(q_ix), to_blocks(w_ix), starts))
    return jnp.moveaxis(out, 0, 1).reshape(B, T, H, R)

def token_mixers(h, w_in, conv_w, a_log, dt_bias, dn_norm_g, kv_norm_g, w_uk, w_uv,
                 idx_k_ln_g, idx_k_ln_b, topk):
    B, T, _ = h.shape
    proj = h @ w_in
    (q_dn, k_dn, v_dn, z_dn, b_dn, a_dn, q_sa, ckv, q_ix, k_ix, w_ix) = split_cols(proj, IN_SIZES)

    qkv = jax.nn.silu(causal_depthwise_conv(jnp.concatenate([q_dn, k_dn, v_dn], axis=-1), conv_w))
    q_dn, k_dn, v_dn = jnp.split(qkv, [DN_QK, 2 * DN_QK], axis=-1)
    q_dn = l2_normalize(q_dn.reshape(B, T, DN_HEADS, DN_DK)) * (DN_DK ** -0.5)
    k_dn = l2_normalize(k_dn.reshape(B, T, DN_HEADS, DN_DK))
    v_dn = v_dn.reshape(B, T, DN_HEADS, DN_DV)
    beta = jax.nn.sigmoid(b_dn.astype(jnp.float32))
    g = -jnp.exp(a_log.astype(jnp.float32)) * jax.nn.softplus(
        a_dn.astype(jnp.float32) + dt_bias.astype(jnp.float32))
    o_dn = gated_delta_rule(q_dn, k_dn, v_dn, g, beta).astype(h.dtype)
    o_dn = rms_norm(o_dn, dn_norm_g) * jax.nn.silu(z_dn.reshape(B, T, DN_HEADS, DN_DV))

    q_sa = q_sa.reshape(B, T, SA_HEADS, SA_DQK)
    ckv = rms_norm(ckv, kv_norm_g)
    q_lat = jnp.einsum("bthd,hrd->bthr", q_sa, w_uk)
    q_ix = q_ix.reshape(B, T, IDX_HEADS, IDX_DIM)
    k_ix = layer_norm(k_ix, idx_k_ln_g, idx_k_ln_b)
    w_ix = w_ix * IDX_W_SCALE
    o_lat = sparse_attention(q_lat, ckv, q_ix, k_ix, w_ix, topk)
    o_sa = jnp.einsum("bthr,hrd->bthd", o_lat, w_uv)

    return jnp.concatenate([o_dn.reshape(B, T, DN_V), o_sa.reshape(B, T, SA_HEADS * SA_DV)], axis=-1)

def moe_ffn(h, router_w, router_b, w_gate, w_up, w_down, s_gate, s_up, s_down):
    B, T, D = h.shape
    xt = h.reshape(-1, D)
    n_tok = xt.shape[0]
    scores = jax.nn.sigmoid((xt @ router_w).astype(jnp.float32))
    choice = scores + router_b.astype(jnp.float32)
    grouped = choice.reshape(n_tok, N_GROUPS, N_EXPERTS // N_GROUPS)
    group_score = jnp.sum(lax.top_k(grouped, 2)[0], axis=-1)
    _, top_groups = lax.top_k(group_score, TOPK_GROUPS)
    group_mask = jnp.any(top_groups[..., None] == jnp.arange(N_GROUPS), axis=1)
    expert_mask = jnp.repeat(group_mask, N_EXPERTS // N_GROUPS, axis=1)
    _, top_e = lax.top_k(jnp.where(expert_mask, choice, -jnp.inf), TOP_K)
    gate = jnp.take_along_axis(scores, top_e, axis=1)
    gate = gate / jnp.sum(gate, axis=-1, keepdims=True) * ROUTED_SCALE

    n_assign = n_tok * TOP_K
    flat_e = top_e.reshape(-1)
    order = jnp.argsort(flat_e)
    sorted_e = flat_e[order]
    sorted_tok = (order // TOP_K).astype(jnp.int32)
    sorted_gate = gate.reshape(-1)[order]
    counts = jnp.bincount(flat_e, length=N_EXPERTS)
    padded = (counts + MOE_BLOCK - 1) // MOE_BLOCK * MOE_BLOCK
    starts = jnp.cumsum(counts) - counts
    pad_ends = jnp.cumsum(padded)
    pad_starts = pad_ends - padded
    dest = pad_starts[sorted_e] + jnp.arange(n_assign) - starts[sorted_e]
    cap = n_assign + N_EXPERTS * MOE_BLOCK
    n_blocks = cap // MOE_BLOCK
    buf_tok = jnp.full((cap,), n_tok, jnp.int32).at[dest].set(sorted_tok)
    buf_gate = jnp.zeros((cap,), jnp.float32).at[dest].set(sorted_gate)
    blk_e = jnp.minimum(jnp.searchsorted(pad_ends, jnp.arange(n_blocks) * MOE_BLOCK, side="right"),
                        N_EXPERTS - 1)

    def expert_block(args):
        tok, gt, e = args
        xb = jnp.take(xt, tok, axis=0, mode="fill", fill_value=0)
        hb = jax.nn.silu(xb @ w_gate[e]) * (xb @ w_up[e])
        return (hb @ w_down[e]) * gt[:, None].astype(xb.dtype)

    y = lax.map(expert_block, (buf_tok.reshape(n_blocks, MOE_BLOCK),
                               buf_gate.reshape(n_blocks, MOE_BLOCK), blk_e))
    routed = jax.ops.segment_sum(y.reshape(cap, D), buf_tok, num_segments=n_tok)
    shared = (jax.nn.silu(xt @ s_gate) * (xt @ s_up)) @ s_down
    return (routed + shared).reshape(B, T, D)

def setup_inputs(seed: int = 0) -> dict:
    key = jax.random.key(seed)
    ks = jax.random.split(key, 32)
    f32 = jnp.float32
    L = DEPTH

    def nrm(k, shape, fan_in):
        return jax.random.normal(k, shape, f32) * (fan_in ** -0.5)

    def gain(k, shape):
        return 1.0 + 0.02 * jax.random.normal(k, shape, f32)

    x = jax.random.normal(ks[0], (BATCH, SEQ, D_MODEL), f32)
    c = jax.random.normal(ks[1], (BATCH, D_MODEL), f32)
    ada_w = 0.02 * jax.random.normal(ks[2], (L, D_MODEL, 6 * D_MODEL), f32)
    ada_b = 0.02 * jax.random.normal(ks[3], (L, 6 * D_MODEL), f32)
    norm1_g = gain(ks[4], (L, D_MODEL))
    w_in = nrm(ks[5], (L, D_MODEL, D_IN), D_MODEL)
    conv_w = nrm(ks[6], (L, CONV_K, CONV_DIM), CONV_K)
    a_log = jnp.log(jax.random.uniform(ks[7], (L, DN_HEADS), f32, 1.0, 16.0))
    dt = jnp.exp(jax.random.uniform(ks[8], (L, DN_HEADS), f32, math.log(1e-3), math.log(1e-1)))
    dt_bias = dt + jnp.log(-jnp.expm1(-dt))
    dn_norm_g = gain(ks[9], (L, DN_DV))
    kv_norm_g = gain(ks[10], (L, KV_RANK))
    w_uk = nrm(ks[11], (L, SA_HEADS, KV_RANK, SA_DQK), KV_RANK)
    w_uv = nrm(ks[12], (L, SA_HEADS, KV_RANK, SA_DV), KV_RANK)
    idx_k_ln_g = gain(ks[13], (L, IDX_DIM))
    idx_k_ln_b = 0.02 * jax.random.normal(ks[14], (L, IDX_DIM), f32)
    w_out = nrm(ks[15], (L, MIX_WIDTH, D_MODEL), MIX_WIDTH)
    norm2_g = gain(ks[16], (L, D_MODEL))
    router_w = nrm(ks[17], (L, D_MODEL, N_EXPERTS), D_MODEL)
    router_b = 0.01 * jax.random.normal(ks[18], (L, N_EXPERTS), f32)
    exp_w_gate = nrm(ks[19], (L, N_EXPERTS, D_MODEL, D_EXPERT), D_MODEL)
    exp_w_up = nrm(ks[20], (L, N_EXPERTS, D_MODEL, D_EXPERT), D_MODEL)
    exp_w_down = nrm(ks[21], (L, N_EXPERTS, D_EXPERT, D_MODEL), D_EXPERT)
    sh_w_gate = nrm(ks[22], (L, D_MODEL, D_SHARED), D_MODEL)
    sh_w_up = nrm(ks[23], (L, D_MODEL, D_SHARED), D_MODEL)
    sh_w_down = nrm(ks[24], (L, D_SHARED, D_MODEL), D_SHARED)
    final_g = gain(ks[25], (D_MODEL,))
    return {"x": x, "c": c, "ada_w": ada_w, "ada_b": ada_b, "norm1_g": norm1_g, "w_in": w_in,
            "conv_w": conv_w, "a_log": a_log, "dt_bias": dt_bias, "dn_norm_g": dn_norm_g,
            "kv_norm_g": kv_norm_g, "w_uk": w_uk, "w_uv": w_uv, "idx_k_ln_g": idx_k_ln_g,
            "idx_k_ln_b": idx_k_ln_b, "w_out": w_out, "norm2_g": norm2_g, "router_w": router_w,
            "router_b": router_b, "exp_w_gate": exp_w_gate, "exp_w_up": exp_w_up,
            "exp_w_down": exp_w_down, "sh_w_gate": sh_w_gate, "sh_w_up": sh_w_up,
            "sh_w_down": sh_w_down, "final_g": final_g}

def reference(x, c, ada_w, ada_b, norm1_g, w_in, conv_w, a_log, dt_bias, dn_norm_g, kv_norm_g,
              w_uk, w_uv, idx_k_ln_g, idx_k_ln_b, w_out, norm2_g, router_w, router_b,
              exp_w_gate, exp_w_up, exp_w_down, sh_w_gate, sh_w_up, sh_w_down, final_g):
    T = x.shape[1]
    topk = min(IDX_TOPK_MAX, T // 4)
    cond = jax.nn.silu(c)
    for l in range(DEPTH):
        mod = (cond @ ada_w[l] + ada_b[l])[:, None, :]
        sh1, sc1, gt1, sh2, sc2, gt2 = jnp.split(mod, 6, axis=-1)
        h = rms_norm(x, norm1_g[l]) * (1 + sc1) + sh1
        mix = token_mixers(h, w_in[l], conv_w[l], a_log[l], dt_bias[l], dn_norm_g[l], kv_norm_g[l],
                           w_uk[l], w_uv[l], idx_k_ln_g[l], idx_k_ln_b[l], topk)
        x = x + gt1 * (mix @ w_out[l])
        h = rms_norm(x, norm2_g[l]) * (1 + sc2) + sh2
        x = x + gt2 * moe_ffn(h, router_w[l], router_b[l], exp_w_gate[l], exp_w_up[l], exp_w_down[l],
                              sh_w_gate[l], sh_w_up[l], sh_w_down[l])
    return rms_norm(x, final_g)


_drawn_inputs = setup_inputs


def setup_inputs(seed=0):
    import zlib

    import numpy as np

    out = dict(_drawn_inputs(seed))
    spreads = {}
    factors = {'dn_norm_g': 2.858,
     'kv_norm_g': 4.052,
     'idx_k_ln_g': 4.206,
     'idx_k_ln_b': 5.072,
     'final_g': 2.802}
    for name, (base, spread) in spreads.items():
        noise = np.random.default_rng([zlib.crc32(name.encode()), seed]).standard_normal(out[name].shape)
        drawn = base * np.exp(spread * noise) if base else spread * noise
        out[name] = __import__('jax').numpy.asarray(drawn.astype(out[name].dtype))
    for name, factor in factors.items():
        out[name] = (out[name] * factor).astype(out[name].dtype)
    return out
```

```python
from contextlib import ExitStack

import concourse.bass as bass
import numpy as np
from concourse import mybir

F32, I32, U32 = mybir.dt.float32, mybir.dt.int32, mybir.dt.uint32
ALU, ACT = mybir.AluOpType, mybir.ActivationFunctionType
AX = mybir.AxisListType

P = 128
D, T = 1024, 1024
NT, NK = T // P, D // P
HALF = 512
EPS = 1e-6
H, DH = 4, 128
CONV_K, CHUNK = 4, 64
KV_R, IX_H, IX_D, TOPK = 256, 4, 64, 256
SM_SCALE, IX_SCALE = DH ** -0.5, (IX_H * IX_D) ** -0.5
NE, NG, TOP_G, TOP_E, FE = 64, 8, 4, 8, 256
ROUTED = 2.5
CAP = T // P
NEG, TAKEN, TAKEN_CUT = -1e30, -3e38, -2e38
C_Q, C_K, C_V, C_Z, C_BA, C_QSA, C_CKV, C_QIX, C_KIX = 0, 512, 1024, 1536, 2048, 2056, 2568, 2824, 3080
AUX = KV_R + IX_D + IX_H + 2 * H
V_ADAB, V_N1, V_N2, V_C, V_KVG, V_KG, V_KB, V_DG, V_ROWS = 0, 48, 56, 64, 72, 74, 75, 76, 77
SEL_TILES = range(TOPK // P, NT)
ROUNDS = TOPK // 8


def conv_slots():
    at = {}
    ct = 0
    for t in SEL_TILES:
        for part in range(2):
            n = 2 if len(at) < 4 else 1
            at[(t, part)] = list(range(ct, min(ct + n, 12)))
            ct = min(ct + n, 12)
    last = (SEL_TILES[-1], 1)
    at[last] = at[last] + list(range(ct, 12))
    return at


def build(nc, x, c, ada_w, ada_b, norm1_g, w_in, conv_w, a_log, dt_bias, dn_norm_g, kv_norm_g, w_uk, w_uv,
          idx_k_ln_g, idx_k_ln_b, w_out, norm2_g, router_w, router_b, exp_w_gate, exp_w_up, exp_w_down,
          sh_w_gate, sh_w_up, sh_w_down, final_g, out):
    ctx = ExitStack()
    with ctx:
        def sb(name, shape, dt=F32):
            return ctx.enter_context(nc.sbuf_tensor(name, shape, dt))

        def sem(name):
            return ctx.enter_context(nc.semaphore(name))

        xn_dram = nc.dram_tensor("xn_tokens", (T + P, D), F32).ap()
        acc_dram = nc.dram_tensor("moe_sum", (T + P, D), F32).ap()
        table_dram = nc.dram_tensor("dispatch", (P * NE * CAP, 2), I32).ap()

        arena = sb("arena", [P, 193 * 256])
        KB = 256

        def at(kb, words):
            return arena[:, int(kb * KB):int(kb * KB) + words]

        hT = at(0, NK * T).rearrange("p (k t) -> p k t", k=NK)
        R_QKV, R_QSA, R_KV, R_Z, R_SC, R_PAN = 32, 80, 96, 128, 144, 161
        qkvT = at(R_QKV, 12 * T).rearrange("p (c t) -> p c t", c=12)
        qsaT = at(R_QSA, H * T).rearrange("p (h t) -> p h t", h=H)
        xt_in = at(R_KV, NT * D).rearrange("p (t d) -> p t d", t=NT)
        khT = at(R_KV, H * T).rearrange("p (h t) -> p h t", h=H)
        vh = at(R_KV + 16, NT * H * DH).rearrange("p (t n) -> p t n", t=NT)
        zg = at(R_Z, NT * H * DH).rearrange("p (t n) -> p t n", t=NT)
        score = {}
        off = R_SC
        for t in SEL_TILES:
            score[t] = at(off, (t + 1) * P)
            off += (t + 1) / 2
        assert off <= R_PAN
        panel = [at(R_PAN + 16 * i, NK * HALF) for i in range(2)]
        qixT = at(R_QKV, 2 * T).rearrange("p (c t) -> p c t", c=2)
        kixT = at(R_QKV + 8, T)
        rel = [at(R_QKV + 12 + 4 * i, T) for i in range(2)]
        ckvT = at(R_QKV + 20, 2 * T).rearrange("p (k t) -> p k t", k=2)
        kx2 = at(R_QKV + 28, NT * 2 * IX_D).rearrange("p (t n) -> p t n", t=NT)
        aux = at(R_QKV + 32, NT * AUX).rearrange("p (t n) -> p t n", t=NT)
        wuk = at(R_QSA, H * 2 * DH).rearrange("p (h k n) -> p h k n", h=H, k=2)
        wuv = at(R_QSA + 4, 2 * H * DH).rearrange("p (k h n) -> p k h n", h=H, k=2)
        sqx = at(R_QSA + 8, D)
        lg = [at(4 * i, T) for i in range(2)]
        prT = [at(8 + 4 * i, T) for i in range(2)]
        osa = at(16, H * DH)

        def dn(i):
            return at(2 * i, HALF)
        (kn, qn, bv, kb, kbe, kd, qd, knT, kbT, qnT, qdT, gbt, ET, AT, QKT) = [dn(i) for i in range(15)]
        CT = at(R_SC, 5 * HALF).rearrange("p (l n) -> p l n", l=5)
        X, XT, P1 = at(R_SC + 10, HALF), at(R_SC + 12, HALF), at(R_SC + 14, HALF)
        wT = at(30, HALF)
        R_DM = R_KV
        S_st = at(R_DM, HALF)
        vn = at(R_DM + 2, HALF)
        osq = at(R_DM + 4, HALF)
        xi = at(R_DM + 6, P).bitcast(I32)
        ji = at(R_DM + 6.5, P).bitcast(I32)
        xor = at(R_DM + 7, P).bitcast(I32)
        gtm = at(R_DM + 7.5, P)
        lvl = [at(R_DM + 8 + 0.5 * i, P) for i in range(6)]
        tmp_m = at(R_DM + 11, P)
        x2 = at(R_KV, NT * D).rearrange("p (t d) -> p t d", t=NT)
        h2T = hT
        xh2 = at(48, NT * D).rearrange("p (t d) -> p t d", t=NT)
        wslot = [at(32 + 24 * i, 6144) for i in range(2)]
        xg, xTm, ysb = at(80, D), at(84, D), at(88, D)
        sg, hm, hmT, upb = (at(92 + i, FE) for i in range(4))
        tbl = at(128, NE * CAP * 2).bitcast(I32)
        condrep = at(132, NK * P).rearrange("p (k n) -> p k n", k=NK)
        ytmp = [at(136 + 2 * i, HALF) for i in range(2)]
        junk = at(140, D)
        r_sc, r_ch, r_mk, r_gt, r_v, r_eq = (at(132 + 2 * i, NT * NE) for i in range(6))
        gt1, gt2, fg, ysh0 = (at(144 + 4 * i, D) for i in range(4))
        ysh = [ysh0, xTm]
        x3 = at(0, NT * D).rearrange("p (t d) -> p t d", t=NT)

        ident = sb("ident", [P, P])
        ones = sb("ones", [P, P])
        tri = sb("tri", [P, P])
        after = sb("after", [P, P])
        before = sb("before", [P, P])
        half = sb("half", [P, 2, P])
        vecs = sb("vecs", [V_ROWS, P])
        cwr = sb("cwr", [48, P])
        vT = sb("vT", [P, V_ROWS + 48])
        cond = sb("cond", [P, NK])
        A1, B1, A2, B2 = (sb(n, [P, NK]) for n in ("A1", "B1", "A2", "B2"))
        epsc = sb("epsc", [P, 4])
        st = sb("st", [P, 4, NT * H * 2])
        gates = sb("gates", [P, 10, NT * H])
        rowc = sb("rowc", [P, 2 * H])
        pre = [sb(f"pre{i}", [P, HALF + 3]) for i in range(2)]
        ints = sb("ints", [1, 2 * NE + 1], I32)
        m8 = sb("m8", [P, 8])
        lowm = sb("lowm", [P, NG, NG])
        rb = sb("rb", [P, NE])
        erow = sb("erow", [P, NE])
        pay = pre[0][:, 0:128].bitcast(I32)
        d8 = pre[0][:, 128:192]
        di = [pre[0][:, 192 + 64 * i:256 + 64 * i].bitcast(I32) for i in range(2)]
        dest_i = pre[0][:, 320:384].bitcast(I32)
        gsm = pre[1][:, 0:128].rearrange("p (a n) -> p a n", a=2)
        cni = pre[1][:, 128:192].bitcast(I32)
        nbf = pre[1][:, 192:256]
        nbc = pre[1][0:NE, 256:384]
        idx_now, idx_last, idx_hold, idx_out, idx_zero = (sb(n, [P, 1], I32) for n in (
            "idx_now", "idx_last", "idx_hold", "idx_out", "idx_zero"))

        psum = ctx.enter_context(nc.psum_tensor("psum", [P, 8 * HALF], F32))

        def bank(b, n=1):
            return psum[:, b * HALF:(b + n) * HALF]

        def heads(ap):
            return ap.rearrange("p (h n) -> p h n", h=H)

        def per_head(col):
            return col.unsqueeze(2).to_broadcast([P, H, DH])

        def each_head(mask):
            return mask.unsqueeze(1).to_broadcast([P, H, P])

        w_in_k = w_in.rearrange("o (k p) n -> p (o k) n", p=P)
        ada_k = ada_w.rearrange("o (k p) n -> p (o k) n", p=P)
        w_out_k = w_out.rearrange("o (k p) n -> p (o k) n", p=P)
        rw_k = router_w.rearrange("o (k p) n -> p (o k) n", p=P)
        sg_k = sh_w_gate.rearrange("o (k p) n -> p (o k) n", p=P)
        su_k = sh_w_up.rearrange("o (k p) n -> p (o k) n", p=P)
        sd_k = sh_w_down.rearrange("o (k p) n -> p (o k) n", p=P)
        PANELS = [(f"ada{i}", HALF, [(ada_k, i * HALF, HALF, 0)]) for i in (0, 1, 2, 3)]
        PANELS += [("aux", AUX, [(w_in_k, C_CKV, KV_R, 0), (w_in_k, C_KIX, IX_D + IX_H, KV_R),
                                 (w_in_k, C_BA, 2 * H, KV_R + IX_D + IX_H)]),
                   ("qix", KV_R, [(w_in_k, C_QIX, IX_H * IX_D, 0)]),
                   ("qsa", HALF, [(w_in_k, C_QSA, HALF, 0)]),
                   ("z", HALF, [(w_in_k, C_Z, HALF, 0)])]
        PANELS += [(n, HALF, [(w_in_k, o, HALF, 0)]) for n, o in (("q", C_Q), ("k", C_K), ("v", C_V))]
        PANELS += [(f"ada{i}", HALF, [(ada_k, i * HALF, HALF, 0)]) for i in (4, 5, 6, 7, 8, 9, 10, 11)]
        PANELS += [(f"wo{i}", HALF, [(w_out_k, i * HALF, HALF, 0)]) for i in range(2)]
        PANELS += [("router", NE, [(rw_k, 0, NE, 0)]),
                   ("sgu", HALF, [(sg_k, 0, FE, 0), (su_k, 0, FE, FE)]), ("sd", D, [(sd_k, 0, D, 0)])]
        NBUF = len(panel)
        PAN = {n: i for i, (n, _, _) in enumerate(PANELS)}
        landed, count = [], [0] * NBUF
        for i, (_, _, parts) in enumerate(PANELS):
            count[i % NBUF] += 16 * len(parts)
            landed.append(count[i % NBUF])

        def pan(name):
            i = PAN[name]
            cols = PANELS[i][1]
            k = 2 if name == "sd" else NK
            return panel[i % NBUF][:, 0:k * cols].rearrange("p (k n) -> p k n", k=k)

        GROUPS = [("hT", k, hf, "act" if k % 2 else "dve") for hf in range(2) for k in range(NK)]
        GROUPS += [("aux", t, 0, "act") for t in range(NT)]
        GROUPS += [("qix", ct, hf, "act") for ct in range(2) for hf in range(2)]
        GROUPS += [("ckvT", k, hf, "dve") for k in range(2) for hf in range(2)]
        GROUPS += [("kixT", 0, hf, "dve") for hf in range(2)]
        GROUPS += [("kh", h, hf, "act") for h in range(H) for hf in range(2)]
        GROUPS += [("vh", t, 0, "act") for t in range(NT)]
        GROUPS += [("qsa", h, hf, "act") for h in range(H) for hf in range(2)]
        GROUPS += [("z", t, 0, "act") for t in range(NT)]
        GROUPS += [("conv", ct, hf, "act") for ct in range(12) for hf in range(2)]
        GIDX = {g[:3]: i for i, g in enumerate(GROUPS)}
        nth, n_of = [], {"act": 0, "dve": 0}
        for g in GROUPS:
            n_of[g[3]] += 1
            nth.append(n_of[g[3]])
        RING = 4

        consts_ready = sem("consts_ready")
        vecs_in, rows_in, x_in, w_small = sem("vecs_in"), sem("rows_in"), sem("x_in"), sem("w_small")
        pan_in = [sem(f"pan_in{i}") for i in range(NBUF)]
        pan_used = sem("pan_used")
        vecs_turned, vT_ready, cond_ready = sem("vecs_turned"), sem("vT_ready"), sem("cond_ready")
        mod1_ready, ab1_ready = sem("mod1_ready"), sem("ab1_ready")
        ssq_ready, rms_ready, rstd_ready, xhat_ready = sem("ssq_ready"), sem("rms_ready"), sem("rstd_ready"), sem("xhat_ready")
        ring_full = sem("ring_full")
        ring_free = {"act": sem("ring_free_act"), "dve": sem("ring_free_dve")}
        dv, av = sem("dv"), sem("av")
        stats_asked, stats_rooted, kv_ready = sem("stats_asked"), sem("stats_rooted"), sem("kv_ready")
        ixs_full, rel_ready, rel_used = sem("ixs_full"), sem("rel_ready"), sem("rel_used")
        gate_in, gate_act, g_ready, gc_full, gc_ready = sem("gate_in"), sem("gate_act"), sem("g_ready"), sem("gc_full"), sem("gc_ready")
        pre_ready, conv_ready, conv_act, sq_ready, nrm_full = sem("pre_ready"), sem("conv_ready"), sem("conv_act"), sem("sq_ready"), sem("nrm_full")
        bias_ready = sem("bias_ready")

        def ring_wait(pe, g):
            if g >= RING:
                pe.wait_ge(ring_free[GROUPS[g - RING][3]], nth[g - RING])

        def ring_bank(g):
            return bank(g % RING)

        s_lg_full, s_lg_ready, s_mx_ready, s_pr_ready, s_pt_full = (sem(n) for n in ("lg_full", "lg_ready", "mx_ready", "pr_ready", "pt_full"))
        s_pt_act, s_pt_dve, s_o_full, s_osa_ready, s_oT_full = (sem(n) for n in ("pt_act", "pt_dve", "o_full", "osa_ready", "oT_full"))
        s_sa_ready, s_dn_consts, s_qkv_full, s_nrm_ready, s_knqn_ready = (sem(n) for n in ("sa_ready", "dn_consts", "qkv_full", "nrm_ready", "knqn_ready"))
        s_pool_k, s_t_full, s_t_act, s_gb_ready, s_gb_full = (sem(n) for n in ("pool_k", "t_full", "t_act", "gb_ready", "gb_full"))
        s_dd_ready, s_dd_exp, s_kk_full, s_at_ready, s_ct_ready = (sem(n) for n in ("dd_ready", "dd_exp", "kk_full", "at_ready", "ct_ready"))
        s_xt1_ready, s_x1_full, s_x1_ready, s_p1_full, s_p1_ready = (sem(n) for n in ("xt1_ready", "x1_full", "x1_ready", "p1_full", "p1_ready"))
        s_dx_full, s_dx_ready, s_w_full, s_w_ready, s_vn_full = (sem(n) for n in ("dx_full", "dx_ready", "w_full", "w_ready", "vn_full"))
        s_vn_ready, s_ods_full, s_s_ready, s_o_sq, s_oz_ready = (sem(n) for n in ("vn_ready", "ods_full", "s_ready", "o_sq", "oz_ready"))
        s_orms_ready, s_on_ready, s_ont_full, s_dnT_ready, s_x_load = (sem(n) for n in ("orms_ready", "on_ready", "ont_full", "dnT_ready", "x_load"))
        s_gt1_full, s_gt1_ready, s_gt2_ready, s_ab2_ready, s_y1_full = (sem(n) for n in ("gt1_full", "gt1_ready", "gt2_ready", "ab2_ready", "y1_full"))
        s_y1_read, s_ssq2_ready, s_rms2_ready, s_xh2_ready, s_xn_out = (sem(n) for n in ("y1_read", "ssq2_ready", "rms2_ready", "xh2_ready", "xn_out"))
        s_h2_full, s_h2_act, s_h2_dve, s_rl_full, s_rsc_ready = (sem(n) for n in ("h2_full", "h2_act", "h2_dve", "rl_full", "rsc_ready"))
        s_mask_ready, s_pos_full, s_nbr_ready, s_nbt_full, s_nbt_ready = (sem(n) for n in ("mask_ready", "pos_full", "nbr_ready", "nbt_full", "nbt_ready"))
        s_bs_full, s_lists_ready, s_tbl_init, s_tbl_out, s_tbl_in = (sem(n) for n in ("bs_full", "lists_ready", "tbl_init", "tbl_out", "tbl_in"))
        s_slots_out, s_sgu_full, s_ssg_ready, s_shm_ready, s_shT_full = (sem(n) for n in ("slots_out", "sgu_full", "ssg_ready", "shm_ready", "shT_full"))
        s_shT_ready, s_sy_full, s_sy_act, s_acc_out0, s_acc_out1 = (sem(n) for n in ("shT_ready", "sy_full", "sy_act", "acc_out0", "acc_out1"))
        s_w_in0, s_w_in1, s_w_used, s_idx_g, s_idx_s = (sem(n) for n in ("w_in0", "w_in1", "w_used", "idx_g", "idx_s"))
        s_paced, s_gathered, s_xg_read, s_xT_act, s_xT_dve = (sem(n) for n in ("paced", "gathered", "xg_read", "xT_act", "xT_dve"))
        s_gu_full, s_silu_done, s_hm_ready, s_hT_full, s_hT_ready = (sem(n) for n in ("gu_full", "silu_done", "hm_ready", "hT_full", "hT_ready"))
        s_y_full, s_y_act, s_y_dve, s_scattered, s_acc_in = (sem(n) for n in ("y_full", "y_act", "y_dve", "scattered", "acc_in"))
        s_x3_ready, s_ssq3_ready, s_rms3_ready, s_o_ready, s_out_done0 = (sem(n) for n in ("x3_ready", "ssq3_ready", "rms3_ready", "o_ready", "out_done0"))
        s_out_done1, s_small_done, s_cnt_ready, s_moe_zero, s_pads_out = (sem(n) for n in ("out_done1", "small_done", "cnt_ready", "moe_zero", "pads_out"))
        s_p_kk,  = (sem(n) for n in ("p_kk",))
        acc_out, out_done = (s_acc_out0, s_acc_out1), (s_out_done0, s_out_done1)

        block = ctx.enter_context(nc.Block())
        TILE = lambda t: slice(t * P, (t + 1) * P)
        HSL = lambda h: slice(h * DH, (h + 1) * DH)

        def pt_groups(u):
            before_ = sum((v // H + 4) // 4 for v in range(u))
            return list(range(before_, before_ + (u // H + 4) // 4))

        def pt_cols(u, gi):
            c0 = (gi - pt_groups(u)[0]) * HALF
            return slice(c0, min(c0 + HALF, (u // H + 1) * P))

        bias01 = [at(18, P), at(18.5, 2 * P)]

        def sa_evac(act, t):
            act.wait_ge(s_oT_full, t + 1)
            act.activation(qsaT[:, :, TILE(t)], heads(bank(3)), ACT.Copy).then_inc(s_sa_ready, 1)

        @block.sync
        def _(sp):
            sp.dma_start(vecs[V_C:V_C + 8, :], c.rearrange("o (k p) -> (o k) p", p=P)).then_inc(vecs_in, 16)
            sp.dma_start(vecs[V_ADAB:48, :], ada_b.rearrange("o (k p) -> (o k) p", p=P)).then_inc(vecs_in, 16)
            sp.dma_start(vecs[V_N1:V_N1 + 8, :], norm1_g.rearrange("o (k p) -> (o k) p", p=P)).then_inc(vecs_in, 16)
            sp.dma_start(vecs[V_N2:V_N2 + 8, :], norm2_g.rearrange("o (k p) -> (o k) p", p=P)).then_inc(vecs_in, 16)
            sp.dma_start(vecs[V_KVG:V_KVG + 2, :], kv_norm_g.rearrange("o (k p) -> (o k) p", p=P)).then_inc(vecs_in, 16)
            for i in range(2):
                sp.dma_start(vecs[V_KG:V_KG + 1, i * IX_D:(i + 1) * IX_D], idx_k_ln_g).then_inc(vecs_in, 16)
                sp.dma_start(vecs[V_KB:V_KB + 1, i * IX_D:(i + 1) * IX_D], idx_k_ln_b).then_inc(vecs_in, 16)
            sp.dma_start(vecs[V_DG:V_DG + 1, :], dn_norm_g).then_inc(vecs_in, 16)
            sp.dma_start(cwr[:, :], conv_w.rearrange("o j (c p) -> (o j c) p", p=P)).then_inc(vecs_in, 16)
            for i, (name, cols, parts) in enumerate(PANELS):
                if name == "ada2":
                    for t in range(NT):
                        sp.dma_start(xt_in[:, t, :], x[0, TILE(t), :]).then_inc(x_in, 16)
                if name == "qix":
                    sp.dma_start(wuk, w_uk.rearrange("o h (k p) n -> p (o h) k n", p=P)).then_inc(w_small, 16)
                    for k in range(2):
                        sp.dma_start(wuv[:, k], w_uv[0, :, k * P:(k + 1) * P, :].rearrange("h p n -> p h n")).then_inc(w_small, 16)
                if name == "ada6":
                    sp.wait_ge(s_oz_ready, NT)
                    sp.wait_ge(s_s_ready, 2 * NT)
                    for t in range(NT):
                        sp.dma_start(x2[:, t, :], x[0, TILE(t), :]).then_inc(s_x_load, 16)
                    sp.dma_start(gt1, ada_b[:, 2 * D:3 * D].partition_broadcast(P)).then_inc(s_x_load, 16)
                    sp.dma_start(gt2, ada_b[:, 5 * D:6 * D].partition_broadcast(P)).then_inc(s_x_load, 16)
                    sp.dma_start(fg, final_g.rearrange("(o n) -> o n", o=1).partition_broadcast(P)).then_inc(s_x_load, 16)
                    sp.dma_start(rb[:, :], router_b.partition_broadcast(P)).then_inc(s_x_load, 16)
                if i >= NBUF:
                    sp.wait_ge(pan_used, i - NBUF + 1)
                for src, c0, n, o in parts:
                    sp.dma_start(pan(name)[:, :, o:o + n], src[:, :, c0:c0 + n]).then_inc(pan_in[i % NBUF], 16)
            for t in range(NT):
                sp.wait_ge(s_xh2_ready, t + 1)
                sp.dma_start(xn_dram[TILE(t), :], xh2[:, t, :]).then_inc(s_xn_out, 16)
            sp.wait_ge(s_xn_out, 16 * NT)
            sp.wait_ge(s_h2_act, NT)
            sp.wait_ge(s_h2_dve, NT)
            gate_k = exp_w_gate.rearrange("o e (k p) n -> (o e) p k n", p=P)
            up_k = exp_w_up.rearrange("o e (k p) n -> (o e) p k n", p=P)
            down_k = exp_w_down.rearrange("o e (k p) n -> (o e) p k n", p=P)

            def load_expert(e, i):
                gu = wslot[i][:, 0:4096].rearrange("p (k n) -> p k n", k=NK)
                dn_w = wslot[i][:, 4096:6144].rearrange("p (k n) -> p k n", k=2)
                arrived = s_w_in0 if i == 0 else s_w_in1
                sp.dma_start(gu[:, :, 0:FE], gate_k[bass.ds(e, 1)].rearrange("a p k n -> (a p) k n")).then_inc(arrived, 16)
                sp.dma_start(gu[:, :, FE:HALF], up_k[bass.ds(e, 1)].rearrange("a p k n -> (a p) k n")).then_inc(arrived, 16)
                sp.dma_start(dn_w, down_k[bass.ds(e, 1)].rearrange("a p k n -> (a p) k n")).then_inc(arrived, 16)

            for i in range(2):
                load_expert(i, i)
            with sp.Fori(1, NE // 2) as pair:
                for i in range(2):
                    sp.wait_ge(s_w_used, pair * 2 + (i - 1))
                    load_expert(pair * 2 + i, i)
            for t in range(NT):
                sp.wait_ge(s_o_ready, t + 1)
                sp.dma_start(out[0, TILE(t), :], xg if t % 2 == 0 else xTm).then_inc(out_done[t % 2], 16)
            for done in out_done:
                sp.wait_ge(done, 8 * NT)

        @block.gpsimd
        def _(pool):
            pool.memset(ident[:, :], 0.0).then_inc(consts_ready, 1)
            pool.memset(ones[:, :], 1.0).then_inc(consts_ready, 1)
            pool.memset(half[:, :, :], 0.0).then_inc(consts_ready, 1)
            pool.memset(tri[:, :], 1.0).then_inc(consts_ready, 1)
            pool.wait_ge(consts_ready, 4)
            pool.affine_select(out=ident[:, :], in_=ident[:, :], compare_op=ALU.not_equal, fill=1.0, base=0,
                               pattern=[[-1, P]], channel_multiplier=1).then_inc(consts_ready, 1)
            pool.affine_select(out=before[:, :], in_=ones[:, :], compare_op=ALU.is_gt, fill=0.0, base=0,
                               pattern=[[1, P]], channel_multiplier=-1).then_inc(consts_ready, 1)
            pool.affine_select(out=after[:, :], in_=ones[:, :], compare_op=ALU.is_gt, fill=0.0, base=0,
                               pattern=[[-1, P]], channel_multiplier=1).then_inc(consts_ready, 1)
            pool.affine_select(out=tri[:, :], in_=ones[:, :], compare_op=ALU.is_ge, fill=0.0, base=0,
                               pattern=[[1, P]], channel_multiplier=-1).then_inc(consts_ready, 1)
            pool.memset(epsc[:, 0:1], EPS).then_inc(consts_ready, 1)
            pool.memset(epsc[:, 1:2], 1.0).then_inc(consts_ready, 1)
            for p in pre:
                pool.memset(p[:, 0:3], 0.0).then_inc(consts_ready, 1)
            for n, (area, value) in enumerate(((tri[0:CHUNK, CHUNK:P], 0.0), (after[CHUNK:P, 0:CHUNK], 0.0),
                                               (half[0:CHUNK, 0, :], 1.0), (half[CHUNK:P, 1, :], 1.0))):
                pool.wait_ge(consts_ready, 12 + n)
                pool.memset(area, value).then_inc(consts_ready, 1)
            pool.wait_ge(consts_ready, 16)
            pool.dma_start(rowc[:, 0:H], a_log.partition_broadcast(P)).then_inc(rows_in, 16)
            pool.dma_start(rowc[:, H:2 * H], dt_bias.partition_broadcast(P)).then_inc(rows_in, 16)

            pool.wait_ge(s_sa_ready, NT)
            pool.iota(xi, pattern=[[1, P]], base=0, channel_multiplier=0).then_inc(s_dn_consts, 1)
            pool.iota(ji, pattern=[[0, P]], base=0, channel_multiplier=1).then_inc(s_dn_consts, 1)
            pool.affine_select(out=gtm, in_=ones[:, :], compare_op=ALU.is_gt, fill=0.0, base=0,
                               pattern=[[1, P]], channel_multiplier=-1).then_inc(s_dn_consts, 1)
            pool.memset(S_st, 0.0).then_inc(s_dn_consts, 1)
            pool.wait_ge(s_dn_consts, 4)
            for t in range(NT):
                col = slice(t * H, (t + 1) * H)
                if t:
                    pool.wait_ge(s_gb_full, t)
                else:
                    pool.wait_ge(gc_ready, 1)
                pool.tensor_copy(heads(gbt), per_head(gates[:, 1, col])).then_inc(s_gb_ready, 1)
                pool.wait_ge(s_knqn_ready, 2 * (t + 1))
                if t:
                    pool.wait_ge(s_w_full, t)
                    pool.wait_ge(s_ods_full, 2 * t)
                pool.tensor_tensor(heads(kbe), heads(kn), per_head(gates[:, 7, col]), ALU.mult).then_inc(s_pool_k, 1)
                pool.tensor_tensor(heads(kd), heads(kn), per_head(gates[:, 4, col]), ALU.mult).then_inc(s_pool_k, 1)
                pool.wait_ge(s_at_ready, 2 * (t + 1))
                if t:
                    pool.wait_ge(s_p1_full, 5 * t)
                for n in range(1, 6):
                    pool.tensor_tensor(heads(CT[:, n - 1]), heads(AT), each_head(lvl[n]), ALU.mult).then_inc(s_ct_ready, 1)

            pool.wait_ge(s_ont_full, NT)
            pool.affine_select(out=lowm[:, :, :], in_=ones[:, 0:NG * NG].rearrange("p (a b) -> p a b", a=NG),
                               compare_op=ALU.is_gt, fill=0.0, base=0, pattern=[[1, NG], [-1, NG]],
                               channel_multiplier=0).then_inc(s_small_done, 1)
            pool.iota(di[0][:, 0:NE], pattern=[[T, NE]], base=1, channel_multiplier=0).then_inc(s_small_done, 1)
            pool.wait_ge(s_small_done, 2)
            pool.tensor_copy(erow[:, :], di[0][:, 0:NE]).then_inc(s_small_done, 1)
            pool.iota(pay.rearrange("p (t k two) -> p t k two", t=NT, two=2)[:, :, :, 0:1],
                      pattern=[[P, NT], [0, TOP_E], [0, 1]], base=0, channel_multiplier=1).then_inc(s_small_done, 1)
            tv = tbl.rearrange("p (n two) -> p n two", two=2)
            pool.iota(tv[:, :, 0:1], pattern=[[0, NE * CAP], [0, 1]], base=T, channel_multiplier=1).then_inc(s_tbl_init, 1)
            pool.iota(tv[:, :, 1:2], pattern=[[0, NE * CAP], [0, 1]], base=0, channel_multiplier=0).then_inc(s_tbl_init, 1)
            pool.wait_ge(s_y1_full, 2 * NT)
            pool.memset(ysb, 0.0).then_inc(s_tbl_init, 1)
            pool.wait_ge(s_tbl_init, 3)
            pool.dma_start(table_dram.rearrange("(p n) two -> p (n two)", p=P), tbl).then_inc(s_tbl_out, 16)
            pool.dma_start(xn_dram[T:T + P, :], ysb).then_inc(s_pads_out, 16)
            pool.dma_start(acc_dram[T:T + P, :], ysb).then_inc(s_scattered, 16)
            pool.wait_ge(s_tbl_out, 16)
            pool.wait_ge(s_pads_out, 16)
            pool.wait_ge(s_scattered, 16)
            for t in range(NT):
                pool.wait_ge(s_ssg_ready, 2 * (t + 1))
                if t:
                    pool.wait_ge(s_shT_full, t)
                pool.tensor_tensor(hm, sg, upb, ALU.mult).then_inc(s_shm_ready, 1)
            for t in range(NT):
                pool.wait_ge(s_lists_ready, t + 1)
                for k in range(TOP_E):
                    j = t * TOP_E + k
                    pool.indirect_dma_start(table_dram, bass.IndirectOffsetOnAxis(dest_i[:, j:j + 1], 0),
                                            pay[:, 2 * j:2 * j + 2], None).then_inc(s_slots_out, 16)
            pool.wait_ge(s_slots_out, 16 * NT * TOP_E)
            pool.dma_start(tbl, table_dram.rearrange("(p n) two -> p (n two)", p=P)).then_inc(s_tbl_in, 16)
            for rows in (idx_now, idx_last, idx_hold):
                pool.iota(rows[:, 0:1], pattern=[[0, 1]], base=T, channel_multiplier=1).then_inc(s_idx_s, 1)
            pool.memset(xg, 0.0).then_inc(s_moe_zero, 1)
            pool.iota(idx_zero[:, 0:1], pattern=[[0, 1]], base=0, channel_multiplier=0).then_inc(s_moe_zero, 1)
            pool.wait_ge(s_moe_zero, 2)
            pool.wait_ge(s_idx_s, 3)
            pool.wait_ge(s_tbl_in, 16)
            pool.wait_ge(s_xn_out, 16 * NT)
            for done in acc_out:
                pool.wait_ge(done, 8 * NT)
            pool.wait_ge(s_cnt_ready, 1)

            def gather(g):
                pool.indirect_dma_start(xg, None, xn_dram, bass.IndirectOffsetOnAxis(idx_now[:, 0:1], 0)).then_inc(s_gathered, 16)

            def shift(dst, src, done):
                pool.tensor_tensor(dst[:, 0:1], src[:, 0:1], idx_zero[:, 0:1], ALU.add).then_inc(s_idx_s, 1)
                pool.wait_ge(s_idx_s, done)
                pool.sem_inc(s_paced, 1)

            def scatter(g):
                pool.wait_ge(s_scattered, 16 * g + 16)
                pool.sem_inc(s_paced, 1)
                shift(idx_out, idx_hold, 3 * g + 4)
                shift(idx_hold, idx_last, 3 * g + 5)
                shift(idx_last, idx_now, 3 * g + 6)
                pool.wait_ge(s_y_act, g + 1)
                pool.sem_inc(s_paced, 1)
                pool.wait_ge(s_y_dve, g + 1)
                pool.sem_inc(s_paced, 1)
                pool.indirect_dma_start(acc_dram, bass.IndirectOffsetOnAxis(idx_out[:, 0:1], 0), ysb, None,
                                        compute_op=ALU.add).then_inc(s_scattered, 16)

            with pool.Fori(0, NE) as e:
                nb = pool.value_load(ints[0:1, bass.ds(e, 1)], min_val=1, max_val=CAP)
                b0 = pool.value_load(ints[0:1, bass.ds(e + NE, 1)], min_val=0, max_val=NE * CAP)
                with pool.Fori(0, nb) as b:
                    g = pool.snap(b0 + b)
                    pool.wait_ge(s_xg_read, g + 1)
                    pool.tensor_tensor(idx_now[:, 0:1], tbl[:, bass.ds((e * CAP + b) * 2, 1)], idx_zero[:, 0:1],
                                       ALU.add).then_inc(s_idx_g, 1)
                    pool.wait_ge(s_idx_g, g + 1)
                    pool.sem_inc(s_paced, 1)
                    gather(g)
                    scatter(g)
            total = pool.value_load(ints[0:1, 2 * NE:2 * NE + 1], min_val=NE, max_val=NE * CAP)
            pool.wait_ge(s_xg_read, total + 1)
            pool.sem_inc(s_paced, 1)
            gather(total)
            scatter(total)
            scatter(total + 1)
            pool.wait_ge(s_scattered, 16 * total + 48)
            pool.sem_inc(s_paced, 1)
            for t in range(NT):
                pool.dma_start(x3[:, t, :], acc_dram[TILE(t), :]).then_inc(s_acc_in, 16)

        @block.scalar
        def _(act):
            def copy(out_, in_, **kw):
                return act.activation(out_, in_, ACT.Copy, **kw)

            chain = [0]

            def link(ins):
                chain[0] += 1
                ins.then_inc(av, 1)
                act.wait_ge(av, chain[0])

            act.wait_ge(vT_ready, 1)
            act.activation(cond[:, :], vT[:, V_C:V_C + NK], ACT.Silu).then_inc(cond_ready, 1)
            act.wait_ge(x_in, 16 * NT)
            for t in range(NT):
                link(act.activation(sqx, xt_in[:, t, :], ACT.Square, accum_out=st[:, 0, t:t + 1]))
            act.wait_ge(consts_ready, 16)
            act.activation(st[:, 1, 0:NT], st[:, 0, 0:NT], ACT.Sqrt, scale=1.0 / D, bias=epsc[:, 0:1]).then_inc(rms_ready, 1)

            def group(name, i, j):
                g = GIDX[(name, i, j)]
                act.wait_ge(ring_full, g + 1)
                return ring_bank(g)

            free = ring_free["act"]
            act.wait_ge(ab1_ready, 1)
            for hf in range(2):
                for k in range(1, NK, 2):
                    b = group("hT", k, hf)
                    act.activation(hT[:, k, hf * HALF:(hf + 1) * HALF], b, ACT.Identity, scale=A1[:, k:k + 1],
                                   bias=B1[:, k:k + 1]).then_inc(free, 1)
            for t in range(NT):
                b = group("aux", t, 0)
                copy(aux[:, t, :], b[:, 0:AUX])
                act.activation(sqx[:, 0:KV_R], b[:, 0:KV_R], ACT.Square, accum_out=st[:, 3, t:t + 1]).then_inc(free, 1)
                act.wait_ge(free, nth[GIDX[("aux", t, 0)]])
            for ct in range(2):
                for hf in range(2):
                    copy(qixT[:, ct, hf * HALF:(hf + 1) * HALF], group("qix", ct, hf)).then_inc(free, 1)
            act.wait_ge(stats_asked, 1)
            act.activation(st[:, 3, 8:16], st[:, 3, 0:8], ACT.Sqrt, scale=1.0 / KV_R, bias=epsc[:, 0:1])
            act.activation(st[:, 2, 16:24], st[:, 2, 8:16], ACT.Sqrt, scale=1.0 / IX_D, bias=epsc[:, 0:1]).then_inc(stats_rooted, 1)
            for u in range(len(SEL_TILES) * H):
                n = (SEL_TILES[u // H] + 1) * P
                act.wait_ge(ixs_full, u + 1)
                if u >= 2:
                    act.wait_ge(rel_used, u - 1)
                act.activation(rel[u % 2][:, 0:n], bank(4 + 2 * (u % 2), 2)[:, 0:n], ACT.Relu).then_inc(rel_ready, 1)
            act.wait_ge(gate_in, 1)
            act.wait_ge(rows_in, 32)
            act.activation(gates[:, 0, :], gates[:, 8, :], ACT.Sigmoid)
            act.activation(rowc[:, 0:H], rowc[:, 0:H], ACT.Exp)
            act.activation(gates[:, 3, :], gates[:, 2, :], ACT.Abs).then_inc(gate_act, 1)
            act.wait_ge(gate_act, 1)
            act.activation(gates[:, 4, :], gates[:, 3, :], ACT.Exp, scale=-1.0).then_inc(gate_act, 1)
            act.wait_ge(gate_act, 2)
            act.activation(gates[:, 5, :], gates[:, 4, :], ACT.Ln, bias=epsc[:, 1:2]).then_inc(gate_act, 1)
            act.wait_ge(gc_full, 1)
            NC = NT * H
            act.activation(gates[:, 3, :], bank(7)[:, 0:NC], ACT.Exp)
            act.activation(gates[:, 4, :], bank(7)[:, NC:2 * NC], ACT.Exp)
            act.activation(gates[:, 5, :], bank(7)[:, 2 * NC:3 * NC], ACT.Exp)
            act.activation(gates[:, 6, :], bank(7)[:, 3 * NC:4 * NC], ACT.Exp).then_inc(gate_act, 1)
            for h in range(H):
                for hf in range(2):
                    copy(khT[:, h, hf * HALF:(hf + 1) * HALF], group("kh", h, hf)).then_inc(free, 1)
            for t in range(NT):
                copy(vh[:, t, :], group("vh", t, 0)).then_inc(free, 1)
            for h in range(H):
                for hf in range(2):
                    copy(qsaT[:, h, hf * HALF:(hf + 1) * HALF], group("qsa", h, hf)).then_inc(free, 1)
            for t in range(NT):
                act.activation(zg[:, t, :], group("z", t, 0), ACT.Silu).then_inc(free, 1)
            act.wait_ge(rel_used, len(SEL_TILES) * H)
            act.wait_ge(gc_ready, 1)
            act.wait_ge(consts_ready, 16)

            def conv_act_fn(ct):
                act.wait_ge(conv_ready, 2 * ct + 2)
                act.activation(qkvT[:, ct, :], qkvT[:, ct, :], ACT.Silu).then_inc(conv_act, 1)

            for ct in range(12):
                for hf in range(2):
                    n = 2 * ct + hf
                    b = group("conv", ct, hf)
                    if n >= 2:
                        act.wait_ge(conv_ready, n - 1)
                    if hf:
                        act.wait_ge(pre_ready, n)
                        link(copy(pre[1][:, 0:3], pre[0][:, HALF:HALF + 3]))
                    copy(pre[hf][:, 3:3 + HALF], b).then_inc(pre_ready, 1)
                    col = V_ROWS + (CONV_K - 1) * 12 + ct
                    copy(qkvT[:, ct, hf * HALF:(hf + 1) * HALF], b, scale=vT[:, col:col + 1]).then_inc(free, 1)
                if ct:
                    conv_act_fn(ct - 1)
            conv_act_fn(11)

            def pt_evac(u):
                for gi in pt_groups(u):
                    if gi % 2 == 0:
                        n = pt_cols(u, gi)
                        act.wait_ge(s_pt_full, gi + 1)
                        if u >= 2:
                            act.wait_ge(s_o_full, u - 1)
                        copy(prT[u % 2][:, n], bank(0)[:, 0:n.stop - n.start]).then_inc(s_pt_act, 1)

            for u in range(NT * H + 1):
                if u < NT * H:
                    n = (u // H + 1) * P
                    act.wait_ge(s_mx_ready, u + 1)
                    act.activation(lg[u % 2][:, 0:n], lg[u % 2][:, 0:n], ACT.Exp, scale=SM_SCALE,
                                   bias=st[:, 1, u:u + 1], accum_out=st[:, 2, u:u + 1]).then_inc(s_pr_ready, 1)
                if u:
                    pt_evac(u - 1)
                if u > H and (u - 1) % H == 1:
                    sa_evac(act, (u - 1) // H - 1)
            sa_evac(act, NT - 1)

            for ct in range(8):
                if ct >= 4:
                    act.wait_ge(nrm_full, ct - 3)
                else:
                    act.wait_ge(s_oT_full, NT)
                act.activation(at(4 * (ct % 4), T), qkvT[:, ct, :], ACT.Square).then_inc(sq_ready, 1)
            act.wait_ge(nrm_full, 8)
            act.activation(st[:, 0, :], bank(7)[:, 0:NT * 8], ACT.Sqrt, bias=epsc[:, 0:1]).then_inc(s_nrm_ready, 1)
            for t in range(NT):
                for i, dst in enumerate((knT, kbT, qnT, qdT)):
                    act.wait_ge(s_t_full, 4 * t + i + 1)
                    copy(dst, bank(3 + i)).then_inc(s_t_act, 1)
                act.wait_ge(s_dd_ready, t + 1)
                act.activation(ET, ET, ACT.Exp).then_inc(s_dd_exp, 1)
                act.wait_ge(s_x1_full, t + 1)
                copy(X, bank(2)).then_inc(s_x1_ready, 1)
                for l in range(5):
                    act.wait_ge(s_p1_full, 5 * t + l + 1)
                    copy(P1, bank(3)).then_inc(s_p1_ready, 1)
                act.wait_ge(s_w_full, t + 1)
                copy(wT, bank(6)).then_inc(s_w_ready, 1)
                for cc in range(2):
                    R = slice(cc * CHUNK, (cc + 1) * CHUNK)
                    act.wait_ge(s_vn_full, 2 * t + cc + 1)
                    copy(vn[R, :], bank(7)[R, :]).then_inc(s_vn_ready, 1)
                act.wait_ge(s_ods_full, 2 * (t + 1))
                if t:
                    act.wait_ge(s_oz_ready, t)
                act.activation(osq, bank(2), ACT.Square).then_inc(s_o_sq, 1)
            act.wait_ge(s_oz_ready, NT)
            act.activation(st[:, 1, 0:NC], st[:, 1, 32:64], ACT.Sqrt, scale=1.0 / DH, bias=epsc[:, 0:1]).then_inc(s_orms_ready, 1)
            for t in range(NT):
                act.wait_ge(s_ont_full, t + 1)
                copy(qkvT[:, 0:H, TILE(t)], heads(bank(t % 2)), scale=vT[:, V_DG:V_DG + 1]).then_inc(s_dnT_ready, 1)

            for t in range(NT):
                act.wait_ge(s_y1_read, 2 * (NT + t + 1))
                act.activation(junk, x2[:, t, :], ACT.Square, accum_out=st[:, 0, t:t + 1]).then_inc(s_ssq2_ready, 1)
                act.wait_ge(s_ssq2_ready, t + 1)
                act.activation(st[:, 1, t:t + 1], st[:, 0, t:t + 1], ACT.Sqrt, scale=1.0 / D, bias=epsc[:, 0:1]).then_inc(s_rms2_ready, 1)
            for m in range(0, 16, 2):
                hf, k = m // 8, m % 8
                act.wait_ge(s_h2_full, m + 1)
                act.wait_ge(s_ab2_ready, 1)
                act.activation(h2T[:, k, hf * HALF:(hf + 1) * HALF], bank(4 + m % 4), ACT.Identity,
                               scale=A2[:, k:k + 1], bias=B2[:, k:k + 1]).then_inc(s_h2_act, 1)
            act.wait_ge(s_rl_full, 1)
            act.activation(r_sc, bank(0), ACT.Sigmoid).then_inc(s_rsc_ready, 1)
            for t in range(NT):
                b = bank(4 + t % 2)
                act.wait_ge(s_sgu_full, t + 1)
                if t:
                    act.wait_ge(s_shm_ready, t)
                act.activation(sg, b[:, 0:FE], ACT.Silu).then_inc(s_ssg_ready, 1)
                copy(upb, b[:, FE:2 * FE]).then_inc(s_ssg_ready, 1)
                act.wait_ge(s_shT_full, t + 1)
                copy(hmT, bank(6)[:, 0:FE]).then_inc(s_shT_ready, 1)
                if t >= 2:
                    act.wait_ge(acc_out[t % 2], 16 * (t // 2))
                act.wait_ge(s_sy_full, 2 * t + 1)
                copy(ysh[t % 2][:, 0:HALF], bank(7)).then_inc(s_sy_act, 1)
                act.wait_ge(s_sy_full, 2 * t + 2)
                copy(ysh[t % 2][:, HALF:D], bank(0)).then_inc(s_sy_act, 1)
                act.wait_ge(s_sy_act, 2 * t + 2)
                act.dma_start(acc_dram[TILE(t), :], ysh[t % 2]).then_inc(acc_out[t % 2], 16)
            for done in acc_out:
                act.wait_ge(done, 8 * NT)

            tf = tbl.bitcast(F32)

            def x_evac():
                for k in range(4):
                    ins = act.activation(xTm[:, k * P:(k + 1) * P], bank(0)[:, k * P:(k + 1) * P], ACT.Identity,
                                         scale=A2[:, k:k + 1], bias=B2[:, k:k + 1])
                ins.then_inc(s_xT_act, 1)

            act.wait_ge(s_cnt_ready, 1)
            act.wait_ge(s_tbl_in, 16)
            act.wait_ge(s_xg_read, 2)
            x_evac()
            act.activation(epsc[:, 2:3], epsc[:, 0:1], ACT.Copy).then_inc(s_y_act, 2)
            with act.Fori(0, NE) as e:
                nb = act.value_load(ints[0:1, bass.ds(e, 1)], min_val=1, max_val=CAP)
                b0 = act.value_load(ints[0:1, bass.ds(e + NE, 1)], min_val=0, max_val=NE * CAP)
                with act.Fori(0, nb) as b:
                    g = act.snap(b0 + b)
                    act.wait_ge(s_gu_full, g + 1)
                    act.activation(sg, bank(2)[:, 0:FE], ACT.Silu).then_inc(s_silu_done, 1)
                    act.wait_ge(s_hT_full, g + 1)
                    copy(hmT, bank(3)[:, 0:FE]).then_inc(s_hT_ready, 1)
                    act.wait_ge(s_xg_read, g + 3)
                    x_evac()
                    act.wait_ge(s_scattered, 16 * g + 48)
                    act.wait_ge(s_y_full, 2 * g + 1)
                    copy(ysb[:, 0:HALF], bank(4), scale=tf[:, bass.ds((e * CAP + b) * 2 + 1, 1)]).then_inc(s_y_act, 1)

            for t in range(NT):
                act.wait_ge(s_x3_ready, t + 1)
                act.activation(ysb, x3[:, t, :], ACT.Square, accum_out=st[:, 0, t:t + 1]).then_inc(s_ssq3_ready, 1)
                act.wait_ge(s_ssq3_ready, t + 1)
                act.activation(st[:, 1, t:t + 1], st[:, 0, t:t + 1], ACT.Sqrt, scale=1.0 / D, bias=epsc[:, 0:1]).then_inc(s_rms3_ready, 1)

        @block.tensor
        def _(pe):
            def mm(out_, lhsT, rhs, first, last):
                return pe.matmul(out_, lhsT, rhs, start=first, stop=last)

            def panel_in(name):
                i = PAN[name]
                pe.wait_ge(pan_in[i % NBUF], landed[i])
                return pan(name)

            pe.wait_ge(consts_ready, 16)
            pe.wait_ge(vecs_in, 16 * 11)
            pe.transpose(bank(7)[:, 0:V_ROWS], vecs[:, :], ident[0:V_ROWS, 0:V_ROWS])
            pe.transpose(bank(7)[:, P:P + 48], cwr[:, :], ident[0:48, 0:48]).then_inc(vecs_turned, 1)
            pe.wait_ge(cond_ready, 1)

            def ada_columns(names, base):
                for i, name in enumerate(names):
                    w = panel_in(name)
                    for j in range(4):
                        for k in range(NK):
                            ins = mm(bank(6)[:, base + 4 * i + j:base + 4 * i + j + 1], w[:, k, j * P:(j + 1) * P],
                                     cond[:, k:k + 1], k == 0, k == NK - 1)
                    ins.then_inc(pan_used, 1)

            ada_columns([f"ada{i}" for i in range(4)], 0)

            def begin(name, i, j):
                g = GIDX[(name, i, j)]
                ring_wait(pe, g)
                return ring_bank(g)

            for hf in range(2):
                pe.wait_ge(xhat_ready, 4 * (hf + 1))
                for k in range(NK):
                    b = begin("hT", k, hf)
                    for q in range(4):
                        ins = pe.transpose(b[:, q * P:(q + 1) * P], xt_in[:, 4 * hf + q, k * P:(k + 1) * P], ident[:, :])
                    ins.then_inc(ring_full, 1)
            for eng in ("act", "dve"):
                pe.wait_ge(ring_free[eng], 8)
            w = panel_in("aux")
            for t in range(NT):
                b = begin("aux", t, 0)
                for k in range(NK):
                    ins = mm(b[:, 0:AUX], hT[:, k, TILE(t)], w[:, k, :], k == 0, k == NK - 1)
                ins.then_inc(ring_full, 1)

            def channels(name, j, w, c0, more=None):
                for hf in range(2):
                    b = begin(name, j, hf)
                    for k in range(NK):
                        ins = mm(b, w[:, k, c0:c0 + P], hT[:, k, hf * HALF:(hf + 1) * HALF], k == 0, k == NK - 1)
                    ins.then_inc(ring_full, 1)

            w = panel_in("qix")
            channels("qix", 0, w, 0)
            channels("qix", 1, w, P)
            pe.wait_ge(kv_ready, 1)
            for k in range(2):
                for hf in range(2):
                    b = begin("ckvT", k, hf)
                    for q in range(4):
                        ins = pe.transpose(b[:, q * P:(q + 1) * P], aux[:, 4 * hf + q, k * P:(k + 1) * P], ident[:, :])
                    ins.then_inc(ring_full, 1)
            for hf in range(2):
                b = begin("kixT", 0, hf)
                for q in range(4):
                    ins = pe.transpose(b[:, q * P:(q + 1) * P], kx2[:, 4 * hf + q, :], ident[:, :])
                ins.then_inc(ring_full, 1)
            pe.drain().then_inc(pan_used, 2)

            pe.wait_ge(ring_free["dve"], nth[GIDX[("kixT", 0, 1)]])
            pe.wait_ge(ring_free["act"], nth[GIDX[("qix", 1, 1)]])
            for u in range(len(SEL_TILES) * H):
                t, h = SEL_TILES[u // H], u % H
                if u >= 2:
                    pe.wait_ge(rel_ready, u - 1)
                R = slice((h % 2) * IX_D, (h % 2) * IX_D + IX_D)
                b = bank(4 + 2 * (u % 2), 2)
                for c0 in range(0, (t + 1) * P, HALF):
                    n = min(HALF, (t + 1) * P - c0)
                    ins = mm(b[:, c0:c0 + n], qixT[R, h // 2, TILE(t)], kixT[R, c0:c0 + n], True, True)
                ins.then_inc(ixs_full, 1)
            pe.wait_ge(g_ready, 1)
            pe.wait_ge(rel_ready, len(SEL_TILES) * H)
            NC = NT * H
            for i, m in enumerate((tri[:, :], after[:, :], half[:, 0, :], half[:, 1, :])):
                ins = mm(bank(7)[:, i * NC:(i + 1) * NC], m, gates[:, 1, :], True, True)
            ins.then_inc(gc_full, 1)
            pe.wait_ge(w_small, 48)
            for h in range(H):
                for hf in range(2):
                    b = begin("kh", h, hf)
                    for k in range(2):
                        ins = mm(b, wuk[:, h, k, :], ckvT[:, k, hf * HALF:(hf + 1) * HALF], k == 0, k == 1)
                    ins.then_inc(ring_full, 1)
            for t in range(NT):
                b = begin("vh", t, 0)
                for k in range(2):
                    ins = mm(b, ckvT[:, k, TILE(t)], wuv[:, k].rearrange("p h n -> p (h n)"), k == 0, k == 1)
                ins.then_inc(ring_full, 1)
            w = panel_in("qsa")
            for h in range(H):
                channels("qsa", h, w, h * DH)
            pe.drain().then_inc(pan_used, 1)
            w = panel_in("z")
            for t in range(NT):
                b = begin("z", t, 0)
                for k in range(NK):
                    ins = mm(b, hT[:, k, TILE(t)], w[:, k, :], k == 0, k == NK - 1)
                ins.then_inc(ring_full, 1)
            pe.drain().then_inc(pan_used, 1)
            for i, name in enumerate(("q", "k", "v")):
                w = panel_in(name)
                for j in range(4):
                    channels("conv", 4 * i + j, w, j * P)
                pe.drain().then_inc(pan_used, 1)

            def logits(u):
                t, h = u // H, u % H
                if u >= 2:
                    pe.wait_ge(s_lg_ready, u - 1)
                b = bank(4 + 2 * (u % 2), 2)
                for c0 in range(0, (t + 1) * P, HALF):
                    n = min(HALF, (t + 1) * P - c0)
                    ins = mm(b[:, c0:c0 + n], qsaT[:, h, TILE(t)], khT[:, h, c0:c0 + n], True, True)
                ins.then_inc(s_lg_full, 1)

            def attend(u):
                t, h = u // H, u % H
                pe.wait_ge(s_pr_ready, u + 1)
                for gi in pt_groups(u):
                    if gi >= 2:
                        pe.wait_ge(s_pt_dve if gi % 2 else s_pt_act, gi // 2)
                    n = pt_cols(u, gi)
                    for c0 in range(n.start, n.stop, P):
                        ins = pe.transpose(bank(gi % 2)[:, c0 - n.start:c0 - n.start + P], lg[u % 2][:, c0:c0 + P], ident[:, :])
                    ins.then_inc(s_pt_full, 1)
                last = pt_groups(u)[-1]
                pe.wait_ge(s_pt_act, last // 2 + 1)
                if last:
                    pe.wait_ge(s_pt_dve, (last + 1) // 2)
                if h == 0 and t:
                    pe.wait_ge(s_osa_ready, t)
                for kb_ in range(t + 1):
                    ins = mm(bank(2)[:, HSL(h)], prT[u % 2][:, kb_ * P:(kb_ + 1) * P], vh[:, kb_, HSL(h)], kb_ == 0, kb_ == t)
                ins.then_inc(s_o_full, 1)

            def turn_out(t):
                pe.wait_ge(s_osa_ready, t + 1)
                if t:
                    pe.wait_ge(s_sa_ready, t)
                for h in range(H):
                    ins = pe.transpose(bank(3)[:, HSL(h)], osa[:, HSL(h)], ident[:, :])
                ins.then_inc(s_oT_full, 1)

            pe.wait_ge(ring_free["act"], n_of["act"])
            logits(0)
            for u in range(NT * H):
                if u + 1 < NT * H:
                    logits(u + 1)
                attend(u)
                if u > H and u % H == 1:
                    turn_out(u // H - 1)
            turn_out(NT - 1)

            pe.wait_ge(s_lg_ready, NT * H)
            for ct in range(8):
                pe.wait_ge(sq_ready, ct + 1)
                for t in range(NT):
                    ins = mm(bank(7)[:, t * 8 + ct:t * 8 + ct + 1], at(4 * (ct % 4), T)[:, TILE(t)], ones[:, 0:1], True, True)
                ins.then_inc(nrm_full, 1)
            pe.wait_ge(s_sa_ready, NT)
            pe.wait_ge(conv_act, 12)
            for t in range(NT):
                if t:
                    pe.wait_ge(s_oz_ready, t)
                    pe.wait_ge(s_o_sq, t)
                for i in range(3):
                    for h in range(H):
                        ins = pe.transpose(bank(i)[:, HSL(h)], qkvT[:, 4 * i + h, TILE(t)], ident[:, :])
                    ins.then_inc(s_qkv_full, 1)
                pe.wait_ge(s_gb_ready, t + 1)
                pe.wait_ge(s_nrm_ready, 1)
                for h in range(H):
                    ins = mm(bank(7)[:, HSL(h)], heads(gbt)[:, h, :], tri[:, :], True, True)
                ins.then_inc(s_gb_full, 1)
                for i, src in enumerate((kn, kb, qn, qd)):
                    pe.wait_ge(s_kk_full, 4 * t + i + 1)
                    for h in range(H):
                        ins = pe.transpose(bank(3 + i)[:, HSL(h)], src[:, HSL(h)], ident[:, :])
                    ins.then_inc(s_t_full, 1)
                pe.wait_ge(s_t_act, 4 * t + 4)
                for i, (l_, r_) in enumerate(((knT, kbT), (knT, qnT))):
                    for h in range(H):
                        ins = mm(bank(i)[:, HSL(h)], l_[:, HSL(h)], r_[:, HSL(h)], True, True)
                    ins.then_inc(s_p_kk, 1)
                pe.wait_ge(s_xt1_ready, t + 1)
                for h in range(H):
                    ins = pe.transpose(bank(2)[:, HSL(h)], XT[:, HSL(h)], ident[:, :])
                ins.then_inc(s_x1_full, 1)
                pe.wait_ge(s_x1_ready, t + 1)
                for l in range(5):
                    pe.wait_ge(s_ct_ready, 5 * t + l + 1)
                    if l:
                        pe.wait_ge(s_dx_ready, 9 * t + 2 * l)
                    for h in range(H):
                        ins = mm(bank(3)[:, HSL(h)], CT[:, l, HSL(h)], X[:, HSL(h)], True, True)
                    ins.then_inc(s_p1_full, 1)
                    pe.wait_ge(s_p1_ready, 5 * t + l + 1)
                    for h in range(H):
                        ins = mm(bank(4)[:, HSL(h)], P1[:, HSL(h)], XT[:, HSL(h)], True, True)
                    ins.then_inc(s_dx_full, 1)
                    if l < 4:
                        for h in range(H):
                            ins = mm(bank(5)[:, HSL(h)], XT[:, HSL(h)], P1[:, HSL(h)], True, True)
                        ins.then_inc(s_dx_full, 1)
                pe.wait_ge(s_dx_ready, 9 * (t + 1))
                pe.wait_ge(s_pool_k, 2 * (t + 1))
                for h in range(H):
                    ins = mm(bank(6)[:, HSL(h)], kbe[:, HSL(h)], XT[:, HSL(h)], True, True)
                ins.then_inc(s_w_full, 1)
                pe.wait_ge(s_w_ready, t + 1)
                for cc in range(2):
                    R = slice(cc * CHUNK, (cc + 1) * CHUNK)
                    n = 2 * t + cc
                    if n:
                        pe.wait_ge(s_s_ready, n)
                    else:
                        pe.wait_ge(s_dn_consts, 4)
                    for h in range(H):
                        C = slice(h * DH + cc * CHUNK, h * DH + (cc + 1) * CHUNK)
                        mm(bank(7)[R, HSL(h)], XT[R, C], bv[R, HSL(h)], True, False)
                        ins = mm(bank(7)[R, HSL(h)], wT[:, C], S_st[:, HSL(h)], False, True)
                    ins.then_inc(s_vn_full, 1)
                    pe.wait_ge(s_vn_ready, n + 1)
                    for h in range(H):
                        C = slice(h * DH + cc * CHUNK, h * DH + (cc + 1) * CHUNK)
                        mm(bank(2)[R, HSL(h)], qdT[:, C], S_st[:, HSL(h)], True, False)
                        mm(bank(2)[R, HSL(h)], QKT[R, C], vn[R, HSL(h)], False, True)
                    for h in range(H):
                        ins = mm(bank(4 + cc)[:, HSL(h)], kd[R, HSL(h)], vn[R, HSL(h)], True, True)
                    ins.then_inc(s_ods_full, 1)
            for t in range(NT):
                pe.wait_ge(s_on_ready, t + 1)
                if t >= 2:
                    pe.wait_ge(s_dnT_ready, t - 1)
                for h in range(H):
                    ins = pe.transpose(bank(t % 2)[:, HSL(h)], zg[:, t, HSL(h)], ident[:, :])
                ins.then_inc(s_ont_full, 1)

            def ada_rows(names, b0):
                for i, name in enumerate(names):
                    w = panel_in(name)
                    for k in range(NK):
                        ins = mm(bank(b0 + i), condrep[:, k, :], w[:, k, :], k == 0, k == NK - 1)
                    ins.then_inc(pan_used, 1)

            pe.wait_ge(s_gt1_full, 1)
            ada_rows(("ada4", "ada5"), 4)
            ada_columns([f"ada{i}" for i in range(6, 10)], 0)
            pe.wait_ge(s_gt1_ready, 1)
            ada_rows(("ada10", "ada11"), 4)
            pe.wait_ge(s_dnT_ready, NT)
            for n in range(2):
                w = panel_in(f"wo{n}")
                for t in range(NT):
                    gi = n * NT + t
                    if gi >= 4:
                        pe.wait_ge(s_y1_read, 2 * (gi - 3) - 1)
                    for k in range(NK):
                        mixT = qkvT[:, k, TILE(t)] if k < H else qsaT[:, k - H, TILE(t)]
                        ins = mm(bank(gi % 4), mixT, w[:, k, :], k == 0, k == NK - 1)
                    ins.then_inc(s_y1_full, 1)
                pe.drain().then_inc(pan_used, 1)
            pe.wait_ge(s_ab2_ready, 1)
            pe.wait_ge(s_gt2_ready, 1)
            for m in range(16):
                hf, k = m // 8, m % 8
                pe.wait_ge(s_xh2_ready, 4 * (hf + 1))
                if m >= 4:
                    pe.wait_ge(s_h2_dve if m % 2 else s_h2_act, (m - 4) // 2 + 1)
                for q in range(4):
                    ins = pe.transpose(bank(4 + m % 4)[:, q * P:(q + 1) * P], xh2[:, 4 * hf + q, k * P:(k + 1) * P], ident[:, :])
                ins.then_inc(s_h2_full, 1)
            pe.wait_ge(s_h2_act, 8)
            pe.wait_ge(s_h2_dve, 8)
            w = panel_in("router")
            for t in range(NT):
                for k in range(NK):
                    ins = mm(bank(0)[:, t * NE:(t + 1) * NE], h2T[:, k, TILE(t)], w[:, k, :], k == 0, k == NK - 1)
            ins.then_inc(s_rl_full, 1)
            pe.wait_ge(s_rsc_ready, 1)
            wgu, wd = panel_in("sgu"), None
            for t in range(NT):
                b = bank(4 + t % 2)
                for k in range(NK):
                    ins = mm(b, h2T[:, k, TILE(t)], wgu[:, k, :], k == 0, k == NK - 1)
                ins.then_inc(s_sgu_full, 1)
                if t == 0:
                    pe.drain().then_inc(pan_used, 1)
                    wd = panel_in("sd")
                if t == 3:
                    pe.wait_ge(s_mask_ready, 1)
                    for tt in range(NT):
                        for t2 in range(tt):
                            mm(bank(1)[:, tt * NE:(tt + 1) * NE], ones[:, :], r_mk[:, t2 * NE:(t2 + 1) * NE], t2 == 0, False)
                        mm(bank(1)[:, tt * NE:(tt + 1) * NE], before[:, :], r_mk[:, tt * NE:(tt + 1) * NE], tt == 0, True)
                    for tt in range(NT):
                        ins = mm(bank(2)[:, 0:NE], ones[:, :], r_mk[:, tt * NE:(tt + 1) * NE], tt == 0, tt == NT - 1)
                    ins.then_inc(s_pos_full, 1)
                if t == 5:
                    pe.wait_ge(s_nbr_ready, 1)
                    mm(bank(3)[0:NE, 0:P], nbf[0:1, :], ones[0:1, :], True, True).then_inc(s_nbt_full, 1)
                    pe.wait_ge(s_nbt_ready, 1)
                    mm(bank(3)[:, P:P + NE], nbc, before[0:NE, 0:NE], True, True).then_inc(s_bs_full, 1)
                pe.wait_ge(s_shm_ready, t + 1)
                for i in range(2):
                    ins = pe.transpose(bank(6)[:, i * P:(i + 1) * P], hm[:, i * P:(i + 1) * P], ident[:, :])
                ins.then_inc(s_shT_full, 1)
                pe.wait_ge(s_shT_ready, t + 1)
                if t:
                    pe.wait_ge(s_sy_act, 2 * t)
                for n, bb in enumerate((bank(7), bank(0))):
                    for k in range(2):
                        ins = mm(bb, hmT[:, k * P:(k + 1) * P], wd[:, k, n * HALF:(n + 1) * HALF], k == 0, k == 1)
                    ins.then_inc(s_sy_full, 1)

            def turn_x():
                for k in range(NK):
                    ins = pe.transpose(bank(0, 2)[:, k * P:(k + 1) * P], xg[:, k * P:(k + 1) * P], ident[:, :])
                ins.then_inc(s_xg_read, 1)

            pe.wait_ge(s_sy_act, 2 * NT)
            pe.wait_ge(s_cnt_ready, 1)
            pe.drain().then_inc(s_xg_read, 1)
            pe.wait_ge(s_gathered, 16)
            turn_x()
            with pe.Fori(0, NE // 2) as pair:
                for i in range(2):
                    e = pair * 2 + i
                    gu = wslot[i][:, 0:4096].rearrange("p (k n) -> p k n", k=NK)
                    dw = wslot[i][:, 4096:6144].rearrange("p (k n) -> p k n", k=2)
                    nb = pe.value_load(ints[0:1, bass.ds(e, 1)], min_val=1, max_val=CAP)
                    b0 = pe.value_load(ints[0:1, bass.ds(e + NE, 1)], min_val=0, max_val=NE * CAP)
                    with pe.Fori(0, nb) as b:
                        g = pe.snap(b0 + b)
                        pe.wait_ge(s_w_in0 if i == 0 else s_w_in1, pair * 48 + 48)
                        pe.wait_ge(s_xT_act, g + 1)
                        pe.wait_ge(s_xT_dve, g + 1)
                        for k in range(NK):
                            ins = mm(bank(2), xTm[:, k * P:(k + 1) * P], gu[:, k, :], k == 0, k == NK - 1)
                        ins.then_inc(s_gu_full, 1)
                        pe.wait_ge(s_gathered, 16 * g + 32)
                        turn_x()
                        pe.wait_ge(s_hm_ready, g + 1)
                        for k in range(2):
                            ins = pe.transpose(bank(3)[:, k * P:(k + 1) * P], hm[:, k * P:(k + 1) * P], ident[:, :])
                        ins.then_inc(s_hT_full, 1)
                        pe.wait_ge(s_hT_ready, g + 1)
                        pe.wait_ge(s_y_act, g + 2)
                        pe.wait_ge(s_y_dve, g + 2)
                        for n in range(2):
                            for k in range(2):
                                ins = mm(bank(4 + n), hmT[:, k * P:(k + 1) * P], dw[:, k, n * HALF:(n + 1) * HALF], k == 0, k == 1)
                            ins.then_inc(s_y_full, 1)
                    pe.drain().then_inc(s_w_used, 1)

        @block.vector
        def _(dve):
            chain = [0]

            def link(ins):
                chain[0] += 1
                ins.then_inc(dv, 1)
                dve.wait_ge(dv, chain[0])

            tt, ts, stt = dve.tensor_tensor, dve.tensor_scalar, dve.scalar_tensor_tensor
            dve.wait_ge(vecs_turned, 1)
            dve.tensor_copy(vT[:, 0:V_ROWS], bank(7)[:, 0:V_ROWS])
            link(dve.tensor_copy(vT[:, V_ROWS:V_ROWS + 48], bank(7)[:, P:P + 48]))
            dve.engine_nop().then_inc(vT_ready, 1)
            dve.wait_ge(rms_ready, 1)
            link(dve.reciprocal(st[:, 2, 0:NT], st[:, 1, 0:NT]))
            for t in range(NT):
                ts(xt_in[:, t, :], xt_in[:, t, :], st[:, 2, t:t + 1], None, ALU.mult).then_inc(xhat_ready, 1)

            def modulation(A, B, n_row, c_sh, c_sc):
                tt(B[:, :], bank(6)[:, 0:8], vT[:, c_sh:c_sh + 8], ALU.add)
                link(tt(A[:, :], bank(6)[:, 8:16], vT[:, c_sc:c_sc + 8], ALU.add))
                link(stt(out=A[:, :], in0=A[:, :], scalar=1.0, in1=vT[:, n_row:n_row + 8], op0=ALU.add, op1=ALU.mult))

            dve.wait_ge(pan_used, 4)
            modulation(A1, B1, V_N1, 0, 8)
            dve.engine_nop().then_inc(ab1_ready, 1)

            def group(name, i, j):
                g = GIDX[(name, i, j)]
                dve.wait_ge(ring_full, g + 1)
                return ring_bank(g)

            free = ring_free["dve"]
            for hf in range(2):
                for k in range(0, NK, 2):
                    ts(hT[:, k, hf * HALF:(hf + 1) * HALF], group("hT", k, hf), A1[:, k:k + 1], B1[:, k:k + 1],
                       ALU.mult, ALU.add).then_inc(free, 1)
            dve.wait_ge(ring_free["act"], nth[GIDX[("aux", NT - 1, 0)]])
            kraw, kc, ksq = aux[:, :, KV_R:KV_R + IX_D], kx2[:, :, 0:IX_D], kx2[:, :, IX_D:2 * IX_D]
            bc = lambda col, n: col.unsqueeze(2).to_broadcast([P, NT, n])
            link(dve.tensor_reduce(st[:, 0, 8:16], kraw, AX.X, ALU.add))
            link(ts(st[:, 0, 8:16], st[:, 0, 8:16], 1.0 / IX_D, None, ALU.mult))
            link(tt(kc, kraw, bc(st[:, 0, 8:16], IX_D), ALU.subtract))
            link(tt(ksq, kc, kc, ALU.mult))
            dve.tensor_reduce(st[:, 2, 8:16], ksq, AX.X, ALU.add).then_inc(stats_asked, 1)
            o = KV_R + IX_D
            v3 = lambda r: gates[:, r, :].rearrange("p (t h) -> p t h", t=NT)
            dve.tensor_copy(v3(8), aux[:, :, o + IX_H:o + IX_H + H])
            ts(v3(9), aux[:, :, o:o + IX_H], IX_SCALE, None, ALU.mult)
            dve.wait_ge(rows_in, 32)
            tt(v3(2), aux[:, :, o + IX_H + H:o + IX_H + 2 * H],
               rowc[:, H:2 * H].unsqueeze(1).to_broadcast([P, NT, H]), ALU.add).then_inc(gate_in, 1)
            dve.wait_ge(stats_rooted, 1)
            dve.reciprocal(st[:, 3, 16:24], st[:, 3, 8:16])
            link(dve.reciprocal(st[:, 2, 24:32], st[:, 2, 16:24]))
            link(tt(kc, kc, bc(st[:, 2, 24:32], IX_D), ALU.mult))
            dve.tensor_copy(ksq, kc)
            tt(aux[:, :, 0:KV_R], aux[:, :, 0:KV_R], bc(st[:, 3, 16:24], KV_R), ALU.mult).then_inc(kv_ready, 1)
            for k in range(2):
                for hf in range(2):
                    ts(ckvT[:, k, hf * HALF:(hf + 1) * HALF], group("ckvT", k, hf), vT[:, V_KVG + k:V_KVG + k + 1],
                       None, ALU.mult).then_inc(free, 1)
            for hf in range(2):
                ts(kixT[:, hf * HALF:(hf + 1) * HALF], group("kixT", 0, hf), vT[:, V_KG:V_KG + 1], vT[:, V_KB:V_KB + 1],
                   ALU.mult, ALU.add).then_inc(free, 1)
            for u in range(len(SEL_TILES) * H):
                t, h = SEL_TILES[u // H], u % H
                n = (t + 1) * P
                w = gates[:, 9, t * H + h:t * H + h + 1]
                dve.wait_ge(rel_ready, u + 1)
                if h:
                    dve.wait_ge(rel_used, u)
                    stt(out=score[t], in0=rel[u % 2][:, 0:n], scalar=w, in1=score[t], op0=ALU.mult, op1=ALU.add).then_inc(rel_used, 1)
                else:
                    ts(score[t], rel[u % 2][:, 0:n], w, None, ALU.mult).then_inc(rel_used, 1)
            dve.wait_ge(gate_act, 3)
            link(stt(out=gates[:, 1, :], in0=gates[:, 2, :], scalar=0.0, in1=gates[:, 5, :], op0=ALU.max, op1=ALU.add))
            link(ts(gates[:, 1, :], gates[:, 1, :], -1.0, None, ALU.mult))
            tt(v3(1), v3(1), rowc[:, 0:H].unsqueeze(1).to_broadcast([P, NT, H]), ALU.mult).then_inc(g_ready, 1)
            dve.wait_ge(gate_act, 4)
            NC = NT * H
            dve.tensor_copy(gates[:, 2, :], bank(7)[:, 0:NC])
            stt(out=gates[:, 7, :], in0=gates[:, 0, :], scalar=-1.0, in1=gates[:, 3, :], op0=ALU.mult, op1=ALU.mult).then_inc(gc_ready, 1)

            slots = conv_slots()

            def conv(ct):
                for hf in range(2):
                    dst = qkvT[:, ct, hf * HALF:(hf + 1) * HALF]
                    dve.wait_ge(ring_free["act"], nth[GIDX[("conv", ct, hf)]])
                    for j in range(CONV_K - 1):
                        col = V_ROWS + j * 12 + ct
                        ins = stt(out=dst, in0=pre[hf][:, j:j + HALF], scalar=vT[:, col:col + 1], in1=dst,
                                  op0=ALU.mult, op1=ALU.add)
                        if j < CONV_K - 2:
                            link(ins)
                    ins.then_inc(conv_ready, 1)

            for t in SEL_TILES:
                sc = score[t]
                link(dve.memset(sc[0:CHUNK, t * P + CHUNK:(t + 1) * P], NEG))
                for part in range(2):
                    for _ in range(ROUNDS // 2):
                        link(dve.max(m8[:, :], sc))
                        link(dve.match_replace(sc, m8[:, :], sc, TAKEN))
                    for ct in slots[(t, part)]:
                        conv(ct)
                link(ts(sc, sc, TAKEN_CUT, NEG, ALU.is_gt, ALU.mult))

            dve.wait_ge(ring_full, len(GROUPS))
            for t in range(2):
                dve.memset(bias01[t], 0.0)
            link(dve.memset(m8[:, :], 0.0))
            for t in range(2):
                link(dve.memset(bias01[t][0:CHUNK, t * P + CHUNK:(t + 1) * P], NEG))

            def pt_evac(u):
                for gi in pt_groups(u):
                    if gi % 2:
                        n = pt_cols(u, gi)
                        dve.wait_ge(s_pt_full, gi + 1)
                        if u >= 2:
                            dve.wait_ge(s_o_full, u - 1)
                        dve.tensor_copy(prT[u % 2][:, n], bank(1)[:, 0:n.stop - n.start]).then_inc(s_pt_dve, 1)

            for u in range(NT * H + 1):
                if u < NT * H:
                    t = u // H
                    n = (t + 1) * P
                    bias = score[t] if t in score else bias01[t]
                    dve.wait_ge(s_lg_full, u + 1)
                    if u >= 2:
                        dve.wait_ge(s_pt_full, pt_groups(u - 1)[0])
                    dve.tensor_tensor_reduce(lg[u % 2][:, 0:n], bank(4 + 2 * (u % 2), 2)[:, 0:n], bias, 1.0, TAKEN,
                                             ALU.add, ALU.max, st[:, 0, u:u + 1]).then_inc(s_lg_ready, 1)
                    dve.wait_ge(s_lg_ready, u + 1)
                    ts(st[:, 1, u:u + 1], st[:, 0, u:u + 1], -SM_SCALE, None, ALU.mult).then_inc(s_mx_ready, 1)
                if u:
                    pt_evac(u - 1)
                    if (u - 1) % H == H - 1:
                        t = (u - 1) // H
                        dve.wait_ge(s_o_full, H * (t + 1))
                        if t:
                            dve.wait_ge(s_oT_full, t)
                        link(dve.reciprocal(st[:, 3, t * H:(t + 1) * H], st[:, 2, t * H:(t + 1) * H]))
                        tt(heads(osa), heads(bank(2)), per_head(st[:, 3, t * H:(t + 1) * H]), ALU.mult).then_inc(s_osa_ready, 1)

            dve.wait_ge(s_dn_consts, 4)
            link(tt(xor, xi, ji, ALU.bitwise_xor))
            for l in range(6):
                link(ts(tmp_m, xor, float(1 << l), None, ALU.is_ge))
                link(stt(out=tmp_m, in0=xor, scalar=float(2 << l), in1=tmp_m, op0=ALU.is_lt, op1=ALU.mult))
                link(tt(lvl[l], tmp_m, gtm, ALU.mult))
            dve.wait_ge(s_nrm_ready, 1)
            link(dve.reciprocal(st[:, 1, :], st[:, 0, :]))
            r4 = lambda lo: st[:, 1, :].rearrange("p (t c) -> p t c", c=8)[:, :, lo:lo + 4]
            s4 = lambda i: st[:, i, 0:NC].rearrange("p (t h) -> p t h", t=NT)
            ts(s4(2), r4(0), DH ** -0.5, None, ALU.mult)
            link(dve.tensor_copy(s4(3), r4(4)))
            for t in range(NT):
                col = slice(t * H, (t + 1) * H)
                dve.wait_ge(s_qkv_full, 3 * t + 3)
                if t:
                    dve.wait_ge(s_pool_k, 2 * t)
                tt(heads(kn), heads(bank(1)), per_head(st[:, 3, col]), ALU.mult).then_inc(s_knqn_ready, 1)
                tt(heads(qn), heads(bank(0)), per_head(st[:, 2, col]), ALU.mult).then_inc(s_knqn_ready, 1)
                tt(heads(bv), heads(bank(2)), per_head(gates[:, 0, col]), ALU.mult)
                dve.wait_ge(s_knqn_ready, 2 * t + 2)
                dve.engine_nop().then_inc(s_kk_full, 1)
                tt(heads(kb), heads(kn), per_head(gates[:, 0, col]), ALU.mult).then_inc(s_kk_full, 1)
                dve.engine_nop().then_inc(s_kk_full, 1)
                tt(heads(qd), heads(qn), per_head(gates[:, 3, col]), ALU.mult).then_inc(s_kk_full, 1)
                dve.wait_ge(s_gb_full, t + 1)
                link(tt(heads(ET), heads(bank(7)), per_head(gates[:, 2, col]), ALU.subtract))
                ts(ET, ET, 0.0, None, ALU.min).then_inc(s_dd_ready, 1)
                dve.wait_ge(s_dd_exp, t + 1)
                link(tt(heads(ET), heads(ET), each_head(tri[:, :]), ALU.mult))
                dve.wait_ge(s_p_kk, 2 * t + 1)
                if t:
                    dve.wait_ge(s_ct_ready, 5 * t)
                tt(AT, bank(0), ET, ALU.mult).then_inc(s_at_ready, 1)
                dve.wait_ge(s_p_kk, 2 * t + 2)
                tt(QKT, bank(1), ET, ALU.mult).then_inc(s_at_ready, 1)
                dve.wait_ge(s_at_ready, 2 * t + 2)
                link(tt(heads(XT), heads(AT), each_head(lvl[0]), ALU.mult))
                tt(heads(XT), each_head(ident[:, :]), heads(XT), ALU.subtract).then_inc(s_xt1_ready, 1)
                dve.wait_ge(s_x1_ready, t + 1)
                for l in range(5):
                    dve.wait_ge(s_dx_full, 9 * t + 2 * l + (2 if l < 4 else 1))
                    tt(XT, XT, bank(4), ALU.subtract).then_inc(s_dx_ready, 1)
                    if l < 4:
                        tt(X, X, bank(5), ALU.subtract).then_inc(s_dx_ready, 1)
                    dve.wait_ge(s_dx_ready, 9 * t + 2 * l + (2 if l < 4 else 1))
                for cc in range(2):
                    dve.wait_ge(s_ods_full, 2 * t + cc + 1)
                    for h in range(H):
                        gcol = t * H + h
                        ins = stt(out=S_st[:, HSL(h)], in0=S_st[:, HSL(h)], scalar=gates[:, 5 + cc, gcol:gcol + 1],
                                  in1=bank(4 + cc)[:, HSL(h)], op0=ALU.mult, op1=ALU.add)
                    ins.then_inc(s_s_ready, 1)
                    dve.wait_ge(s_s_ready, 2 * t + cc + 1)
                dve.wait_ge(s_o_sq, t + 1)
                dve.tensor_reduce(st[:, 1, 32 + t * H:32 + (t + 1) * H], heads(osq), AX.X, ALU.add)
                tt(zg[:, t, :], bank(2), zg[:, t, :], ALU.mult).then_inc(s_oz_ready, 1)
            dve.wait_ge(s_orms_ready, 1)
            link(dve.reciprocal(st[:, 0, 0:NC], st[:, 1, 0:NC]))
            for t in range(NT):
                tt(heads(zg[:, t, :]), heads(zg[:, t, :]), per_head(st[:, 0, t * H:(t + 1) * H]), ALU.mult).then_inc(s_on_ready, 1)

            dve.wait_ge(s_ont_full, NT)
            dve.tensor_copy(condrep, cond[:, :].unsqueeze(2).to_broadcast([P, NK, P])).then_inc(s_gt1_full, 1)
            dve.wait_ge(s_x_load, 16 * (NT + 4))
            dve.wait_ge(pan_used, PAN["ada5"] + 1)
            tt(gt1[:, 0:HALF], gt1[:, 0:HALF], bank(4), ALU.add)
            link(tt(gt1[:, HALF:D], gt1[:, HALF:D], bank(5), ALU.add))
            dve.engine_nop().then_inc(s_gt1_ready, 1)
            dve.wait_ge(pan_used, PAN["ada9"] + 1)
            modulation(A2, B2, V_N2, 24, 32)
            dve.engine_nop().then_inc(s_ab2_ready, 1)
            dve.wait_ge(pan_used, PAN["ada11"] + 1)
            tt(gt2[:, 0:HALF], gt2[:, 0:HALF], bank(4), ALU.add)
            tt(gt2[:, HALF:D], gt2[:, HALF:D], bank(5), ALU.add).then_inc(s_gt2_ready, 1)
            for gi in range(2 * NT):
                n, t = gi // NT, gi % NT
                N = slice(n * HALF, (n + 1) * HALF)
                dve.wait_ge(s_y1_full, gi + 1)
                tt(ytmp[gi % 2], bank(gi % 4), gt1[:, N], ALU.mult).then_inc(s_y1_read, 1)
                dve.wait_ge(s_y1_read, 2 * gi + 1)
                tt(x2[:, t, N], x2[:, t, N], ytmp[gi % 2], ALU.add).then_inc(s_y1_read, 1)
            for t in range(NT):
                dve.wait_ge(s_rms2_ready, t + 1)
                link(dve.reciprocal(st[:, 2, t:t + 1], st[:, 1, t:t + 1]))
                ts(xh2[:, t, :], x2[:, t, :], st[:, 2, t:t + 1], None, ALU.mult).then_inc(s_xh2_ready, 1)
            for m in range(1, 16, 2):
                hf, k = m // 8, m % 8
                dve.wait_ge(s_h2_full, m + 1)
                ts(h2T[:, k, hf * HALF:(hf + 1) * HALF], bank(4 + m % 4), A2[:, k:k + 1], B2[:, k:k + 1],
                   ALU.mult, ALU.add).then_inc(s_h2_dve, 1)
            te = lambda a: a.rearrange("p (t e) -> p t e", t=NT)
            dve.wait_ge(s_rsc_ready, 1)
            dve.wait_ge(s_small_done, 4)
            link(tt(te(r_ch), te(r_sc), rb[:, :].unsqueeze(1).to_broadcast([P, NT, NE]), ALU.add))
            for i in range(NT * NG):
                ins = dve.max(r_eq[:, 8 * i:8 * i + 8], r_ch[:, 8 * i:8 * i + 8])
            link(ins)
            top = r_eq.rearrange("p (n k) -> p n k", k=8)
            gs, rank = gsm[:, 0, :], gsm[:, 1, :]
            link(tt(gs.unsqueeze(2), top[:, :, 0:1], top[:, :, 1:2], ALU.add))
            g3 = gs.rearrange("p (t g) -> p t g", t=NT)
            other, own = g3.unsqueeze(2).to_broadcast([P, NT, NG, NG]), g3.unsqueeze(3).to_broadcast([P, NT, NG, NG])
            c4 = lambda a: a.rearrange("p (t g q) -> p t g q", t=NT, g=NG)
            tt(c4(r_gt), other, own, ALU.is_gt)
            link(tt(c4(r_eq), other, own, ALU.is_equal))
            link(tt(c4(r_eq), c4(r_eq), lowm[:, :, :].unsqueeze(1).to_broadcast([P, NT, NG, NG]), ALU.mult))
            link(tt(r_gt, r_gt, r_eq, ALU.add))
            link(dve.tensor_reduce(rank, r_gt.rearrange("p (n q) -> p n q", q=NG), AX.X, ALU.add))
            link(ts(rank, rank, float(TOP_G), NEG, ALU.is_ge, ALU.mult))
            n8 = lambda a: a.rearrange("p (n q) -> p n q", q=8)
            link(tt(n8(r_ch), n8(r_ch), rank.unsqueeze(2).to_broadcast([P, NT * NG, 8]), ALU.add))
            E = lambda a, t: a[:, t * NE:(t + 1) * NE]
            for t in range(NT):
                link(dve.max(m8[:, :], E(r_ch, t)))
                link(dve.match_replace(E(r_v, t), m8[:, :], E(r_ch, t), TAKEN))
            ts(r_mk, r_v, TAKEN_CUT, None, ALU.is_lt).then_inc(s_mask_ready, 1)
            dve.wait_ge(s_mask_ready, 1)
            link(tt(r_gt, r_sc, r_mk, ALU.mult))
            link(dve.tensor_reduce(gsm[:, 0, 0:NT], te(r_gt), AX.X, ALU.add))
            link(dve.reciprocal(gsm[:, 0, 8:8 + NT], gsm[:, 0, 0:NT]))
            link(ts(gsm[:, 0, 8:8 + NT], gsm[:, 0, 8:8 + NT], ROUTED, None, ALU.mult))
            link(tt(te(r_gt), te(r_gt), gsm[:, 0, 8:8 + NT].unsqueeze(2).to_broadcast([P, NT, NE]), ALU.mult))
            dve.wait_ge(s_pos_full, 1)
            link(tt(te(r_v), te(bank(1)), erow[:, :].unsqueeze(1).to_broadcast([P, NT, NE]), ALU.add))
            link(tt(r_v, r_v, r_mk, ALU.mult))
            link(ts(cni, bank(2)[:, 0:NE], float(P - 1), None, ALU.add))
            link(ts(cni, cni, 7, None, ALU.arith_shift_right))
            link(ts(nbf, cni, 1.0, None, ALU.max))
            dve.tensor_copy(ints[0:1, 0:NE], nbf[0:1, :]).then_inc(s_nbr_ready, 1)
            for t in range(NT):
                ins = dve.max(d8[:, t * 8:t * 8 + 8], E(r_v, t))
            link(ins)
            link(ts(di[0][:, :], d8[:, :], -1.0, None, ALU.add))
            ts(di[1][:, :], di[0][:, :], 7, None, ALU.arith_shift_right)
            link(ts(di[0][:, :], di[0][:, :], P - 1, 9, ALU.bitwise_and, ALU.logical_shift_left))
            link(tt(dest_i[:, :], di[0][:, :], di[1][:, :], ALU.bitwise_or))
            payf = pay.bitcast(F32).rearrange("p (t k two) -> p t k two", t=NT, two=2)
            ke = lambda a: a.rearrange("p (k e) -> p k e", e=NE)
            for t in range(NT):
                link(tt(ke(r_eq), E(r_v, t).unsqueeze(1).to_broadcast([P, 8, NE]),
                        d8[:, t * 8:t * 8 + 8].unsqueeze(2).to_broadcast([P, 8, NE]), ALU.is_equal))
                link(tt(ke(r_eq), ke(r_eq), E(r_gt, t).unsqueeze(1).to_broadcast([P, 8, NE]), ALU.mult))
                dve.tensor_reduce(payf[:, t, :, 1:2], ke(r_eq), AX.X, ALU.add).then_inc(s_lists_ready, 1)
                dve.wait_ge(s_lists_ready, t + 1)
            dve.wait_ge(s_nbt_full, 1)
            dve.tensor_copy(nbc, bank(3)[0:NE, 0:P]).then_inc(s_nbt_ready, 1)
            dve.wait_ge(s_bs_full, 1)
            dve.tensor_copy(ints[0:1, NE:2 * NE], bank(3)[0:1, P:P + NE])
            tt(ints[0:1, 2 * NE:2 * NE + 1], bank(3)[0:1, P + NE - 1:P + NE], nbf[0:1, NE - 1:NE], ALU.add).then_inc(s_cnt_ready, 1)
            dve.wait_ge(s_cnt_ready, 1)

            tf = tbl.bitcast(F32)

            def x_evac():
                for k in range(4, NK):
                    ins = ts(xTm[:, k * P:(k + 1) * P], bank(0, 2)[:, k * P:(k + 1) * P], A2[:, k:k + 1], B2[:, k:k + 1],
                             ALU.mult, ALU.add)
                ins.then_inc(s_xT_dve, 1)

            dve.wait_ge(s_tbl_in, 16)
            for done in acc_out:
                dve.wait_ge(done, 8 * NT)
            dve.wait_ge(s_xg_read, 2)
            x_evac()
            dve.engine_nop().then_inc(s_y_dve, 2)
            with dve.Fori(0, NE) as e:
                nb = dve.value_load(ints[0:1, bass.ds(e, 1)], min_val=1, max_val=CAP)
                b0 = dve.value_load(ints[0:1, bass.ds(e + NE, 1)], min_val=0, max_val=NE * CAP)
                with dve.Fori(0, nb) as b:
                    g = dve.snap(b0 + b)
                    dve.wait_ge(s_silu_done, g + 1)
                    tt(hm, sg, bank(2)[:, FE:2 * FE], ALU.mult).then_inc(s_hm_ready, 1)
                    dve.wait_ge(s_xg_read, g + 3)
                    x_evac()
                    dve.wait_ge(s_scattered, 16 * g + 48)
                    dve.wait_ge(s_y_full, 2 * g + 2)
                    ts(ysb[:, HALF:D], bank(5), tf[:, bass.ds((e * CAP + b) * 2 + 1, 1)], None, ALU.mult).then_inc(s_y_dve, 1)

            def finish(t):
                dst = xg if t % 2 == 0 else xTm
                dve.wait_ge(s_rms3_ready, t + 1)
                link(dve.reciprocal(st[:, 2, t:t + 1], st[:, 1, t:t + 1]))
                if t >= 2:
                    dve.wait_ge(out_done[t % 2], 16 * (t // 2))
                stt(out=dst, in0=x3[:, t, :], scalar=st[:, 2, t:t + 1], in1=fg, op0=ALU.mult, op1=ALU.mult).then_inc(s_o_ready, 1)

            dve.wait_ge(s_acc_in, 16 * NT)
            for t in range(NT):
                link(tt(x3[:, t, :], x3[:, t, :], gt2, ALU.mult))
                tt(x3[:, t, :], x3[:, t, :], x2[:, t, :], ALU.add).then_inc(s_x3_ready, 1)
                if t:
                    finish(t - 1)
            finish(NT - 1)


_INS = ["x", "c", "ada_w", "ada_b", "norm1_g", "w_in", "conv_w", "a_log", "dt_bias", "dn_norm_g", "kv_norm_g", "w_uk",
        "w_uv", "idx_k_ln_g", "idx_k_ln_b", "w_out", "norm2_g", "router_w", "router_b", "exp_w_gate", "exp_w_up",
        "exp_w_down", "sh_w_gate", "sh_w_up", "sh_w_down", "final_g"]
_OUTS = [((1, T, D), "float32")]


def kernel(**inputs):
    import numpy as _np
    import concourse.bacc as _bacc
    from concourse import mybir as _mybir
    from concourse.bass_utils import run_bass_kernel_spmd as _run

    nc = _bacc.Bacc("TRN2", target_bir_lowering=False, num_devices=1)
    arrays, args = {}, []
    for name in _INS:
        a = _np.ascontiguousarray(inputs[name])
        arrays[f"in_{name}_dram"] = a
        args.append(nc.dram_tensor(f"in_{name}_dram", a.shape, _mybir.dt.from_np(a.dtype), kind="ExternalInput").ap())
    for i, (shape, dtype) in enumerate(_OUTS):
        dt = _mybir.dt.from_np(_np.dtype(dtype))
        args.append(nc.dram_tensor(f"out_{i}_dram", shape, dt, kind="ExternalOutput").ap())
    build(nc, *args)
    r = _run(nc, [arrays], core_ids=[0])
    got = tuple(r.results[0][f"out_{i}_dram"] for i in range(len(_OUTS)))
    return got[0]
```

```python
from contextlib import ExitStack

import concourse.bass as bass
import numpy as np
from concourse import mybir

F32, F32R, I32 = mybir.dt.float32, mybir.dt.float32r, mybir.dt.int32
ALU, ACT = mybir.AluOpType, mybir.ActivationFunctionType
AX = mybir.AxisListType

P = 128
D, T = 1024, 1024
NT, NK = T // P, D // P
HALF = 512
EPS = 1e-6
H, DH = 4, 128
CONV_K, CHUNK = 4, 64
KV_R, IX_H, IX_D, TOPK = 256, 4, 64, 256
SM_SCALE, IX_SCALE = DH ** -0.5, (IX_H * IX_D) ** -0.5
NE, NG, TOP_G, TOP_E, FE = 64, 8, 4, 8, 256
ROUTED = 2.5
CAP = T // P
NEG, TAKEN, TAKEN_CUT = -1e30, -3e38, -2e38
C_Q, C_K, C_V, C_Z, C_BA, C_QSA, C_CKV, C_QIX, C_KIX = 0, 512, 1024, 1536, 2048, 2056, 2568, 2824, 3080
AUX = KV_R + IX_D + IX_H + 2 * H
V_ADAB, V_N1, V_N2, V_C, V_KVG, V_KG, V_KB, V_DG, V_ROWS = 0, 48, 56, 64, 72, 74, 75, 76, 77
SEL_TILES = range(TOPK // P, NT)
ROUNDS = TOPK // 8


SPLIT = {"before conv": [106] + [4] * 11, "first": 2, "gates": 1, "w": 1, "state": 1}


SLOTS_AFTER = [0, 0, 12, 13, 13, 13, 13, 0]
assert sum(SLOTS_AFTER) == NT * TOP_E


def build(nc, x, c, ada_w, ada_b, norm1_g, w_in, conv_w, a_log, dt_bias, dn_norm_g, kv_norm_g, w_uk, w_uv,
          idx_k_ln_g, idx_k_ln_b, w_out, norm2_g, router_w, router_b, exp_w_gate, exp_w_up, exp_w_down,
          sh_w_gate, sh_w_up, sh_w_down, final_g, out):
    ctx = ExitStack()
    with ctx:
        def sb(name, shape, dt=F32):
            return ctx.enter_context(nc.sbuf_tensor(name, shape, dt))

        def sem(name):
            return ctx.enter_context(nc.semaphore(name))

        xn_dram = nc.dram_tensor("xn_tokens", (T + P, D), F32).ap()
        acc_dram = nc.dram_tensor("moe_sum", (T + P, D), F32).ap()
        table_dram = nc.dram_tensor("dispatch", (P * NE * CAP, 2), I32).ap()

        KB = 256
        AREA = 193 * KB + 2 * (HALF + 3)
        with nc.sbuf_tensor("arena", [P, AREA], F32) as arena:
            pass
        reached = [0]

        def at(kb, words):
            return arena[:, int(kb * KB):int(kb * KB) + words]

        def over(name, kb, words, dt):
            if int(kb * KB) > reached[0]:
                sb(f"below_{name}", [P, int(kb * KB) - reached[0]])
            reached[0] = int(kb * KB) + words
            return sb(name, [P, words], dt)[:, :]

        wh0 = over("wh0", 0, 6144, F32R)
        w_down0 = over("w_down0", 24, 2048, F32)
        wl0, wl1 = over("wl0", 32, 6144, F32R), over("wl1", 56, 6144, F32R)
        xTm = over("xT", 84, D, F32)
        hTh, hTl = over("hT_high", 94, FE, F32R), over("hT_low", 95, FE, F32R)
        w_up = over("w_up", 132, 2048, F32)
        xh = over("xT_high", 140, D, F32R)
        w_down1 = over("w_down1", 152, 2048, F32)
        wh1 = over("wh1", 161, 6144, F32R)
        w_gate = over("w_gate", 185, 2048, F32)
        xl = [over(f"xT_low{i}", 193 + 2 * i, HALF, F32R) for i in range(2)]
        sb("above", [P, AREA - reached[0]])
        wh, wl, w_down = (wh0, wh1), (wl0, wl1), (w_down0, w_down1)

        hT = at(0, NK * T).rearrange("p (k t) -> p k t", k=NK)
        R_QKV, R_QSA, R_KV, R_Z, R_SC, R_PAN = 32, 80, 96, 128, 144, 161
        qkvT = at(R_QKV, 12 * T).rearrange("p (c t) -> p c t", c=12)
        qsaT = at(R_QSA, H * T).rearrange("p (h t) -> p h t", h=H)
        xt_in = at(R_KV, NT * D).rearrange("p (t d) -> p t d", t=NT)
        khT = at(R_KV, H * T).rearrange("p (h t) -> p h t", h=H)
        vh = at(R_KV + 16, NT * H * DH).rearrange("p (t n) -> p t n", t=NT)
        zg = at(R_Z, NT * H * DH).rearrange("p (t n) -> p t n", t=NT)
        score = {}
        off = R_SC
        for t in SEL_TILES:
            score[t] = at(off, (t + 1) * P)
            off += (t + 1) / 2
        assert off <= R_PAN
        panel = [at(R_PAN + 16 * i, NK * HALF) for i in range(2)]
        square = [at(R_PAN + 16 + 4 * i, T) for i in range(4)]
        qixT = at(R_QKV, 2 * T).rearrange("p (c t) -> p c t", c=2)
        kixT = at(R_QKV + 8, T)
        rel = [at(R_QKV + 12 + 4 * i, T) for i in range(2)]
        ckvT = at(R_QKV + 20, 2 * T).rearrange("p (k t) -> p k t", k=2)
        kx2 = at(R_QKV + 28, NT * 2 * IX_D).rearrange("p (t n) -> p t n", t=NT)
        aux = at(R_QKV + 32, NT * AUX).rearrange("p (t n) -> p t n", t=NT)
        wuk = at(R_QSA, H * 2 * DH).rearrange("p (h k n) -> p h k n", h=H, k=2)
        wuv = at(R_QSA + 4, 2 * H * DH).rearrange("p (k h n) -> p k h n", h=H, k=2)
        sqx = at(R_QSA + 8, D)
        lg = [at(4 * i, T) for i in range(2)]
        prT = [at(8 + 4 * i, T) for i in range(2)]
        osa = at(16, H * DH)

        def dn(i):
            return at(2 * i, HALF)
        (kn, qn, bv, kb, kbe, kd, qd, knT, kbT, qnT, qdT, gbt, ET, AT, QKT) = [dn(i) for i in range(15)]
        CT = at(R_PAN, 5 * HALF).rearrange("p (l n) -> p l n", l=5)
        X, XT, P1 = at(R_PAN + 10, HALF), at(R_PAN + 12, HALF), at(R_PAN + 14, HALF)
        wT = at(30, HALF)
        R_DM = R_PAN + 16
        S_st = at(R_DM, HALF)
        vn = at(R_DM + 2, HALF)
        osq = at(R_DM + 4, HALF)
        xi = at(R_DM + 6, P).bitcast(I32)
        ji = at(R_DM + 6.5, P).bitcast(I32)
        xor = at(R_DM + 7, P).bitcast(I32)
        gtm = at(R_DM + 7.5, P)
        lvl = [at(R_DM + 8 + 0.5 * i, P) for i in range(6)]
        tmp_m = at(R_DM + 11, P)
        x2 = at(R_KV, NT * D).rearrange("p (t d) -> p t d", t=NT)
        h2T = hT
        ab_rep = at(40, 2 * D).rearrange("p (i k n) -> p i k n", i=2, k=NK)
        A2_row, B2_row = at(32, D), at(36, D)
        xh2 = at(48, NT * D).rearrange("p (t d) -> p t d", t=NT)
        pre = [at(193 + i * (HALF + 3) / KB, HALF + 3) for i in range(2)]
        xg, ysb = at(80, D), at(88, D)
        sg, hm, hmT, upb = (at(92 + i, FE) for i in range(4))
        tbl = at(128, NE * CAP * 2).bitcast(I32)
        condrep = at(132, NK * P).rearrange("p (k n) -> p k n", k=NK)
        ytmp = [at(136 + 2 * i, HALF) for i in range(2)]
        junk = at(140, D)
        mod_r = at(136, 4 * HALF)
        r_sc, r_ch, r_mk, r_gt, r_v, r_eq = (at(132 + 2 * i, NT * NE) for i in range(6))
        gt2, fg, gt1, ysh0 = (at(144 + 4 * i, D) for i in range(4))
        ysh = [ysh0, xTm]
        x3 = at(0, NT * D).rearrange("p (t d) -> p t d", t=NT)

        ident = sb("ident", [P, P])
        ones = sb("ones", [P, P])
        tri = sb("tri", [P, P])
        after = sb("after", [P, P])
        before = sb("before", [P, P])
        half = sb("half", [P, 2, P])
        vecs = sb("vecs", [V_ROWS, P])
        cwr = sb("cwr", [48, P])
        vT = sb("vT", [P, V_ROWS + 48])
        cond = sb("cond", [P, NK])
        A1, B1, A2, B2 = (sb(n, [P, NK]) for n in ("A1", "B1", "A2", "B2"))
        epsc = sb("epsc", [P, 4])
        st = sb("st", [P, 4, NT * H * 2])
        gates = sb("gates", [P, 10, NT * H])
        rowc = sb("rowc", [P, 2 * H])
        ints = sb("ints", [1, 2 * NE + 1], I32)
        m8 = sb("m8", [P, 8])
        lowm = sb("lowm", [P, NG, NG])
        rb = sb("rb", [P, NE])
        erow = sb("erow", [P, NE])
        pay = pre[0][:, 0:128].bitcast(I32)
        d8 = pre[0][:, 128:192]
        di = [pre[0][:, 192 + 64 * i:256 + 64 * i].bitcast(I32) for i in range(2)]
        dest_i = pre[0][:, 320:384].bitcast(I32)
        gsm = pre[1][:, 0:128].rearrange("p (a n) -> p a n", a=2)
        cni = pre[1][:, 128:192].bitcast(I32)
        nbf = pre[1][:, 192:256]
        nbc = pre[1][0:NE, 256:384]
        idx_now, idx_last, idx_hold, idx_out, idx_zero = (sb(n, [P, 1], I32) for n in (
            "idx_now", "idx_last", "idx_hold", "idx_out", "idx_zero"))

        psum = ctx.enter_context(nc.psum_tensor("psum", [P, 8 * HALF], F32))

        def bank(b, n=1):
            return psum[:, b * HALF:(b + n) * HALF]

        def heads(ap):
            return ap.rearrange("p (h n) -> p h n", h=H)

        def per_head(col):
            return col.unsqueeze(2).to_broadcast([P, H, DH])

        def each_head(mask):
            return mask.unsqueeze(1).to_broadcast([P, H, P])

        w_in_k = w_in.rearrange("o (k p) n -> p (o k) n", p=P)
        ada_k = ada_w.rearrange("o (k p) n -> p (o k) n", p=P)
        w_out_k = w_out.rearrange("o (k p) n -> p (o k) n", p=P)
        rw_k = router_w.rearrange("o (k p) n -> p (o k) n", p=P)
        sg_k = sh_w_gate.rearrange("o (k p) n -> p (o k) n", p=P)
        su_k = sh_w_up.rearrange("o (k p) n -> p (o k) n", p=P)
        sd_k = sh_w_down.rearrange("o (k p) n -> p (o k) n", p=P)
        PANELS = [(f"ada{i}", HALF, [(ada_k, i * HALF, HALF, 0)]) for i in (0, 1, 2, 3)]
        PANELS += [("aux", AUX, [(w_in_k, C_CKV, KV_R, 0), (w_in_k, C_KIX, IX_D + IX_H, KV_R),
                                 (w_in_k, C_BA, 2 * H, KV_R + IX_D + IX_H)]),
                   ("qix", KV_R, [(w_in_k, C_QIX, IX_H * IX_D, 0)]),
                   ("qsa", HALF, [(w_in_k, C_QSA, HALF, 0)]),
                   ("z", HALF, [(w_in_k, C_Z, HALF, 0)])]
        PANELS += [(n, HALF, [(w_in_k, o, HALF, 0)]) for n, o in (("q", C_Q), ("k", C_K), ("v", C_V))]
        PANELS += [(f"ada{i}", HALF, [(ada_k, i * HALF, HALF, 0)]) for i in (4, 5, 6, 7, 8, 9, 10, 11)]
        PANELS += [(f"wo{i}", HALF, [(w_out_k, i * HALF, HALF, 0)]) for i in range(2)]
        PANELS += [("router", NE, [(rw_k, 0, NE, 0)]),
                   ("sgu", HALF, [(sg_k, 0, FE, 0), (su_k, 0, FE, FE)]), ("sd", D, [(sd_k, 0, D, 0)])]
        NBUF = len(panel)
        PAN = {n: i for i, (n, _, _) in enumerate(PANELS)}
        landed, count = [], [0] * NBUF
        for i, (_, _, parts) in enumerate(PANELS):
            count[i % NBUF] += 16 * len(parts)
            landed.append(count[i % NBUF])

        def pan(name):
            i = PAN[name]
            cols = PANELS[i][1]
            k = 2 if name == "sd" else NK
            return panel[i % NBUF][:, 0:k * cols].rearrange("p (k n) -> p k n", k=k)

        GROUPS = [("hT", k, hf, "act" if k % 2 else "dve") for hf in range(2) for k in range(NK)]
        GROUPS += [("aux", t, 0, "act") for t in range(NT)]
        GROUPS += [("qix", ct, hf, "act") for ct in range(2) for hf in range(2)]
        GROUPS += [("ckvT", k, hf, "dve") for k in range(2) for hf in range(2)]
        GROUPS += [("kixT", 0, hf, "dve") for hf in range(2)]
        GROUPS += [("kh", h, hf, "act") for h in range(H) for hf in range(2)]
        GROUPS += [("vh", t, 0, "act") for t in range(NT)]
        GROUPS += [("qsa", h, hf, "act") for h in range(H) for hf in range(2)]
        GROUPS += [("z", t, 0, "act") for t in range(NT)]
        GROUPS += [("conv", ct, hf, "act") for ct in range(12) for hf in range(2)]
        GIDX = {g[:3]: i for i, g in enumerate(GROUPS)}
        nth, n_of = [], {"act": 0, "dve": 0}
        for g in GROUPS:
            n_of[g[3]] += 1
            nth.append(n_of[g[3]])
        RING = 4

        consts_ready = sem("consts_ready")
        vecs_in, rows_in, x_in, w_small = sem("vecs_in"), sem("rows_in"), sem("x_in"), sem("w_small")
        pan_in = [sem(f"pan_in{i}") for i in range(NBUF)]
        pan_used = sem("pan_used")
        vecs_turned, vT_ready, cond_ready = sem("vecs_turned"), sem("vT_ready"), sem("cond_ready")
        mod_row, mod_full, ab1_ready = sem("mod_row"), sem("mod_full"), sem("ab1_ready")
        ssq_ready, rms_ready, rstd_ready, xhat_ready = sem("ssq_ready"), sem("rms_ready"), sem("rstd_ready"), sem("xhat_ready")
        ring_full = sem("ring_full")
        ring_free = {"act": sem("ring_free_act"), "dve": sem("ring_free_dve")}
        dv, av = sem("dv"), sem("av")
        stats_asked, stats_rooted, kv_ready = sem("stats_asked"), sem("stats_rooted"), sem("kv_ready")
        ixs_full, rel_ready, rel_used = sem("ixs_full"), sem("rel_ready"), sem("rel_used")
        gate_in, gate_act, g_ready, gc_full, gc_ready = sem("gate_in"), sem("gate_act"), sem("g_ready"), sem("gc_full"), sem("gc_ready")
        pre_ready, conv_ready, conv_act, sq_ready, nrm_full = sem("pre_ready"), sem("conv_ready"), sem("conv_act"), sem("sq_ready"), sem("nrm_full")

        def ring_wait(pe, g):
            if g >= RING:
                pe.wait_ge(ring_free[GROUPS[g - RING][3]], nth[g - RING])

        def ring_bank(g):
            return bank(g % RING)

        s_lg_full, s_lg_ready, s_mx_ready, s_pr_ready, s_pt_full = (sem(n) for n in ("lg_full", "lg_ready", "mx_ready", "pr_ready", "pt_full"))
        s_pt_act, s_pt_dve, s_o_full, s_osa_ready, s_oT_full = (sem(n) for n in ("pt_act", "pt_dve", "o_full", "osa_ready", "oT_full"))
        s_sa_ready, s_dn_consts, s_qkv_full, s_nrm_ready, s_knqn_ready = (sem(n) for n in ("sa_ready", "dn_consts", "qkv_full", "nrm_ready", "knqn_ready"))
        s_pool_k, s_t_full, s_t_act, s_gb_ready, s_gb_full = (sem(n) for n in ("pool_k", "t_full", "t_act", "gb_ready", "gb_full"))
        s_dd_ready, s_dd_exp, s_kk_full, s_at_ready, s_ct_ready = (sem(n) for n in ("dd_ready", "dd_exp", "kk_full", "at_ready", "ct_ready"))
        s_xt1_ready, s_x1_full, s_x1_ready, s_p1_full, s_p1_ready = (sem(n) for n in ("xt1_ready", "x1_full", "x1_ready", "p1_full", "p1_ready"))
        s_dx_full, s_dx_ready, s_w_full, s_w_ready, s_vn_full = (sem(n) for n in ("dx_full", "dx_ready", "w_full", "w_ready", "vn_full"))
        s_vn_ready, s_ods_full, s_s_ready, s_o_sq, s_oz_ready = (sem(n) for n in ("vn_ready", "ods_full", "s_ready", "o_sq", "oz_ready"))
        s_orms_ready, s_on_ready, s_ont_full, s_dnT_ready, s_x_load = (sem(n) for n in ("orms_ready", "on_ready", "ont_full", "dnT_ready", "x_load"))
        s_gt1_full, s_gt1_ready, s_gt2_ready, s_ab2_ready, s_y1_full = (sem(n) for n in ("gt1_full", "gt1_ready", "gt2_ready", "ab2_ready", "y1_full"))
        s_y1_read, s_ssq2_ready, s_rms2_ready, s_xh2_ready, s_xn_out = (sem(n) for n in ("y1_read", "ssq2_ready", "rms2_ready", "xh2_ready", "xn_out"))
        s_h2_full, s_h2_act, s_h2_dve, s_rl_full, s_rsc_ready = (sem(n) for n in ("h2_full", "h2_act", "h2_dve", "rl_full", "rsc_ready"))
        s_mask_ready, s_pos_full, s_nbr_ready, s_nbt_full, s_nbt_ready = (sem(n) for n in ("mask_ready", "pos_full", "nbr_ready", "nbt_full", "nbt_ready"))
        s_lists_ready, s_tbl_init, s_filler_out, s_tbl_in = (sem(n) for n in ("lists_ready", "tbl_init", "filler_out", "tbl_in"))
        s_slots_out, s_sgu_full, s_ssg_ready, s_shm_ready, s_shT_full = (sem(n) for n in ("slots_out", "sgu_full", "ssg_ready", "shm_ready", "shT_full"))
        s_shT_ready, s_sy_full, s_sy_act, s_acc_out0, s_acc_out1 = (sem(n) for n in ("shT_ready", "sy_full", "sy_act", "acc_out0", "acc_out1"))
        s_w_in, s_shared_done, s_idx_g, s_idx_s = (sem(n) for n in ("w_in", "shared_done", "idx_g", "idx_s"))
        s_wh_ready, s_split_gu, s_split_d, s_x2_in, s_ab_rows, s_hl_ready, s_h2_rows = (sem(n) for n in (
            "wh_ready", "split_gu", "split_d", "x2_in", "ab_rows", "hl_ready", "h2_rows"))
        s_paced, s_gathered, s_xg_read, s_xT_act, s_xT_dve = (sem(n) for n in ("paced", "gathered", "xg_read", "xT_act", "xT_dve"))
        s_gu_full, s_silu_done, s_hm_ready, s_hT_full, s_hT_ready = (sem(n) for n in ("gu_full", "silu_done", "hm_ready", "hT_full", "hT_ready"))
        s_y_full, s_y_ready, s_scattered, s_gated = (sem(n) for n in ("y_full", "y_ready", "scattered", "gated"))
        acc_in = [sem(f"acc_in{i}") for i in range(2)]
        s_x3_ready, s_ssq3_ready, s_rms3_ready, s_o_ready = (sem(n) for n in ("x3_ready", "ssq3_ready", "rms3_ready", "o_ready"))
        s_small_done, s_cnt_ready, s_ab_full = (sem(n) for n in ("small_done", "cnt_ready", "ab_full"))
        s_p_kk,  = (sem(n) for n in ("p_kk",))
        s_wd_in = [sem(f"wd_in{i}") for i in range(2)]
        acc_out = out_done = (s_acc_out0, s_acc_out1)
        OUT0 = 8 * NT

        def gate_up_parts():
            parts = []
            for i, w in enumerate((w_gate, w_up)):
                for k in (0, 4):
                    where = lambda slot, i=i, k=k: slot[:, 0:4096].rearrange("p (k n) -> p k n", k=NK)[:, k:k + 4, i * FE:(i + 1) * FE]
                    parts.append((w.rearrange("p (k n) -> p k n", k=NK)[:, k:k + 4, :], where))
            return parts

        def down_parts(i):
            return [(w_down[i][:, k * D:(k + 1) * D], lambda slot, k=k: slot[:, 4096 + k * D:4096 + (k + 1) * D]) for k in range(2)]

        GU_PARTS, D_PARTS = gate_up_parts(), [down_parts(i) for i in range(2)]
        PARTS = len(GU_PARTS) + len(D_PARTS[0])
        block = ctx.enter_context(nc.Block())
        TILE = lambda t: slice(t * P, (t + 1) * P)
        HSL = lambda h: slice(h * DH, (h + 1) * DH)
        PAIR = lambda pr: slice(pr * 2 * DH, (pr + 1) * 2 * DH)
        B_P1, B_XT, B_X = (3, 2), (4, 0), (5, 1)

        def pt_groups(u):
            before_ = sum((v // H + 4) // 4 for v in range(u))
            return list(range(before_, before_ + (u // H + 4) // 4))

        def pt_cols(u, gi):
            c0 = (gi - pt_groups(u)[0]) * HALF
            return slice(c0, min(c0 + HALF, (u // H + 1) * P))

        bias01 = [at(18, P), at(18.5, 2 * P)]

        def sa_evac(act, t):
            act.wait_ge(s_oT_full, t + 1)
            act.activation(qsaT[:, :, TILE(t)], heads(bank(3)), ACT.Copy).then_inc(s_sa_ready, 1)

        @block.sync
        def _(sp):
            sp.dma_start(vecs[V_C:V_C + 8, :], c.rearrange("o (k p) -> (o k) p", p=P)).then_inc(vecs_in, 16)
            sp.dma_start(vecs[V_ADAB:48, :], ada_b.rearrange("o (k p) -> (o k) p", p=P)).then_inc(vecs_in, 16)
            sp.dma_start(vecs[V_N1:V_N1 + 8, :], norm1_g.rearrange("o (k p) -> (o k) p", p=P)).then_inc(vecs_in, 16)
            sp.dma_start(vecs[V_N2:V_N2 + 8, :], norm2_g.rearrange("o (k p) -> (o k) p", p=P)).then_inc(vecs_in, 16)
            sp.dma_start(vecs[V_KVG:V_KVG + 2, :], kv_norm_g.rearrange("o (k p) -> (o k) p", p=P)).then_inc(vecs_in, 16)
            for i in range(2):
                sp.dma_start(vecs[V_KG:V_KG + 1, i * IX_D:(i + 1) * IX_D], idx_k_ln_g).then_inc(vecs_in, 16)
                sp.dma_start(vecs[V_KB:V_KB + 1, i * IX_D:(i + 1) * IX_D], idx_k_ln_b).then_inc(vecs_in, 16)
            sp.dma_start(vecs[V_DG:V_DG + 1, :], dn_norm_g).then_inc(vecs_in, 16)
            sp.dma_start(cwr[:, :], conv_w.rearrange("o j (c p) -> (o j c) p", p=P)).then_inc(vecs_in, 16)
            for i, (name, cols, parts) in enumerate(PANELS):
                if name == "ada2":
                    for t in range(NT):
                        sp.dma_start(xt_in[:, t, :], x[0, TILE(t), :]).then_inc(x_in, 16)
                if name == "qix":
                    sp.dma_start(wuk, w_uk.rearrange("o h (k p) n -> p (o h) k n", p=P)).then_inc(w_small, 16)
                    for k in range(2):
                        sp.dma_start(wuv[:, k], w_uv[0, :, k * P:(k + 1) * P, :].rearrange("h p n -> p h n")).then_inc(w_small, 16)
                if name == "ada4":
                    sp.wait_ge(s_oz_ready, NT)
                    sp.wait_ge(s_s_ready, 2 * NT)
                if name == "wo0":
                    for t in range(NT):
                        sp.dma_start(x2[:, t, :], x[0, TILE(t), :]).then_inc(s_x2_in, 16)
                if name == "ada6":
                    sp.wait_ge(s_sa_ready, NT)
                    sp.dma_start(gt1, ada_b[:, 2 * D:3 * D].partition_broadcast(P)).then_inc(s_x_load, 16)
                    sp.dma_start(gt2, ada_b[:, 5 * D:6 * D].partition_broadcast(P)).then_inc(s_x_load, 16)
                    sp.dma_start(fg, final_g.rearrange("(o n) -> o n", o=1).partition_broadcast(P)).then_inc(s_x_load, 16)
                    sp.dma_start(rb[:, :], router_b.partition_broadcast(P)).then_inc(s_x_load, 16)
                if i >= NBUF:
                    sp.wait_ge(pan_used, i - NBUF + 1)
                for src, c0, n, o in parts:
                    sp.dma_start(pan(name)[:, :, o:o + n], src[:, :, c0:c0 + n]).then_inc(pan_in[i % NBUF], 16)
            for t in range(NT):
                sp.wait_ge(s_h2_rows, NT + t + 1)
                sp.dma_start(xn_dram[TILE(t), :], xh2[:, t, :]).then_inc(s_xn_out, 16)
            gate_k = exp_w_gate.rearrange("o e (k p) n -> (o e) p k n", p=P)
            up_k = exp_w_up.rearrange("o e (k p) n -> (o e) p k n", p=P)
            down_k = exp_w_down.rearrange("o e (k p) n -> (o e) p k n", p=P)

            def load_gu(e, w, source):
                sp.dma_start(w.rearrange("p (k n) -> p k n", k=NK), source[bass.ds(e, 1)].rearrange("a p k n -> (a p) k n")).then_inc(s_w_in, 16)

            def load_d(e, i):
                sp.dma_start(w_down[i].rearrange("p (k n) -> p k n", k=2), down_k[bass.ds(e, 1)].rearrange("a p k n -> (a p) k n")).then_inc(s_wd_in[i], 16)

            sp.wait_ge(s_shared_done, 1)
            sp.wait_ge(s_cnt_ready, 1)
            load_gu(0, w_gate, gate_k)
            load_gu(0, w_up, up_k)
            for done in acc_out:
                sp.wait_ge(done, 8 * NT)
            sp.wait_ge(s_gathered, 16)
            for i in range(2):
                load_d(i, i)
            sp.wait_ge(s_split_gu, 1)
            load_gu(1, w_gate, gate_k)
            sp.wait_ge(s_split_gu, 2)
            load_gu(1, w_up, up_k)
            with sp.Fori(1, NE // 2) as pair:
                for i in range(2):
                    sp.wait_ge(s_split_d, pair * 2 + (i - 1))
                    load_d(pair * 2 + i, i)
                    sp.wait_ge(s_split_gu, pair * 4 + (2 * i - 1))
                    load_gu(pair * 2 + i, w_gate, gate_k)
                    sp.wait_ge(s_split_gu, pair * 4 + 2 * i)
                    load_gu(pair * 2 + i, w_up, up_k)
            sp.wait_ge(s_small_done, 7)
            for t in range(NT):
                sp.dma_start(x3[:, t, :], acc_dram[TILE(t), :]).then_inc(acc_in[t >= 2], 16)
            for t in range(NT):
                sp.wait_ge(s_o_ready, t + 1)
                sp.dma_start(out[0, TILE(t), :], xg if t % 2 == 0 else xTm).then_inc(out_done[t % 2], 16)
            for done in out_done:
                sp.wait_ge(done, OUT0 + 8 * NT)

        @block.gpsimd
        def _(pool):
            pool.memset(ident[:, :], 0.0).then_inc(consts_ready, 1)
            pool.memset(ones[:, :], 1.0).then_inc(consts_ready, 1)
            pool.memset(half[:, :, :], 0.0).then_inc(consts_ready, 1)
            pool.memset(tri[:, :], 1.0).then_inc(consts_ready, 1)
            pool.wait_ge(consts_ready, 4)
            pool.affine_select(out=ident[:, :], in_=ident[:, :], compare_op=ALU.not_equal, fill=1.0, base=0,
                               pattern=[[-1, P]], channel_multiplier=1).then_inc(consts_ready, 1)
            pool.affine_select(out=before[:, :], in_=ones[:, :], compare_op=ALU.is_gt, fill=0.0, base=0,
                               pattern=[[1, P]], channel_multiplier=-1).then_inc(consts_ready, 1)
            pool.affine_select(out=after[:, :], in_=ones[:, :], compare_op=ALU.is_gt, fill=0.0, base=0,
                               pattern=[[-1, P]], channel_multiplier=1).then_inc(consts_ready, 1)
            pool.affine_select(out=tri[:, :], in_=ones[:, :], compare_op=ALU.is_ge, fill=0.0, base=0,
                               pattern=[[1, P]], channel_multiplier=-1).then_inc(consts_ready, 1)
            pool.memset(epsc[:, 0:1], EPS).then_inc(consts_ready, 1)
            pool.memset(epsc[:, 1:2], 1.0).then_inc(consts_ready, 1)
            for p in pre:
                pool.memset(p[:, 0:3], 0.0).then_inc(consts_ready, 1)
            for n, (area, value) in enumerate(((tri[0:CHUNK, CHUNK:P], 0.0), (after[CHUNK:P, 0:CHUNK], 0.0),
                                               (half[0:CHUNK, 0, :], 1.0), (half[CHUNK:P, 1, :], 1.0))):
                pool.wait_ge(consts_ready, 12 + n)
                pool.memset(area, value).then_inc(consts_ready, 1)
            pool.wait_ge(consts_ready, 16)
            pool.dma_start(rowc[:, 0:H], a_log.partition_broadcast(P)).then_inc(rows_in, 16)
            pool.dma_start(rowc[:, H:2 * H], dt_bias.partition_broadcast(P)).then_inc(rows_in, 16)

            pool.wait_ge(pan_used, PAN["v"] + 1)
            pool.wait_ge(nrm_full, 8)
            pool.iota(xi, pattern=[[1, P]], base=0, channel_multiplier=0).then_inc(s_dn_consts, 1)
            pool.iota(ji, pattern=[[0, P]], base=0, channel_multiplier=1).then_inc(s_dn_consts, 1)
            pool.affine_select(out=gtm, in_=ones[:, :], compare_op=ALU.is_gt, fill=0.0, base=0,
                               pattern=[[1, P]], channel_multiplier=-1).then_inc(s_dn_consts, 1)
            pool.memset(S_st, 0.0).then_inc(s_dn_consts, 1)
            pool.wait_ge(s_dn_consts, 4)
            for t in range(NT):
                col = slice(t * H, (t + 1) * H)
                if t:
                    pool.wait_ge(s_gb_full, t)
                else:
                    pool.wait_ge(gc_ready, 1)
                pool.tensor_copy(heads(gbt), per_head(gates[:, 1, col])).then_inc(s_gb_ready, 1)
                pool.wait_ge(s_knqn_ready, 2 * (t + 1))
                if t:
                    pool.wait_ge(s_w_full, t)
                    pool.wait_ge(s_ods_full, 2 * t)
                pool.tensor_tensor(heads(kbe), heads(kn), per_head(gates[:, 7, col]), ALU.mult).then_inc(s_pool_k, 1)
                pool.tensor_tensor(heads(kd), heads(kn), per_head(gates[:, 4, col]), ALU.mult).then_inc(s_pool_k, 1)
                pool.wait_ge(s_at_ready, 2 * (t + 1))
                if t:
                    pool.wait_ge(s_p1_full, 10 * t)
                for n in range(1, 6):
                    pool.tensor_tensor(heads(CT[:, n - 1]), heads(AT), each_head(lvl[n]), ALU.mult).then_inc(s_ct_ready, 1)

            pool.wait_ge(s_ont_full, NT)
            pool.affine_select(out=lowm[:, :, :], in_=ones[:, 0:NG * NG].rearrange("p (a b) -> p a b", a=NG),
                               compare_op=ALU.is_gt, fill=0.0, base=0, pattern=[[1, NG], [-1, NG]],
                               channel_multiplier=0).then_inc(s_small_done, 1)
            pool.iota(di[0][:, 0:NE], pattern=[[T, NE]], base=1, channel_multiplier=0).then_inc(s_small_done, 1)
            pool.wait_ge(s_small_done, 2)
            pool.tensor_copy(erow[:, :], di[0][:, 0:NE]).then_inc(s_small_done, 1)
            pool.iota(pay.rearrange("p (t k two) -> p t k two", t=NT, two=2)[:, :, :, 0:1],
                      pattern=[[P, NT], [0, TOP_E], [0, 1]], base=0, channel_multiplier=1).then_inc(s_small_done, 1)
            tv = tbl.rearrange("p (n two) -> p n two", two=2)
            pool.iota(tv[:, :, 0:1], pattern=[[0, NE * CAP], [0, 1]], base=T, channel_multiplier=1).then_inc(s_tbl_init, 1)
            pool.iota(tv[:, :, 1:2], pattern=[[0, NE * CAP], [0, 1]], base=0, channel_multiplier=0).then_inc(s_tbl_init, 1)
            pool.wait_ge(s_y1_full, 2 * NT)
            pool.memset(ysb, 0.0).then_inc(s_tbl_init, 1)
            pool.wait_ge(s_tbl_init, 3)
            pool.dma_start(table_dram.rearrange("(p n) two -> p (n two)", p=P), tbl).then_inc(s_filler_out, 16)
            pool.dma_start(xn_dram[T:T + P, :], ysb).then_inc(s_filler_out, 16)
            pool.dma_start(acc_dram[T:T + P, :], ysb).then_inc(s_scattered, 16)
            pool.wait_ge(s_filler_out, 32)
            pool.wait_ge(s_scattered, 16)
            put = 0
            for t, n in enumerate(SLOTS_AFTER):
                pool.wait_ge(s_ssg_ready, 2 * (t + 1))
                if t:
                    pool.wait_ge(s_shT_full, t)
                pool.tensor_tensor(hm, sg, upb, ALU.mult).then_inc(s_shm_ready, 1)
                for j in range(put, put + n):
                    if j % TOP_E == 0:
                        pool.wait_ge(s_lists_ready, j // TOP_E + 1)
                    pool.indirect_dma_start(table_dram, bass.IndirectOffsetOnAxis(dest_i[:, j:j + 1], 0),
                                            pay[:, 2 * j:2 * j + 2], None).then_inc(s_slots_out, 16)
                put += n
            pool.wait_ge(s_slots_out, 16 * NT * TOP_E)
            pool.dma_start(tbl, table_dram.rearrange("(p n) two -> p (n two)", p=P)).then_inc(s_tbl_in, 16)
            for rows in (idx_now, idx_last, idx_hold):
                pool.iota(rows[:, 0:1], pattern=[[0, 1]], base=T, channel_multiplier=1).then_inc(s_idx_s, 1)
            pool.memset(xg, 0.0).then_inc(s_small_done, 1)
            pool.iota(idx_zero[:, 0:1], pattern=[[0, 1]], base=0, channel_multiplier=0).then_inc(s_small_done, 1)
            pool.wait_ge(s_small_done, 6)
            pool.wait_ge(s_idx_s, 3)
            pool.wait_ge(s_tbl_in, 16)
            pool.wait_ge(s_xn_out, 16 * NT)
            for done in acc_out:
                pool.wait_ge(done, 8 * NT)
            pool.wait_ge(s_cnt_ready, 1)

            def gather(g):
                pool.indirect_dma_start(xg, None, xn_dram, bass.IndirectOffsetOnAxis(idx_now[:, 0:1], 0)).then_inc(s_gathered, 16)

            def shift(dst, src, done):
                pool.tensor_tensor(dst[:, 0:1], src[:, 0:1], idx_zero[:, 0:1], ALU.add).then_inc(s_idx_s, 1)
                pool.wait_ge(s_idx_s, done)
                pool.sem_inc(s_paced, 1)

            def scatter(g):
                pool.wait_ge(s_scattered, 16 * g + 16)
                pool.sem_inc(s_paced, 1)
                shift(idx_out, idx_hold, 3 * g + 4)
                shift(idx_hold, idx_last, 3 * g + 5)
                shift(idx_last, idx_now, 3 * g + 6)
                pool.wait_ge(s_y_ready, g + 1)
                pool.sem_inc(s_paced, 1)
                pool.indirect_dma_start(acc_dram, bass.IndirectOffsetOnAxis(idx_out[:, 0:1], 0), ysb, None,
                                        compute_op=ALU.add).then_inc(s_scattered, 16)

            with pool.Fori(0, NE) as e:
                nb = pool.value_load(ints[0:1, bass.ds(e, 1)], min_val=1, max_val=CAP)
                b0 = pool.value_load(ints[0:1, bass.ds(e + NE, 1)], min_val=0, max_val=NE * CAP)
                with pool.Fori(0, nb) as b:
                    g = pool.snap(b0 + b)
                    pool.wait_ge(s_xg_read, g + 1)
                    pool.tensor_tensor(idx_now[:, 0:1], tbl[:, bass.ds((e * CAP + b) * 2, 1)], idx_zero[:, 0:1],
                                       ALU.add).then_inc(s_idx_g, 1)
                    pool.wait_ge(s_idx_g, g + 1)
                    pool.sem_inc(s_paced, 1)
                    gather(g)
                    scatter(g)
            total = pool.value_load(ints[0:1, 2 * NE:2 * NE + 1], min_val=NE, max_val=NE * CAP)
            pool.wait_ge(s_xg_read, total + 1)
            pool.sem_inc(s_paced, 1)
            gather(total)
            scatter(total)
            scatter(total + 1)
            pool.wait_ge(s_scattered, 16 * total + 48)
            pool.sem_inc(s_paced, 1)
            pool.sem_inc(s_small_done, 1)
            for t in range(NT):
                pool.wait_ge(s_gated, t + 1)
                pool.tensor_tensor(x3[:, t, :], x3[:, t, :], x2[:, t, :], ALU.add).then_inc(s_x3_ready, 1)

        @block.scalar
        def _(act):
            def copy(out_, in_, **kw):
                return act.activation(out_, in_, ACT.Copy, **kw)

            chain = [0]

            def link(ins):
                chain[0] += 1
                ins.then_inc(av, 1)
                act.wait_ge(av, chain[0])

            act.wait_ge(vT_ready, 1)
            act.activation(cond[:, :], vT[:, V_C:V_C + NK], ACT.Silu).then_inc(cond_ready, 1)
            act.wait_ge(x_in, 16 * NT)
            for t in range(NT):
                link(act.activation(sqx, xt_in[:, t, :], ACT.Square, accum_out=st[:, 0, t:t + 1]))
            act.wait_ge(consts_ready, 16)
            act.activation(st[:, 1, 0:NT], st[:, 0, 0:NT], ACT.Sqrt, scale=1.0 / D, bias=epsc[:, 0:1]).then_inc(rms_ready, 1)

            def group(name, i, j):
                g = GIDX[(name, i, j)]
                act.wait_ge(ring_full, g + 1)
                return ring_bank(g)

            free = ring_free["act"]
            act.wait_ge(ab1_ready, 1)
            for hf in range(2):
                for k in range(1, NK, 2):
                    b = group("hT", k, hf)
                    act.activation(hT[:, k, hf * HALF:(hf + 1) * HALF], b, ACT.Identity, scale=A1[:, k:k + 1],
                                   bias=B1[:, k:k + 1]).then_inc(free, 1)
            for t in range(NT):
                b = group("aux", t, 0)
                copy(aux[:, t, :], b[:, 0:AUX])
                act.activation(sqx[:, 0:KV_R], b[:, 0:KV_R], ACT.Square, accum_out=st[:, 3, t:t + 1]).then_inc(free, 1)
                act.wait_ge(free, nth[GIDX[("aux", t, 0)]])
            for ct in range(2):
                for hf in range(2):
                    copy(qixT[:, ct, hf * HALF:(hf + 1) * HALF], group("qix", ct, hf)).then_inc(free, 1)
            act.wait_ge(stats_asked, 1)
            act.activation(st[:, 3, 8:16], st[:, 3, 0:8], ACT.Sqrt, scale=1.0 / KV_R, bias=epsc[:, 0:1])
            act.activation(st[:, 2, 16:24], st[:, 2, 8:16], ACT.Sqrt, scale=1.0 / IX_D, bias=epsc[:, 0:1]).then_inc(stats_rooted, 1)
            for u in range(len(SEL_TILES) * H):
                n = (SEL_TILES[u // H] + 1) * P
                act.wait_ge(ixs_full, u + 1)
                if u >= 2:
                    act.wait_ge(rel_used, u - 1)
                act.activation(rel[u % 2][:, 0:n], bank(4 + 2 * (u % 2), 2)[:, 0:n], ACT.Relu).then_inc(rel_ready, 1)
            act.wait_ge(gate_in, 1)
            act.wait_ge(rows_in, 32)
            act.activation(gates[:, 0, :], gates[:, 8, :], ACT.Sigmoid)
            act.activation(rowc[:, 0:H], rowc[:, 0:H], ACT.Exp)
            act.activation(gates[:, 3, :], gates[:, 2, :], ACT.Abs).then_inc(gate_act, 1)
            act.wait_ge(gate_act, 1)
            act.activation(gates[:, 4, :], gates[:, 3, :], ACT.Exp, scale=-1.0).then_inc(gate_act, 1)
            act.wait_ge(gate_act, 2)
            act.activation(gates[:, 5, :], gates[:, 4, :], ACT.Ln, bias=epsc[:, 1:2]).then_inc(gate_act, 1)
            act.wait_ge(gc_full, 1)
            NC = NT * H
            act.activation(gates[:, 3, :], bank(7)[:, 0:NC], ACT.Exp)
            act.activation(gates[:, 4, :], bank(7)[:, NC:2 * NC], ACT.Exp)
            act.activation(gates[:, 5, :], bank(7)[:, 2 * NC:3 * NC], ACT.Exp)
            act.activation(gates[:, 6, :], bank(7)[:, 3 * NC:4 * NC], ACT.Exp).then_inc(gate_act, 1)
            for h in range(H):
                for hf in range(2):
                    copy(khT[:, h, hf * HALF:(hf + 1) * HALF], group("kh", h, hf)).then_inc(free, 1)
            for t in range(NT):
                copy(vh[:, t, :], group("vh", t, 0)).then_inc(free, 1)
            for h in range(H):
                for hf in range(2):
                    copy(qsaT[:, h, hf * HALF:(hf + 1) * HALF], group("qsa", h, hf)).then_inc(free, 1)
            for t in range(NT):
                act.activation(zg[:, t, :], group("z", t, 0), ACT.Silu).then_inc(free, 1)
            act.wait_ge(rel_used, len(SEL_TILES) * H)
            act.wait_ge(gc_ready, 1)
            act.wait_ge(consts_ready, 16)

            def conv_act_fn(ct):
                act.wait_ge(conv_ready, 2 * ct + 2)
                act.activation(qkvT[:, ct, :], qkvT[:, ct, :], ACT.Silu).then_inc(conv_act, 1)

            for ct in range(12):
                for hf in range(2):
                    n = 2 * ct + hf
                    b = group("conv", ct, hf)
                    if n >= 2:
                        act.wait_ge(conv_ready, n - 1)
                    if hf:
                        act.wait_ge(pre_ready, n)
                        link(copy(pre[1][:, 0:3], pre[0][:, HALF:HALF + 3]))
                    copy(pre[hf][:, 3:3 + HALF], b).then_inc(pre_ready, 1)
                    col = V_ROWS + (CONV_K - 1) * 12 + ct
                    copy(qkvT[:, ct, hf * HALF:(hf + 1) * HALF], b, scale=vT[:, col:col + 1]).then_inc(free, 1)
                if ct:
                    conv_act_fn(ct - 1)
                if ct >= 8:
                    for c2 in (2 * (ct - 8), 2 * (ct - 8) + 1):
                        act.wait_ge(pan_used, PAN["k"] + 1)
                        act.wait_ge(conv_act, c2 + 1)
                        if c2 >= 4:
                            act.wait_ge(nrm_full, c2 - 3)
                        act.activation(square[c2 % 4], qkvT[:, c2, :], ACT.Square).then_inc(sq_ready, 1)
            conv_act_fn(11)

            act.wait_ge(nrm_full, 8)
            act.activation(st[:, 0, :], bank(7)[:, 0:NT * 8], ACT.Sqrt, bias=epsc[:, 0:1]).then_inc(s_nrm_ready, 1)
            for t in range(NT):
                for i, dst in enumerate((knT, kbT, qnT, qdT)):
                    act.wait_ge(s_t_full, 4 * t + i + 1)
                    copy(dst, bank(3 + i)).then_inc(s_t_act, 1)
                act.wait_ge(s_dd_ready, t + 1)
                act.activation(ET, ET, ACT.Exp).then_inc(s_dd_exp, 1)
                act.wait_ge(s_x1_full, t + 1)
                copy(X, bank(2)).then_inc(s_x1_ready, 1)
                for n in range(10):
                    act.wait_ge(s_p1_full, 10 * t + n + 1)
                    copy(P1[:, PAIR(n % 2)], bank(B_P1[n % 2])[:, PAIR(n % 2)]).then_inc(s_p1_ready, 1)
                act.wait_ge(s_w_full, t + 1)
                copy(wT, bank(6)).then_inc(s_w_ready, 1)
                for cc in range(2):
                    R = slice(cc * CHUNK, (cc + 1) * CHUNK)
                    act.wait_ge(s_vn_full, 2 * t + cc + 1)
                    copy(vn[R, :], bank(7)[R, :]).then_inc(s_vn_ready, 1)
                act.wait_ge(s_ods_full, 2 * (t + 1))
                if t:
                    act.wait_ge(s_oz_ready, t)
                act.activation(osq, bank(3), ACT.Square).then_inc(s_o_sq, 1)
            act.wait_ge(s_oz_ready, NT)
            act.activation(st[:, 1, 0:NC], st[:, 1, 32:64], ACT.Sqrt, scale=1.0 / DH, bias=epsc[:, 0:1]).then_inc(s_orms_ready, 1)
            for t in range(NT):
                act.wait_ge(s_ont_full, t + 1)
                copy(qkvT[:, 0:H, TILE(t)], heads(bank(t % 2)), scale=vT[:, V_DG:V_DG + 1]).then_inc(s_dnT_ready, 1)

            def pt_evac(u):
                for gi in pt_groups(u):
                    if gi % 2 == 0:
                        n = pt_cols(u, gi)
                        act.wait_ge(s_pt_full, gi + 1)
                        if u >= 2:
                            act.wait_ge(s_o_full, u - 1)
                        copy(prT[u % 2][:, n], bank(0)[:, 0:n.stop - n.start]).then_inc(s_pt_act, 1)

            for u in range(NT * H + 1):
                if u:
                    pt_evac(u - 1)
                if u < NT * H:
                    n = (u // H + 1) * P
                    act.wait_ge(s_mx_ready, u + 1)
                    act.activation(lg[u % 2][:, 0:n], lg[u % 2][:, 0:n], ACT.Exp, scale=SM_SCALE,
                                   bias=st[:, 1, u:u + 1], accum_out=st[:, 2, u:u + 1]).then_inc(s_pr_ready, 1)
                if u > H and (u - 1) % H == 1:
                    sa_evac(act, (u - 1) // H - 1)
            sa_evac(act, NT - 1)

            for t in range(NT):
                act.wait_ge(s_y1_read, 2 * (NT + t + 1))
                act.activation(junk, x2[:, t, :], ACT.Square, accum_out=st[:, 0, t:t + 1]).then_inc(s_ssq2_ready, 1)
                act.wait_ge(s_ssq2_ready, t + 1)
                act.activation(st[:, 1, t:t + 1], st[:, 0, t:t + 1], ACT.Sqrt, scale=1.0 / D, bias=epsc[:, 0:1]).then_inc(s_rms2_ready, 1)
            for i, row in enumerate((A2_row, B2_row)):
                act.wait_ge(s_ab_full, i + 1)
                for n in range(2):
                    copy(row[:, n * HALF:(n + 1) * HALF], bank(2 * i + n)).then_inc(s_ab_rows, 1)
            for m in range(0, 16, 2):
                hf, k = m // 8, m % 8
                act.wait_ge(s_h2_full, m + 1)
                act.wait_ge(s_ab2_ready, 1)
                act.activation(h2T[:, k, hf * HALF:(hf + 1) * HALF], bank(4 + m % 4), ACT.Identity,
                               scale=A2[:, k:k + 1], bias=B2[:, k:k + 1]).then_inc(s_h2_act, 1)
            act.wait_ge(s_rl_full, 1)
            act.activation(r_sc, bank(0), ACT.Sigmoid).then_inc(s_rsc_ready, 1)
            for t in range(NT):
                b = bank(4 + t % 2)
                act.wait_ge(s_sgu_full, t + 1)
                if t:
                    act.wait_ge(s_shm_ready, t)
                act.activation(sg, b[:, 0:FE], ACT.Silu).then_inc(s_ssg_ready, 1)
                copy(upb, b[:, FE:2 * FE]).then_inc(s_ssg_ready, 1)
                act.wait_ge(s_shT_full, t + 1)
                copy(hmT, bank(6)[:, 0:FE]).then_inc(s_shT_ready, 1)
                if t >= 2:
                    act.wait_ge(acc_out[t % 2], 16 * (t // 2))
                act.wait_ge(s_sy_full, 2 * t + 1)
                copy(ysh[t % 2][:, 0:HALF], bank(7)).then_inc(s_sy_act, 1)
                act.wait_ge(s_sy_full, 2 * t + 2)
                copy(ysh[t % 2][:, HALF:D], bank(0)).then_inc(s_sy_act, 1)
                act.wait_ge(s_sy_act, 2 * t + 2)
                act.dma_start(acc_dram[TILE(t), :], ysh[t % 2]).then_inc(acc_out[t % 2], 16)
            for done in acc_out:
                act.wait_ge(done, 8 * NT)

            tf = tbl.bitcast(F32)

            def split_gu(e, i):
                act.wait_ge(s_w_in, e * 32 + 32)
                for w, where in GU_PARTS:
                    copy(where(wh[i]), w).then_inc(s_wh_ready, 1)

            def split_d(i, n):
                act.wait_ge(s_wd_in[i], n * 16 + 16)
                for w, where in D_PARTS[i]:
                    copy(where(wh[i]), w).then_inc(s_wh_ready, 1)

            def x_evac(n):
                for i in range(2):
                    ins = copy(xh[:, i * HALF:(i + 1) * HALF], bank(i))
                ins.then_inc(s_xT_act, 1)

            act.wait_ge(s_shared_done, 1)
            split_gu(0, 0)
            act.wait_ge(s_tbl_in, 16)
            act.wait_ge(s_xg_read, 2)
            x_evac(0)
            split_d(0, 0)
            act.activation(epsc[:, 2:3], epsc[:, 0:1], ACT.Copy).then_inc(s_y_ready, 2)

            def expert(e, i, pair, more=True):
                if more:
                    split_gu(e + 1, 1 - i)
                    split_d(1 - i, pair + i)
                nb = act.value_load(ints[0:1, bass.ds(e, 1)], min_val=1, max_val=CAP)
                b0 = act.value_load(ints[0:1, bass.ds(e + NE, 1)], min_val=0, max_val=NE * CAP)
                with act.Fori(0, nb) as b:
                    g = act.snap(b0 + b)
                    act.wait_ge(s_gu_full, g + 1)
                    act.activation(sg, bank(2)[:, 0:FE], ACT.Silu).then_inc(s_silu_done, 1)
                    act.wait_ge(s_hT_full, g + 1)
                    copy(hTh, bank(3)[:, 0:FE]).then_inc(s_hT_ready, 1)
                    act.wait_ge(s_xg_read, g + 3)
                    x_evac(g + 1)
                    act.wait_ge(s_scattered, 16 * g + 48)
                    for n in range(2):
                        act.wait_ge(s_y_full, 2 * g + (n + 2))
                        act.sem_inc(s_paced, 1)
                        ins = copy(ysb[:, n * HALF:(n + 1) * HALF], bank(4 + n), scale=tf[:, bass.ds((e * CAP + b) * 2 + 1, 1)])
                    ins.then_inc(s_y_ready, 1)

            with act.Fori(0, NE // 2 - 1) as pair:
                for i in range(2):
                    expert(pair * 2 + i, i, pair)
            for i in range(2):
                expert(NE - 2 + i, i, NE // 2 - 1, i == 0)

            for t in range(NT):
                act.wait_ge(s_x3_ready, t + 1)
                act.activation(ysb, x3[:, t, :], ACT.Square, accum_out=st[:, 0, t:t + 1]).then_inc(s_ssq3_ready, 1)
                act.wait_ge(s_ssq3_ready, t + 1)
                act.activation(st[:, 1, t:t + 1], st[:, 0, t:t + 1], ACT.Sqrt, scale=1.0 / D, bias=epsc[:, 0:1]).then_inc(s_rms3_ready, 1)

        @block.tensor
        def _(pe):
            def mm(out_, lhsT, rhs, first, last):
                return pe.matmul(out_, lhsT, rhs, start=first, stop=last)

            def panel_in(name):
                i = PAN[name]
                pe.wait_ge(pan_in[i % NBUF], landed[i])
                return pan(name)

            pe.wait_ge(consts_ready, 16)
            pe.wait_ge(vecs_in, 16 * 11)
            pe.transpose(bank(7)[:, 0:V_ROWS], vecs[:, :], ident[0:V_ROWS, 0:V_ROWS])
            pe.transpose(bank(7)[:, P:P + 48], cwr[:, :], ident[0:48, 0:48]).then_inc(vecs_turned, 1)
            pe.wait_ge(cond_ready, 1)

            def ada_columns(names, turn):
                for i, name in enumerate(names):
                    w = panel_in(name)
                    for k in range(NK):
                        ins = mm(bank(i)[0:1, :], cond[:, k:k + 1], w[:, k, :], k == 0, k == NK - 1)
                    ins.then_inc(pan_used, 1)
                pe.wait_ge(mod_row, 4 * (turn + 1))
                for n in range(16):
                    ins = mm(bank(6)[:, n:n + 1], mod_r[0:1, n * P:(n + 1) * P], ones[0:1, 0:1], True, True)
                ins.then_inc(mod_full, 1)

            ada_columns([f"ada{i}" for i in range(4)], 0)

            def begin(name, i, j):
                g = GIDX[(name, i, j)]
                ring_wait(pe, g)
                return ring_bank(g)

            for hf in range(2):
                pe.wait_ge(xhat_ready, 4 * (hf + 1))
                for k in range(NK):
                    b = begin("hT", k, hf)
                    for q in range(4):
                        ins = pe.transpose(b[:, q * P:(q + 1) * P], xt_in[:, 4 * hf + q, k * P:(k + 1) * P], ident[:, :])
                    ins.then_inc(ring_full, 1)
            for eng in ("act", "dve"):
                pe.wait_ge(ring_free[eng], 8)
            w = panel_in("aux")
            for t in range(NT):
                b = begin("aux", t, 0)
                for k in range(NK):
                    ins = mm(b[:, 0:AUX], hT[:, k, TILE(t)], w[:, k, :], k == 0, k == NK - 1)
                ins.then_inc(ring_full, 1)

            def channels(name, j, w, c0, more=None):
                for hf in range(2):
                    b = begin(name, j, hf)
                    for k in range(NK):
                        ins = mm(b, w[:, k, c0:c0 + P], hT[:, k, hf * HALF:(hf + 1) * HALF], k == 0, k == NK - 1)
                    ins.then_inc(ring_full, 1)

            w = panel_in("qix")
            channels("qix", 0, w, 0)
            channels("qix", 1, w, P)
            pe.wait_ge(kv_ready, 1)
            for k in range(2):
                for hf in range(2):
                    b = begin("ckvT", k, hf)
                    for q in range(4):
                        ins = pe.transpose(b[:, q * P:(q + 1) * P], aux[:, 4 * hf + q, k * P:(k + 1) * P], ident[:, :])
                    ins.then_inc(ring_full, 1)
            for hf in range(2):
                b = begin("kixT", 0, hf)
                for q in range(4):
                    ins = pe.transpose(b[:, q * P:(q + 1) * P], kx2[:, 4 * hf + q, :], ident[:, :])
                ins.then_inc(ring_full, 1)
            pe.drain().then_inc(pan_used, 2)

            pe.wait_ge(ring_free["dve"], nth[GIDX[("kixT", 0, 1)]])
            pe.wait_ge(ring_free["act"], nth[GIDX[("qix", 1, 1)]])
            for u in range(len(SEL_TILES) * H):
                t, h = SEL_TILES[u // H], u % H
                if u >= 2:
                    pe.wait_ge(rel_ready, u - 1)
                R = slice((h % 2) * IX_D, (h % 2) * IX_D + IX_D)
                b = bank(4 + 2 * (u % 2), 2)
                for c0 in range(0, (t + 1) * P, HALF):
                    n = min(HALF, (t + 1) * P - c0)
                    ins = mm(b[:, c0:c0 + n], qixT[R, h // 2, TILE(t)], kixT[R, c0:c0 + n], True, True)
                ins.then_inc(ixs_full, 1)
            pe.wait_ge(g_ready, 1)
            pe.wait_ge(rel_ready, len(SEL_TILES) * H)
            NC = NT * H
            for i, m in enumerate((tri[:, :], after[:, :], half[:, 0, :], half[:, 1, :])):
                ins = mm(bank(7)[:, i * NC:(i + 1) * NC], m, gates[:, 1, :], True, True)
            ins.then_inc(gc_full, 1)
            pe.wait_ge(w_small, 48)
            for h in range(H):
                for hf in range(2):
                    b = begin("kh", h, hf)
                    for k in range(2):
                        ins = mm(b, wuk[:, h, k, :], ckvT[:, k, hf * HALF:(hf + 1) * HALF], k == 0, k == 1)
                    ins.then_inc(ring_full, 1)
            for t in range(NT):
                b = begin("vh", t, 0)
                for k in range(2):
                    ins = mm(b, ckvT[:, k, TILE(t)], wuv[:, k].rearrange("p h n -> p (h n)"), k == 0, k == 1)
                ins.then_inc(ring_full, 1)
            w = panel_in("qsa")
            for h in range(H):
                channels("qsa", h, w, h * DH)
            pe.drain().then_inc(pan_used, 1)
            w = panel_in("z")
            for t in range(NT):
                b = begin("z", t, 0)
                for k in range(NK):
                    ins = mm(b, hT[:, k, TILE(t)], w[:, k, :], k == 0, k == NK - 1)
                ins.then_inc(ring_full, 1)
            pe.drain().then_inc(pan_used, 1)
            def norms(first):
                for ct in (first, first + 1):
                    pe.wait_ge(sq_ready, ct + 1)
                    for t in range(NT):
                        ins = mm(bank(7)[:, t * 8 + ct:t * 8 + ct + 1], square[ct % 4][:, TILE(t)], ones[:, 0:1], True, True)
                    ins.then_inc(nrm_full, 1)

            pe.wait_ge(gc_ready, 1)
            for i, name in enumerate(("q", "k", "v")):
                w = panel_in(name)
                for j in range(4):
                    channels("conv", 4 * i + j, w, j * P)
                    if name == "v" and j:
                        norms(2 * (j - 1))
                pe.drain().then_inc(pan_used, 1)

            norms(6)

            pe.wait_ge(ring_free["act"], n_of["act"])
            pe.wait_ge(conv_act, 12)
            def turn_qkv(t, i):
                for h in range(H):
                    ins = pe.transpose(bank(i)[:, HSL(h)], qkvT[:, 4 * i + h, TILE(t)], ident[:, :])
                ins.then_inc(s_qkv_full, 1)

            for i in range(3):
                turn_qkv(0, i)
            for t in range(NT):
                pe.wait_ge(s_gb_ready, t + 1)
                pe.wait_ge(s_nrm_ready, 1)
                for h in range(H):
                    ins = mm(bank(7)[:, HSL(h)], heads(gbt)[:, h, :], tri[:, :], True, True)
                ins.then_inc(s_gb_full, 1)
                if t:
                    pe.wait_ge(s_oz_ready, t)
                    pe.wait_ge(s_o_sq, t)
                for i, src in enumerate((kn, kb, qn, qd)):
                    pe.wait_ge(s_kk_full, 4 * t + i + 1)
                    for h in range(H):
                        ins = pe.transpose(bank(3 + i)[:, HSL(h)], src[:, HSL(h)], ident[:, :])
                    ins.then_inc(s_t_full, 1)
                pe.wait_ge(s_t_act, 4 * t + 4)
                for i, (l_, r_) in enumerate(((knT, kbT), (knT, qnT))):
                    for h in range(H):
                        ins = mm(bank(i)[:, HSL(h)], l_[:, HSL(h)], r_[:, HSL(h)], True, True)
                    ins.then_inc(s_p_kk, 1)
                pe.wait_ge(s_xt1_ready, t + 1)
                for h in range(H):
                    ins = pe.transpose(bank(2)[:, HSL(h)], XT[:, HSL(h)], ident[:, :])
                ins.then_inc(s_x1_full, 1)
                pe.wait_ge(s_x1_ready, t + 1)
                for l in range(5):
                    pe.wait_ge(s_ct_ready, 5 * t + l + 1)
                    for pr in range(2):
                        if l:
                            pe.wait_ge(s_dx_ready, 18 * t + 4 * (l - 1) + 2 * pr + 2)
                        for h in (2 * pr, 2 * pr + 1):
                            ins = mm(bank(B_P1[pr])[:, HSL(h)], CT[:, l, HSL(h)], X[:, HSL(h)], True, True)
                        ins.then_inc(s_p1_full, 1)
                    for pr in range(2):
                        pe.wait_ge(s_p1_ready, 10 * t + 2 * l + pr + 1)
                        for h in (2 * pr, 2 * pr + 1):
                            ins = mm(bank(B_XT[pr])[:, HSL(h)], P1[:, HSL(h)], XT[:, HSL(h)], True, True)
                        ins.then_inc(s_dx_full, 1)
                        if l < 4:
                            for h in (2 * pr, 2 * pr + 1):
                                ins = mm(bank(B_X[pr])[:, HSL(h)], XT[:, HSL(h)], P1[:, HSL(h)], True, True)
                            ins.then_inc(s_dx_full, 1)
                pe.wait_ge(s_dx_ready, 18 * (t + 1))
                pe.wait_ge(s_pool_k, 2 * (t + 1))
                for h in range(H):
                    ins = mm(bank(6)[:, HSL(h)], kbe[:, HSL(h)], XT[:, HSL(h)], True, True)
                ins.then_inc(s_w_full, 1)
                pe.wait_ge(s_w_ready, t + 1)
                for cc in range(2):
                    R = slice(cc * CHUNK, (cc + 1) * CHUNK)
                    n = 2 * t + cc
                    if n:
                        pe.wait_ge(s_s_ready, n)
                    else:
                        pe.wait_ge(s_dn_consts, 4)
                    for h in range(H):
                        C = slice(h * DH + cc * CHUNK, h * DH + (cc + 1) * CHUNK)
                        mm(bank(7)[R, HSL(h)], XT[R, C], bv[R, HSL(h)], True, False)
                        ins = mm(bank(7)[R, HSL(h)], wT[:, C], S_st[:, HSL(h)], False, True)
                    ins.then_inc(s_vn_full, 1)
                    if t + 1 < NT:
                        turn_qkv(t + 1, 2 * cc)
                    pe.wait_ge(s_vn_ready, n + 1)
                    for h in range(H):
                        C = slice(h * DH + cc * CHUNK, h * DH + (cc + 1) * CHUNK)
                        mm(bank(3)[R, HSL(h)], qdT[:, C], S_st[:, HSL(h)], True, False)
                        mm(bank(3)[R, HSL(h)], QKT[R, C], vn[R, HSL(h)], False, True)
                    for h in range(H):
                        ins = mm(bank(4 + cc)[:, HSL(h)], kd[R, HSL(h)], vn[R, HSL(h)], True, True)
                    ins.then_inc(s_ods_full, 1)
                    if cc == 0 and t + 1 < NT:
                        turn_qkv(t + 1, 1)
            for t in range(NT):
                pe.wait_ge(s_on_ready, t + 1)
                if t >= 2:
                    pe.wait_ge(s_dnT_ready, t - 1)
                for h in range(H):
                    ins = pe.transpose(bank(t % 2)[:, HSL(h)], zg[:, t, HSL(h)], ident[:, :])
                ins.then_inc(s_ont_full, 1)

            def logits(u):
                t, h = u // H, u % H
                if u >= 2:
                    pe.wait_ge(s_lg_ready, u - 1)
                b = bank(4 + 2 * (u % 2), 2)
                for c0 in range(0, (t + 1) * P, HALF):
                    n = min(HALF, (t + 1) * P - c0)
                    ins = mm(b[:, c0:c0 + n], qsaT[:, h, TILE(t)], khT[:, h, c0:c0 + n], True, True)
                ins.then_inc(s_lg_full, 1)

            def attend(u):
                t, h = u // H, u % H
                pe.wait_ge(s_pr_ready, u + 1)
                for gi in pt_groups(u):
                    if gi >= 2:
                        pe.wait_ge(s_pt_dve if gi % 2 else s_pt_act, gi // 2)
                    n = pt_cols(u, gi)
                    for c0 in range(n.start, n.stop, P):
                        ins = pe.transpose(bank(gi % 2)[:, c0 - n.start:c0 - n.start + P], lg[u % 2][:, c0:c0 + P], ident[:, :])
                    ins.then_inc(s_pt_full, 1)
                last = pt_groups(u)[-1]
                pe.wait_ge(s_pt_act, last // 2 + 1)
                if last:
                    pe.wait_ge(s_pt_dve, (last + 1) // 2)
                if h == 0 and t:
                    pe.wait_ge(s_osa_ready, t)
                for kb_ in range(t + 1):
                    ins = mm(bank(2)[:, HSL(h)], prT[u % 2][:, kb_ * P:(kb_ + 1) * P], vh[:, kb_, HSL(h)], kb_ == 0, kb_ == t)
                ins.then_inc(s_o_full, 1)

            def turn_out(t):
                pe.wait_ge(s_osa_ready, t + 1)
                if t:
                    pe.wait_ge(s_sa_ready, t)
                for h in range(H):
                    ins = pe.transpose(bank(3)[:, HSL(h)], osa[:, HSL(h)], ident[:, :])
                ins.then_inc(s_oT_full, 1)

            pe.wait_ge(s_s_ready, 2 * NT)
            pe.wait_ge(s_oz_ready, NT)
            pe.wait_ge(s_dnT_ready, NT)
            logits(0)
            for u in range(NT * H):
                if u + 1 < NT * H:
                    logits(u + 1)
                attend(u)
                if u > H and u % H == 1:
                    turn_out(u // H - 1)
            turn_out(NT - 1)

            pe.wait_ge(s_lg_ready, NT * H)
            pe.wait_ge(s_sa_ready, NT)

            def ada_rows(names, b0):
                for i, name in enumerate(names):
                    w = panel_in(name)
                    for k in range(NK):
                        ins = mm(bank(b0 + i), condrep[:, k, :], w[:, k, :], k == 0, k == NK - 1)
                    ins.then_inc(pan_used, 1)

            pe.wait_ge(s_gt1_full, 1)
            ada_rows(("ada4", "ada5"), 4)
            ada_columns([f"ada{i}" for i in range(6, 10)], 1)
            pe.wait_ge(s_gt1_ready, 1)
            ada_rows(("ada10", "ada11"), 4)
            for n in range(2):
                w = panel_in(f"wo{n}")
                for t in range(NT):
                    gi = n * NT + t
                    if gi >= 4:
                        pe.wait_ge(s_y1_read, 2 * (gi - 3) - 1)
                    for k in range(NK):
                        mixT = qkvT[:, k, TILE(t)] if k < H else qsaT[:, k - H, TILE(t)]
                        ins = mm(bank(gi % 4), mixT, w[:, k, :], k == 0, k == NK - 1)
                    ins.then_inc(s_y1_full, 1)
                pe.drain().then_inc(pan_used, 1)
            pe.wait_ge(s_ab2_ready, 1)
            pe.wait_ge(s_gt2_ready, 1)
            pe.wait_ge(s_y1_read, 4 * NT)
            pe.wait_ge(s_ab2_ready, 2)
            for i in range(2):
                for k in range(NK):
                    ins = mm(bank(2 * i, 2)[:, k * P:(k + 1) * P], ab_rep[:, i, k, :], ident[:, :], True, True)
                ins.then_inc(s_ab_full, 1)
            for m in range(16):
                hf, k = m // 8, m % 8
                pe.wait_ge(s_xh2_ready, 4 * (hf + 1))
                if m >= 4:
                    pe.wait_ge(s_h2_dve if m % 2 else s_h2_act, (m - 4) // 2 + 1)
                for q in range(4):
                    ins = pe.transpose(bank(4 + m % 4)[:, q * P:(q + 1) * P], xh2[:, 4 * hf + q, k * P:(k + 1) * P], ident[:, :])
                ins.then_inc(s_h2_full, 1)
            pe.wait_ge(s_h2_act, 8)
            pe.wait_ge(s_h2_dve, 8)
            pe.wait_ge(s_ab_rows, 4)
            w = panel_in("router")
            for t in range(NT):
                for k in range(NK):
                    ins = mm(bank(0)[:, t * NE:(t + 1) * NE], h2T[:, k, TILE(t)], w[:, k, :], k == 0, k == NK - 1)
            ins.then_inc(s_rl_full, 1)
            pe.wait_ge(s_rsc_ready, 1)
            wgu, wd = panel_in("sgu"), None
            for t in range(NT):
                if t == 2:
                    pe.wait_ge(s_mask_ready, 1)
                    for tt in range(NT):
                        for t2 in range(tt):
                            mm(bank(1)[:, tt * NE:(tt + 1) * NE], ones[:, :], r_mk[:, t2 * NE:(t2 + 1) * NE], t2 == 0, False)
                        mm(bank(1)[:, tt * NE:(tt + 1) * NE], before[:, :], r_mk[:, tt * NE:(tt + 1) * NE], tt == 0, True)
                    for tt in range(NT):
                        ins = mm(bank(2)[:, 0:NE], ones[:, :], r_mk[:, tt * NE:(tt + 1) * NE], tt == 0, tt == NT - 1)
                    ins.then_inc(s_pos_full, 1)
                if t == 4:
                    pe.wait_ge(s_nbr_ready, 1)
                    mm(bank(3)[0:NE, 0:P], nbf[0:1, :], ones[0:1, :], True, True).then_inc(s_nbt_full, 1)
                    pe.wait_ge(s_nbt_ready, 1)
                    mm(bank(3)[:, P:P + NE], nbc, before[0:NE, 0:NE], True, True).then_inc(s_nbt_full, 1)
                b = bank(4 + t % 2)
                for k in range(NK):
                    ins = mm(b, h2T[:, k, TILE(t)], wgu[:, k, :], k == 0, k == NK - 1)
                ins.then_inc(s_sgu_full, 1)
                if t == 0:
                    pe.drain().then_inc(pan_used, 1)
                    wd = panel_in("sd")
                pe.wait_ge(s_shm_ready, t + 1)
                for i in range(2):
                    ins = pe.transpose(bank(6)[:, i * P:(i + 1) * P], hm[:, i * P:(i + 1) * P], ident[:, :])
                ins.then_inc(s_shT_full, 1)
                pe.wait_ge(s_shT_ready, t + 1)
                if t:
                    pe.wait_ge(s_sy_act, 2 * t)
                for n, bb in enumerate((bank(7), bank(0))):
                    for k in range(2):
                        ins = mm(bb, hmT[:, k * P:(k + 1) * P], wd[:, k, n * HALF:(n + 1) * HALF], k == 0, k == 1)
                    ins.then_inc(s_sy_full, 1)

            def turn_x(ks):
                for k in ks:
                    ins = pe.transpose(bank(0, 2)[:, k * P:(k + 1) * P], xg[:, k * P:(k + 1) * P], ident[:, :])
                return ins

            pe.wait_ge(s_sy_act, 2 * NT)
            pe.wait_ge(s_cnt_ready, 1)
            pe.drain().then_inc(s_shared_done, 1)
            pe.drain().then_inc(s_y_full, 1)
            pe.drain().then_inc(s_xg_read, 1)
            pe.wait_ge(s_gathered, 16)
            turn_x(range(NK)).then_inc(s_xg_read, 1)
            with pe.Fori(0, NE // 2) as pair:
                for i in range(2):
                    e = pair * 2 + i
                    guh, gul = (w[:, 0:4096].rearrange("p (k n) -> p k n", k=NK) for w in (wh[i], wl[i]))
                    dwh, dwl = (w[:, 4096:6144].rearrange("p (k n) -> p k n", k=2) for w in (wh[i], wl[i]))
                    nb = pe.value_load(ints[0:1, bass.ds(e, 1)], min_val=1, max_val=CAP)
                    b0 = pe.value_load(ints[0:1, bass.ds(e + NE, 1)], min_val=0, max_val=NE * CAP)
                    with pe.Fori(0, nb) as b:
                        g = pe.snap(b0 + b)
                        pe.wait_ge(s_split_gu, pair * 4 + (2 * i + 2))
                        pe.wait_ge(s_xT_act, g + 1)
                        for k in range(NK):
                            mm(bank(2), xh[:, k * P:(k + 1) * P], guh[:, k, :], k == 0, False)
                            mm(bank(2), xh[:, k * P:(k + 1) * P], gul[:, k, :], False, False)
                        pe.wait_ge(s_xT_dve, g + 1)
                        for k in range(NK):
                            ins = mm(bank(2), xl[k // 4][:, k % 4 * P:(k % 4 + 1) * P], guh[:, k, :], False, k == NK - 1)
                        ins.then_inc(s_gu_full, 1)
                        pe.wait_ge(s_gathered, 16 * g + 32)
                        turn_x(range(5))
                        pe.wait_ge(s_hm_ready, g + 1)
                        for k in range(2):
                            ins = pe.transpose(bank(3)[:, k * P:(k + 1) * P], hm[:, k * P:(k + 1) * P], ident[:, :])
                        ins.then_inc(s_hT_full, 1)
                        turn_x(range(5, NK)).then_inc(s_xg_read, 1)
                        pe.wait_ge(s_hT_ready, g + 1)
                        pe.wait_ge(s_split_d, pair * 2 + (i + 1))
                        pe.wait_ge(s_y_ready, g + 2)
                        for n in range(2):
                            for k in range(2):
                                for w in (dwh, dwl):
                                    mm(bank(4 + n), hTh[:, k * P:(k + 1) * P], w[:, k, n * HALF:(n + 1) * HALF],
                                       k == 0 and w is dwh, False)
                        pe.wait_ge(s_hl_ready, g + 1)
                        for n in range(2):
                            for k in range(2):
                                ins = mm(bank(4 + n), hTl[:, k * P:(k + 1) * P], dwh[:, k, n * HALF:(n + 1) * HALF], False, k == 1)
                            ins.then_inc(s_y_full, 1)

        @block.vector
        def _(dve):
            chain = [0]

            def link(ins):
                chain[0] += 1
                ins.then_inc(dv, 1)
                dve.wait_ge(dv, chain[0])

            tt, ts, stt = dve.tensor_tensor, dve.tensor_scalar, dve.scalar_tensor_tensor
            dve.wait_ge(vecs_turned, 1)
            dve.tensor_copy(vT[:, 0:V_ROWS], bank(7)[:, 0:V_ROWS])
            link(dve.tensor_copy(vT[:, V_ROWS:V_ROWS + 48], bank(7)[:, P:P + 48]))
            dve.engine_nop().then_inc(vT_ready, 1)
            dve.wait_ge(rms_ready, 1)
            link(dve.reciprocal(st[:, 2, 0:NT], st[:, 1, 0:NT]))
            for t in range(NT):
                ts(xt_in[:, t, :], xt_in[:, t, :], st[:, 2, t:t + 1], None, ALU.mult).then_inc(xhat_ready, 1)

            def modulation(A, B, n_row, c_sh, c_sc, turn):
                for i in range(4):
                    dve.wait_ge(pan_used, PAN["ada6" if turn else "ada0"] + i + 1)
                    dve.tensor_copy(mod_r[0:1, i * HALF:(i + 1) * HALF], bank(i)[0:1, :]).then_inc(mod_row, 1)
                dve.wait_ge(mod_full, turn + 1)
                tt(B[:, :], bank(6)[:, 0:8], vT[:, c_sh:c_sh + 8], ALU.add)
                link(tt(A[:, :], bank(6)[:, 8:16], vT[:, c_sc:c_sc + 8], ALU.add))
                link(stt(out=A[:, :], in0=A[:, :], scalar=1.0, in1=vT[:, n_row:n_row + 8], op0=ALU.add, op1=ALU.mult))

            modulation(A1, B1, V_N1, 0, 8, 0)
            dve.engine_nop().then_inc(ab1_ready, 1)

            def group(name, i, j):
                g = GIDX[(name, i, j)]
                dve.wait_ge(ring_full, g + 1)
                return ring_bank(g)

            free = ring_free["dve"]
            for hf in range(2):
                for k in range(0, NK, 2):
                    ts(hT[:, k, hf * HALF:(hf + 1) * HALF], group("hT", k, hf), A1[:, k:k + 1], B1[:, k:k + 1],
                       ALU.mult, ALU.add).then_inc(free, 1)
            dve.wait_ge(ring_free["act"], nth[GIDX[("aux", NT - 1, 0)]])
            kraw, kc, ksq = aux[:, :, KV_R:KV_R + IX_D], kx2[:, :, 0:IX_D], kx2[:, :, IX_D:2 * IX_D]
            bc = lambda col, n: col.unsqueeze(2).to_broadcast([P, NT, n])
            link(dve.tensor_reduce(st[:, 0, 8:16], kraw, AX.X, ALU.add))
            link(ts(st[:, 0, 8:16], st[:, 0, 8:16], 1.0 / IX_D, None, ALU.mult))
            link(tt(kc, kraw, bc(st[:, 0, 8:16], IX_D), ALU.subtract))
            link(tt(ksq, kc, kc, ALU.mult))
            dve.tensor_reduce(st[:, 2, 8:16], ksq, AX.X, ALU.add).then_inc(stats_asked, 1)
            o = KV_R + IX_D
            v3 = lambda r: gates[:, r, :].rearrange("p (t h) -> p t h", t=NT)
            dve.tensor_copy(v3(8), aux[:, :, o + IX_H:o + IX_H + H])
            ts(v3(9), aux[:, :, o:o + IX_H], IX_SCALE, None, ALU.mult)
            dve.wait_ge(rows_in, 32)
            tt(v3(2), aux[:, :, o + IX_H + H:o + IX_H + 2 * H],
               rowc[:, H:2 * H].unsqueeze(1).to_broadcast([P, NT, H]), ALU.add).then_inc(gate_in, 1)
            dve.wait_ge(stats_rooted, 1)
            dve.reciprocal(st[:, 3, 16:24], st[:, 3, 8:16])
            link(dve.reciprocal(st[:, 2, 24:32], st[:, 2, 16:24]))
            link(tt(kc, kc, bc(st[:, 2, 24:32], IX_D), ALU.mult))
            dve.tensor_copy(ksq, kc)
            tt(aux[:, :, 0:KV_R], aux[:, :, 0:KV_R], bc(st[:, 3, 16:24], KV_R), ALU.mult).then_inc(kv_ready, 1)
            for k in range(2):
                for hf in range(2):
                    ts(ckvT[:, k, hf * HALF:(hf + 1) * HALF], group("ckvT", k, hf), vT[:, V_KVG + k:V_KVG + k + 1],
                       None, ALU.mult).then_inc(free, 1)
            for hf in range(2):
                ts(kixT[:, hf * HALF:(hf + 1) * HALF], group("kixT", 0, hf), vT[:, V_KG:V_KG + 1], vT[:, V_KB:V_KB + 1],
                   ALU.mult, ALU.add).then_inc(free, 1)
            for u in range(len(SEL_TILES) * H):
                t, h = SEL_TILES[u // H], u % H
                n = (t + 1) * P
                w = gates[:, 9, t * H + h:t * H + h + 1]
                dve.wait_ge(rel_ready, u + 1)
                if h:
                    dve.wait_ge(rel_used, u)
                    stt(out=score[t], in0=rel[u % 2][:, 0:n], scalar=w, in1=score[t], op0=ALU.mult, op1=ALU.add).then_inc(rel_used, 1)
                else:
                    ts(score[t], rel[u % 2][:, 0:n], w, None, ALU.mult).then_inc(rel_used, 1)
            dve.wait_ge(gate_act, 3)
            link(stt(out=gates[:, 1, :], in0=gates[:, 2, :], scalar=0.0, in1=gates[:, 5, :], op0=ALU.max, op1=ALU.add))
            link(ts(gates[:, 1, :], gates[:, 1, :], -1.0, None, ALU.mult))
            tt(v3(1), v3(1), rowc[:, 0:H].unsqueeze(1).to_broadcast([P, NT, H]), ALU.mult).then_inc(g_ready, 1)
            dve.wait_ge(gate_act, 4)
            NC = NT * H
            dve.tensor_copy(gates[:, 2, :], bank(7)[:, 0:NC])
            stt(out=gates[:, 7, :], in0=gates[:, 0, :], scalar=-1.0, in1=gates[:, 3, :], op0=ALU.mult, op1=ALU.mult).then_inc(gc_ready, 1)

            picked = [0]

            def pick(n):
                for i in range(picked[0], min(picked[0] + n, ROUNDS * len(SEL_TILES))):
                    t, r = SEL_TILES[i // ROUNDS], i % ROUNDS
                    sc = score[t]
                    if r == 0:
                        link(dve.memset(sc[0:CHUNK, t * P + CHUNK:(t + 1) * P], NEG))
                    link(dve.max(m8[:, :], sc))
                    link(dve.match_replace(sc, m8[:, :], sc, TAKEN))
                    if r == ROUNDS - 1:
                        link(ts(sc, sc, TAKEN_CUT, NEG, ALU.is_gt, ALU.mult))
                picked[0] += n

            def conv(ct):
                for hf in range(2):
                    dst = qkvT[:, ct, hf * HALF:(hf + 1) * HALF]
                    dve.wait_ge(ring_free["act"], nth[GIDX[("conv", ct, hf)]])
                    for j in range(CONV_K - 1):
                        col = V_ROWS + j * 12 + ct
                        ins = stt(out=dst, in0=pre[hf][:, j:j + HALF], scalar=vT[:, col:col + 1], in1=dst,
                                  op0=ALU.mult, op1=ALU.add)
                        if j < CONV_K - 2:
                            link(ins)
                    ins.then_inc(conv_ready, 1)

            for ct in range(12):
                pick(SPLIT["before conv"][ct])
                conv(ct)

            dve.wait_ge(s_dn_consts, 4)
            link(tt(xor, xi, ji, ALU.bitwise_xor))
            for l in range(6):
                link(ts(tmp_m, xor, float(1 << l), None, ALU.is_ge))
                link(stt(out=tmp_m, in0=xor, scalar=float(2 << l), in1=tmp_m, op0=ALU.is_lt, op1=ALU.mult))
                link(tt(lvl[l], tmp_m, gtm, ALU.mult))
            dve.wait_ge(s_nrm_ready, 1)
            link(dve.reciprocal(st[:, 1, :], st[:, 0, :]))
            r4 = lambda lo: st[:, 1, :].rearrange("p (t c) -> p t c", c=8)[:, :, lo:lo + 4]
            s4 = lambda i: st[:, i, 0:NC].rearrange("p (t h) -> p t h", t=NT)
            ts(s4(2), r4(0), DH ** -0.5, None, ALU.mult)
            link(dve.tensor_copy(s4(3), r4(4)))
            for t in range(NT):
                col = slice(t * H, (t + 1) * H)
                dve.wait_ge(s_qkv_full, 3 * t + 3)
                if t:
                    dve.wait_ge(s_pool_k, 2 * t)
                tt(heads(kn), heads(bank(1)), per_head(st[:, 3, col]), ALU.mult).then_inc(s_knqn_ready, 1)
                tt(heads(qn), heads(bank(0)), per_head(st[:, 2, col]), ALU.mult).then_inc(s_knqn_ready, 1)
                tt(heads(bv), heads(bank(2)), per_head(gates[:, 0, col]), ALU.mult)
                dve.wait_ge(s_knqn_ready, 2 * t + 2)
                dve.engine_nop().then_inc(s_kk_full, 1)
                tt(heads(kb), heads(kn), per_head(gates[:, 0, col]), ALU.mult).then_inc(s_kk_full, 1)
                dve.engine_nop().then_inc(s_kk_full, 1)
                tt(heads(qd), heads(qn), per_head(gates[:, 3, col]), ALU.mult).then_inc(s_kk_full, 1)
                dve.wait_ge(s_gb_full, t + 1)
                link(tt(heads(ET), heads(bank(7)), per_head(gates[:, 2, col]), ALU.subtract))
                ts(ET, ET, 0.0, None, ALU.min).then_inc(s_dd_ready, 1)
                pick(SPLIT["gates"])
                dve.wait_ge(s_dd_exp, t + 1)
                link(tt(heads(ET), heads(ET), each_head(tri[:, :]), ALU.mult))
                dve.wait_ge(s_p_kk, 2 * t + 1)
                if t:
                    dve.wait_ge(s_ct_ready, 5 * t)
                tt(AT, bank(0), ET, ALU.mult).then_inc(s_at_ready, 1)
                dve.wait_ge(s_p_kk, 2 * t + 2)
                tt(QKT, bank(1), ET, ALU.mult).then_inc(s_at_ready, 1)
                dve.wait_ge(s_at_ready, 2 * t + 2)
                link(tt(heads(XT), heads(AT), each_head(lvl[0]), ALU.mult))
                tt(heads(XT), each_head(ident[:, :]), heads(XT), ALU.subtract).then_inc(s_xt1_ready, 1)
                pick(SPLIT["first"])
                dve.wait_ge(s_x1_ready, t + 1)
                for l in range(5):
                    for pr in range(2):
                        n = 18 * t + 4 * l + (2 * pr if l < 4 else pr)
                        dve.wait_ge(s_dx_full, n + (2 if l < 4 else 1))
                        tt(XT[:, PAIR(pr)], XT[:, PAIR(pr)], bank(B_XT[pr])[:, PAIR(pr)], ALU.subtract).then_inc(s_dx_ready, 1)
                        if l < 4:
                            tt(X[:, PAIR(pr)], X[:, PAIR(pr)], bank(B_X[pr])[:, PAIR(pr)], ALU.subtract).then_inc(s_dx_ready, 1)
                dve.wait_ge(s_dx_ready, 18 * (t + 1))
                pick(SPLIT["w"])
                for cc in range(2):
                    pick(SPLIT["state"])
                    dve.wait_ge(s_ods_full, 2 * t + cc + 1)
                    for h in range(H):
                        gcol = t * H + h
                        ins = stt(out=S_st[:, HSL(h)], in0=S_st[:, HSL(h)], scalar=gates[:, 5 + cc, gcol:gcol + 1],
                                  in1=bank(4 + cc)[:, HSL(h)], op0=ALU.mult, op1=ALU.add)
                    ins.then_inc(s_s_ready, 1)
                    dve.wait_ge(s_s_ready, 2 * t + cc + 1)
                dve.wait_ge(s_o_sq, t + 1)
                dve.tensor_reduce(st[:, 1, 32 + t * H:32 + (t + 1) * H], heads(osq), AX.X, ALU.add)
                tt(zg[:, t, :], bank(3), zg[:, t, :], ALU.mult).then_inc(s_oz_ready, 1)
            dve.wait_ge(s_orms_ready, 1)
            link(dve.reciprocal(st[:, 0, 0:NC], st[:, 1, 0:NC]))
            for t in range(NT):
                tt(heads(zg[:, t, :]), heads(zg[:, t, :]), per_head(st[:, 0, t * H:(t + 1) * H]), ALU.mult).then_inc(s_on_ready, 1)

            pick(ROUNDS * len(SEL_TILES) - picked[0])

            dve.wait_ge(s_ont_full, NT)
            for t in range(2):
                dve.memset(bias01[t], 0.0)
            link(dve.memset(m8[:, :], 0.0))
            for t in range(2):
                link(dve.memset(bias01[t][0:CHUNK, t * P + CHUNK:(t + 1) * P], NEG))

            def pt_evac(u):
                for gi in pt_groups(u):
                    if gi % 2:
                        n = pt_cols(u, gi)
                        dve.wait_ge(s_pt_full, gi + 1)
                        if u >= 2:
                            dve.wait_ge(s_o_full, u - 1)
                        dve.tensor_copy(prT[u % 2][:, n], bank(1)[:, 0:n.stop - n.start]).then_inc(s_pt_dve, 1)

            for u in range(NT * H + 1):
                if u:
                    pt_evac(u - 1)
                if u < NT * H:
                    t = u // H
                    n = (t + 1) * P
                    bias = score[t] if t in score else bias01[t]
                    dve.wait_ge(s_lg_full, u + 1)
                    if u >= 2:
                        dve.wait_ge(s_pt_full, pt_groups(u - 1)[0])
                    dve.tensor_tensor_reduce(lg[u % 2][:, 0:n], bank(4 + 2 * (u % 2), 2)[:, 0:n], bias, 1.0, TAKEN,
                                             ALU.add, ALU.max, st[:, 0, u:u + 1]).then_inc(s_lg_ready, 1)
                    dve.wait_ge(s_lg_ready, u + 1)
                    ts(st[:, 1, u:u + 1], st[:, 0, u:u + 1], -SM_SCALE, None, ALU.mult).then_inc(s_mx_ready, 1)
                if u and (u - 1) % H == H - 1:
                    t = (u - 1) // H
                    dve.wait_ge(s_o_full, H * (t + 1))
                    if t:
                        dve.wait_ge(s_oT_full, t)
                    link(dve.reciprocal(st[:, 3, t * H:(t + 1) * H], st[:, 2, t * H:(t + 1) * H]))
                    tt(heads(osa), heads(bank(2)), per_head(st[:, 3, t * H:(t + 1) * H]), ALU.mult).then_inc(s_osa_ready, 1)

            dve.tensor_copy(condrep, cond[:, :].unsqueeze(2).to_broadcast([P, NK, P])).then_inc(s_gt1_full, 1)
            dve.wait_ge(s_x_load, 16 * 4)
            dve.wait_ge(pan_used, PAN["ada5"] + 1)
            tt(gt1[:, 0:HALF], gt1[:, 0:HALF], bank(4), ALU.add)
            link(tt(gt1[:, HALF:D], gt1[:, HALF:D], bank(5), ALU.add))
            dve.engine_nop().then_inc(s_gt1_ready, 1)
            modulation(A2, B2, V_N2, 24, 32, 1)
            dve.engine_nop().then_inc(s_ab2_ready, 1)
            dve.wait_ge(pan_used, PAN["ada11"] + 1)
            tt(gt2[:, 0:HALF], gt2[:, 0:HALF], bank(4), ALU.add)
            tt(gt2[:, HALF:D], gt2[:, HALF:D], bank(5), ALU.add).then_inc(s_gt2_ready, 1)
            dve.wait_ge(s_x2_in, 16 * NT)
            for gi in range(2 * NT):
                n, t = gi // NT, gi % NT
                N = slice(n * HALF, (n + 1) * HALF)
                dve.wait_ge(s_y1_full, gi + 1)
                tt(ytmp[gi % 2], bank(gi % 4), gt1[:, N], ALU.mult).then_inc(s_y1_read, 1)
                dve.wait_ge(s_y1_read, 2 * gi + 1)
                tt(x2[:, t, N], x2[:, t, N], ytmp[gi % 2], ALU.add).then_inc(s_y1_read, 1)
            dve.tensor_copy(ab_rep[:, 0], A2[:, :].unsqueeze(2).to_broadcast([P, NK, P]))
            dve.tensor_copy(ab_rep[:, 1], B2[:, :].unsqueeze(2).to_broadcast([P, NK, P])).then_inc(s_ab2_ready, 1)
            for t in range(NT):
                dve.wait_ge(s_rms2_ready, t + 1)
                link(dve.reciprocal(st[:, 2, t:t + 1], st[:, 1, t:t + 1]))
                ts(xh2[:, t, :], x2[:, t, :], st[:, 2, t:t + 1], None, ALU.mult).then_inc(s_xh2_ready, 1)
            for m in range(1, 16, 2):
                hf, k = m // 8, m % 8
                dve.wait_ge(s_h2_full, m + 1)
                ts(h2T[:, k, hf * HALF:(hf + 1) * HALF], bank(4 + m % 4), A2[:, k:k + 1], B2[:, k:k + 1],
                   ALU.mult, ALU.add).then_inc(s_h2_dve, 1)
            dve.wait_ge(s_h2_full, 16)
            dve.wait_ge(s_ab_rows, 4)
            for op, row in ((ALU.mult, A2_row), (ALU.add, B2_row)):
                for t in range(NT):
                    if op == ALU.add:
                        dve.wait_ge(s_h2_rows, t + 1)
                    tt(xh2[:, t, :], xh2[:, t, :], row, op).then_inc(s_h2_rows, 1)
            te = lambda a: a.rearrange("p (t e) -> p t e", t=NT)
            dve.wait_ge(s_rsc_ready, 1)
            dve.wait_ge(s_small_done, 4)
            link(tt(te(r_ch), te(r_sc), rb[:, :].unsqueeze(1).to_broadcast([P, NT, NE]), ALU.add))
            for i in range(NT * NG):
                ins = dve.max(r_eq[:, 8 * i:8 * i + 8], r_ch[:, 8 * i:8 * i + 8])
            link(ins)
            top = r_eq.rearrange("p (n k) -> p n k", k=8)
            gs, rank = gsm[:, 0, :], gsm[:, 1, :]
            link(tt(gs.unsqueeze(2), top[:, :, 0:1], top[:, :, 1:2], ALU.add))
            g3 = gs.rearrange("p (t g) -> p t g", t=NT)
            other, own = g3.unsqueeze(2).to_broadcast([P, NT, NG, NG]), g3.unsqueeze(3).to_broadcast([P, NT, NG, NG])
            c4 = lambda a: a.rearrange("p (t g q) -> p t g q", t=NT, g=NG)
            tt(c4(r_gt), other, own, ALU.is_gt)
            link(tt(c4(r_eq), other, own, ALU.is_equal))
            link(tt(c4(r_eq), c4(r_eq), lowm[:, :, :].unsqueeze(1).to_broadcast([P, NT, NG, NG]), ALU.mult))
            link(tt(r_gt, r_gt, r_eq, ALU.add))
            link(dve.tensor_reduce(rank, r_gt.rearrange("p (n q) -> p n q", q=NG), AX.X, ALU.add))
            link(ts(rank, rank, float(TOP_G), NEG, ALU.is_ge, ALU.mult))
            n8 = lambda a: a.rearrange("p (n q) -> p n q", q=8)
            link(tt(n8(r_ch), n8(r_ch), rank.unsqueeze(2).to_broadcast([P, NT * NG, 8]), ALU.add))
            E = lambda a, t: a[:, t * NE:(t + 1) * NE]
            for t in range(NT):
                link(dve.max(m8[:, :], E(r_ch, t)))
                link(dve.match_replace(E(r_v, t), m8[:, :], E(r_ch, t), TAKEN))
            ts(r_mk, r_v, TAKEN_CUT, None, ALU.is_lt).then_inc(s_mask_ready, 1)
            dve.wait_ge(s_mask_ready, 1)
            link(tt(r_gt, r_sc, r_mk, ALU.mult))
            link(dve.tensor_reduce(gsm[:, 0, 0:NT], te(r_gt), AX.X, ALU.add))
            link(dve.reciprocal(gsm[:, 0, 8:8 + NT], gsm[:, 0, 0:NT]))
            link(ts(gsm[:, 0, 8:8 + NT], gsm[:, 0, 8:8 + NT], ROUTED, None, ALU.mult))
            link(tt(te(r_gt), te(r_gt), gsm[:, 0, 8:8 + NT].unsqueeze(2).to_broadcast([P, NT, NE]), ALU.mult))
            dve.wait_ge(s_pos_full, 1)
            link(tt(te(r_v), te(bank(1)), erow[:, :].unsqueeze(1).to_broadcast([P, NT, NE]), ALU.add))
            link(tt(r_v, r_v, r_mk, ALU.mult))
            link(ts(cni, bank(2)[:, 0:NE], float(P - 1), None, ALU.add))
            link(ts(cni, cni, 7, None, ALU.arith_shift_right))
            link(ts(nbf, cni, 1.0, None, ALU.max))
            dve.tensor_copy(ints[0:1, 0:NE], nbf[0:1, :]).then_inc(s_nbr_ready, 1)
            for t in range(NT):
                ins = dve.max(d8[:, t * 8:t * 8 + 8], E(r_v, t))
            link(ins)
            link(ts(di[0][:, :], d8[:, :], -1.0, None, ALU.add))
            ts(di[1][:, :], di[0][:, :], 7, None, ALU.arith_shift_right)
            link(ts(di[0][:, :], di[0][:, :], P - 1, 9, ALU.bitwise_and, ALU.logical_shift_left))
            link(tt(dest_i[:, :], di[0][:, :], di[1][:, :], ALU.bitwise_or))
            payf = pay.bitcast(F32).rearrange("p (t k two) -> p t k two", t=NT, two=2)
            ke = lambda a: a.rearrange("p (k e) -> p k e", e=NE)
            for t in range(NT):
                link(tt(ke(r_eq), E(r_v, t).unsqueeze(1).to_broadcast([P, 8, NE]),
                        d8[:, t * 8:t * 8 + 8].unsqueeze(2).to_broadcast([P, 8, NE]), ALU.is_equal))
                link(tt(ke(r_eq), ke(r_eq), E(r_gt, t).unsqueeze(1).to_broadcast([P, 8, NE]), ALU.mult))
                dve.tensor_reduce(payf[:, t, :, 1:2], ke(r_eq), AX.X, ALU.add).then_inc(s_lists_ready, 1)
                dve.wait_ge(s_lists_ready, t + 1)
            dve.wait_ge(s_nbt_full, 1)
            dve.tensor_copy(nbc, bank(3)[0:NE, 0:P]).then_inc(s_nbt_ready, 1)
            dve.wait_ge(s_nbt_full, 2)
            dve.tensor_copy(ints[0:1, NE:2 * NE], bank(3)[0:1, P:P + NE])
            tt(ints[0:1, 2 * NE:2 * NE + 1], bank(3)[0:1, P + NE - 1:P + NE], nbf[0:1, NE - 1:NE], ALU.add).then_inc(s_cnt_ready, 1)
            dve.wait_ge(s_cnt_ready, 1)

            def rest(out_, x_, high):
                return tt(out_, x_, high.bitcast(F32), ALU.subtract)

            def split_gu(e, i):
                for n, (w, where) in enumerate(GU_PARTS):
                    dve.wait_ge(s_wh_ready, e * PARTS + (n + 1))
                    ins = rest(where(wl[i]), w, where(wh[i]))
                    if n % 2:
                        ins.then_inc(s_split_gu, 1)

            def split_d(e, i):
                for n, (w, where) in enumerate(D_PARTS[i]):
                    dve.wait_ge(s_wh_ready, e * PARTS + (len(GU_PARTS) + n + 1))
                    ins = rest(where(wl[i]), w, where(wh[i]))
                ins.then_inc(s_split_d, 1)

            def x_evac(n):
                dve.wait_ge(s_xT_act, n + 1)
                for i in range(2):
                    ins = rest(xl[i], bank(i), xh[:, i * HALF:(i + 1) * HALF])
                ins.then_inc(s_xT_dve, 1)

            dve.wait_ge(s_xn_out, 16 * NT)
            split_gu(0, 0)
            dve.wait_ge(s_tbl_in, 16)
            for done in acc_out:
                dve.wait_ge(done, 8 * NT)
            dve.wait_ge(s_xg_read, 2)
            x_evac(0)
            split_d(0, 0)

            def expert(e, i, more=True):
                if more:
                    split_gu(e + 1, 1 - i)
                nb = dve.value_load(ints[0:1, bass.ds(e, 1)], min_val=1, max_val=CAP)
                b0 = dve.value_load(ints[0:1, bass.ds(e + NE, 1)], min_val=0, max_val=NE * CAP)
                with dve.Fori(0, nb) as b:
                    g = dve.snap(b0 + b)
                    dve.wait_ge(s_silu_done, g + 1)
                    tt(hm, sg, bank(2)[:, FE:2 * FE], ALU.mult).then_inc(s_hm_ready, 1)
                    dve.wait_ge(s_hT_ready, g + 1)
                    rest(hTl, bank(3)[:, 0:FE], hTh).then_inc(s_hl_ready, 1)
                    dve.wait_ge(s_xg_read, g + 3)
                    x_evac(g + 1)
                if more:
                    split_d(e + 1, 1 - i)

            with dve.Fori(0, NE // 2 - 1) as pair:
                for i in range(2):
                    expert(pair * 2 + i, i)
            for i in range(2):
                expert(NE - 2 + i, i, i == 0)

            def finish(t):
                dst = xg if t % 2 == 0 else xTm
                dve.wait_ge(s_rms3_ready, t + 1)
                link(dve.reciprocal(st[:, 2, t:t + 1], st[:, 1, t:t + 1]))
                if t >= 2:
                    dve.wait_ge(out_done[t % 2], OUT0 + 16 * (t // 2))
                stt(out=dst, in0=x3[:, t, :], scalar=st[:, 2, t:t + 1], in1=fg, op0=ALU.mult, op1=ALU.mult).then_inc(s_o_ready, 1)

            for t in range(NT + 2):
                if t < NT:
                    dve.wait_ge(acc_in[t >= 2], 16 * (2 if t < 2 else NT - 2))
                    tt(x3[:, t, :], x3[:, t, :], gt2, ALU.mult).then_inc(s_gated, 1)
                if t >= 2:
                    finish(t - 2)


_INS = ["x", "c", "ada_w", "ada_b", "norm1_g", "w_in", "conv_w", "a_log", "dt_bias", "dn_norm_g", "kv_norm_g", "w_uk",
        "w_uv", "idx_k_ln_g", "idx_k_ln_b", "w_out", "norm2_g", "router_w", "router_b", "exp_w_gate", "exp_w_up",
        "exp_w_down", "sh_w_gate", "sh_w_up", "sh_w_down", "final_g"]
_OUTS = [((1, T, D), "float32")]


def kernel(**inputs):
    import numpy as _np
    import concourse.bacc as _bacc
    from concourse import mybir as _mybir
    from concourse.bass_utils import run_bass_kernel_spmd as _run

    nc = _bacc.Bacc("TRN2", target_bir_lowering=False, num_devices=1)
    arrays, args = {}, []
    for name in _INS:
        a = _np.ascontiguousarray(inputs[name])
        arrays[f"in_{name}_dram"] = a
        args.append(nc.dram_tensor(f"in_{name}_dram", a.shape, _mybir.dt.from_np(a.dtype), kind="ExternalInput").ap())
    for i, (shape, dtype) in enumerate(_OUTS):
        dt = _mybir.dt.from_np(_np.dtype(dtype))
        args.append(nc.dram_tensor(f"out_{i}_dram", shape, dt, kind="ExternalOutput").ap())
    build(nc, *args)
    r = _run(nc, [arrays], core_ids=[0])
    got = tuple(r.results[0][f"out_{i}_dram"] for i in range(len(_OUTS)))
    return got[0]
```
